# Optimizing a Trainium2 kernel written in Bass

```python
import math
import jax, jax.numpy as jnp
from jax import lax
import numpy as np

D_MODEL = 1024
BATCH = 1
SEQ = 512
DEPTH = 1

N_META = 16
ATTN_HEADS = 4
ATTN_HEAD_DIM = 64
ATTN_VALUE_DIM = 2 * ATTN_HEAD_DIM
ATTN_WIDTH = ATTN_HEADS * ATTN_VALUE_DIM
CONV_WIDTH = D_MODEL - ATTN_WIDTH
CONV_K = 3
MIX_WIDTH = ATTN_WIDTH + CONV_WIDTH
IN_PROJ_WIDTH = 3 * ATTN_WIDTH + 3 * CONV_WIDTH
N_EXPERTS = 16
EC_CAPACITY_FACTOR = 2
D_FF_EXPERT = 2 * D_MODEL
ROPE_THETA = 10000.0
Q_BLOCK = 128
NORM_EPS = 1e-6


def rms_norm(x, g):
    xf = x.astype(jnp.float32)
    y = xf * lax.rsqrt(jnp.mean(xf * xf, axis=-1, keepdims=True) + NORM_EPS)
    return (y * g.astype(jnp.float32)).astype(x.dtype)

def rope_tables(n):
    d = ATTN_HEAD_DIM
    inv_freq = ROPE_THETA ** (-jnp.arange(0, d, 2, dtype=jnp.float32) / d)
    ang = jnp.arange(n, dtype=jnp.float32)[:, None] * inv_freq[None, :]
    ang = jnp.concatenate([ang, ang], axis=-1)
    return jnp.cos(ang), jnp.sin(ang)

def apply_rope(x, cos, sin):
    half = x.shape[-1] // 2
    x1, x2 = x[..., :half], x[..., half:]
    rot = jnp.concatenate([-x2, x1], axis=-1)
    return (x * cos + rot * sin).astype(x.dtype)

def diff_attention_group(q, k, v, lq1, lk1, lq2, lk2, subln_g, lam_init, cos, sin):
    B, L, _ = q.shape
    Lp = cos.shape[0]
    H, d = ATTN_HEADS, ATTN_HEAD_DIM
    pad = Lp - L
    q = jnp.pad(q.reshape(B, L, H, 2, d), ((0, 0), (0, pad), (0, 0), (0, 0), (0, 0)))
    k = jnp.pad(k.reshape(B, L, H, 2, d), ((0, 0), (0, pad), (0, 0), (0, 0), (0, 0)))
    v = jnp.pad(v.reshape(B, L, H, 2 * d), ((0, 0), (0, pad), (0, 0), (0, 0)))
    q = apply_rope(q.transpose(0, 2, 3, 1, 4), cos, sin)
    k = apply_rope(k.transpose(0, 2, 3, 1, 4), cos, sin)
    v32 = v.transpose(0, 2, 1, 3).astype(jnp.float32)

    lam = (jnp.exp(jnp.sum(lq1.astype(jnp.float32) * lk1.astype(jnp.float32)))
           - jnp.exp(jnp.sum(lq2.astype(jnp.float32) * lk2.astype(jnp.float32)))
           + lam_init)
    key_valid = jnp.arange(Lp) < L
    scale = d ** -0.5
    n_blk = Lp // Q_BLOCK
    qb = jnp.moveaxis(q.reshape(B, H, 2, n_blk, Q_BLOCK, d), 3, 0)

    def one_block(qi):
        s = jnp.einsum('bhiqd,bhikd->bhiqk', qi, k,
                       preferred_element_type=jnp.float32) * scale
        s = jnp.where(key_valid, s, jnp.finfo(jnp.float32).min)
        p = jax.nn.softmax(s, axis=-1)
        a = p[:, :, 0] - lam * p[:, :, 1]
        return jnp.einsum('bhqk,bhkv->bhqv', a, v32)

    o = lax.map(one_block, qb)
    o = o.transpose(1, 0, 3, 2, 4).reshape(B, Lp, H, 2 * d)[:, :L]
    o = rms_norm(o, subln_g) * (1.0 - lam_init)
    return o.reshape(B, L, ATTN_WIDTH).astype(q.dtype)

def centred_depthwise_conv(u, w):
    L = u.shape[1]
    half = CONV_K // 2
    up = jnp.pad(u, ((0, 0), (half, half), (0, 0)))
    return sum(w[j] * up[:, j:j + L] for j in range(CONV_K))

def expert_choice_ffn(h, w_router, w_gate, w_up, w_down):
    B, L, D = h.shape
    cap = EC_CAPACITY_FACTOR * L // N_EXPERTS

    def one_group(hs):
        logits = jnp.einsum('ld,de->le', hs, w_router, preferred_element_type=jnp.float32)
        aff = jax.nn.softmax(logits, axis=-1)
        g, idx = lax.top_k(aff.T, cap)
        xg = hs[idx]
        a = jnp.einsum('ecd,edf->ecf', xg, w_gate)
        u = jnp.einsum('ecd,edf->ecf', xg, w_up)
        y = jnp.einsum('ecf,efd->ecd', jax.nn.silu(a) * u, w_down)
        y = y * g[..., None].astype(y.dtype)
        out = jnp.zeros((L, D), y.dtype).at[idx.reshape(-1)].add(y.reshape(-1, D))
        return out.astype(hs.dtype)

    return lax.map(one_group, h)

def first_inputs(seed: int = 0) -> dict:
    key = jax.random.key(seed)
    ks = jax.random.split(key, 20)
    f32 = jnp.float32
    nrm = lambda k, shape, s: jax.random.normal(k, shape, f32) * s
    gain = lambda k, shape: 1.0 + 0.02 * jax.random.normal(k, shape, f32)
    return {
        "x": nrm(ks[0], (BATCH, SEQ, D_MODEL), 1.0),
        "meta_tokens": nrm(ks[1], (N_META, D_MODEL), 1.0),
        "mix_norm_g": gain(ks[2], (DEPTH, D_MODEL)),
        "w_in": nrm(ks[3], (DEPTH, D_MODEL, IN_PROJ_WIDTH), D_MODEL ** -0.5),
        "conv_w": nrm(ks[4], (DEPTH, CONV_K, CONV_WIDTH), CONV_K ** -0.5),
        "lambda_q1": nrm(ks[5], (DEPTH, ATTN_HEAD_DIM), 0.1),
        "lambda_k1": nrm(ks[6], (DEPTH, ATTN_HEAD_DIM), 0.1),
        "lambda_q2": nrm(ks[7], (DEPTH, ATTN_HEAD_DIM), 0.1),
        "lambda_k2": nrm(ks[8], (DEPTH, ATTN_HEAD_DIM), 0.1),
        "attn_subln_g": gain(ks[9], (DEPTH, ATTN_VALUE_DIM)),
        "w_out": nrm(ks[10], (DEPTH, MIX_WIDTH, D_MODEL), MIX_WIDTH ** -0.5),
        "ffn_norm_g": gain(ks[11], (DEPTH, D_MODEL)),
        "w_router": nrm(ks[12], (DEPTH, D_MODEL, N_EXPERTS), D_MODEL ** -0.5),
        "w_gate": nrm(ks[13], (DEPTH, N_EXPERTS, D_MODEL, D_FF_EXPERT), D_MODEL ** -0.5),
        "w_up": nrm(ks[14], (DEPTH, N_EXPERTS, D_MODEL, D_FF_EXPERT), D_MODEL ** -0.5),
        "w_down": nrm(ks[15], (DEPTH, N_EXPERTS, D_FF_EXPERT, D_MODEL), D_FF_EXPERT ** -0.5),
        "final_norm_g": gain(ks[16], (D_MODEL,)),
    }

def first_block(x, meta_tokens, mix_norm_g, w_in, conv_w, lambda_q1, lambda_k1, lambda_q2,
              lambda_k2, attn_subln_g, w_out, ffn_norm_g, w_router, w_gate, w_up, w_down,
              final_norm_g):
    B = x.shape[0]
    meta = jnp.broadcast_to(meta_tokens.astype(x.dtype)[None], (B, N_META, D_MODEL))
    h = jnp.concatenate([meta, x], axis=1)
    L = h.shape[1]
    Lp = -(-L // Q_BLOCK) * Q_BLOCK
    cos, sin = rope_tables(Lp)
    splits = [ATTN_WIDTH, 2 * ATTN_WIDTH, 3 * ATTN_WIDTH,
              3 * ATTN_WIDTH + CONV_WIDTH, 3 * ATTN_WIDTH + 2 * CONV_WIDTH]

    for l in range(DEPTH):
        lam_init = 0.8 - 0.6 * math.exp(-0.3 * l)
        hn = rms_norm(h, mix_norm_g[l])
        proj = jnp.einsum('bld,dp->blp', hn, w_in[l])
        q, k, v, cx, cb, cc = jnp.split(proj, splits, axis=-1)
        attn = diff_attention_group(q, k, v, lambda_q1[l], lambda_k1[l], lambda_q2[l],
                                    lambda_k2[l], attn_subln_g[l], lam_init, cos, sin)
        conv = cb * centred_depthwise_conv(cc * cx, conv_w[l])
        mixed = jnp.concatenate([attn, conv.astype(attn.dtype)], axis=-1)
        h = h + jnp.einsum('blm,md->bld', mixed, w_out[l])
        h = h + expert_choice_ffn(rms_norm(h, ffn_norm_g[l]), w_router[l], w_gate[l],
                                  w_up[l], w_down[l])

    y = rms_norm(h, final_norm_g)
    return y[:, N_META:, :]


DEPTH_2 = 2

CHUNK = 64
N_MEM = 256
N_A_LAYERS = DEPTH_2 // 2
N_B_LAYERS = DEPTH_2 - N_A_LAYERS
EPS = 1e-6
M_HEADS = 4
M_HEAD_DIM = D_MODEL // M_HEADS
M_WIDTH = M_HEADS * M_HEAD_DIM
CONV_W = 4
B_HEADS = 8
QK_NOPE = 128
QK_ROPE = 64
QK_HEAD = QK_NOPE + QK_ROPE
V_HEAD = 128
B_WIDTH = B_HEADS * V_HEAD
Q_LORA = 384
KV_LORA = 256
MEM_HEADS = 4
MEM_HEAD_DIM = 128
MEM_WIDTH = MEM_HEADS * MEM_HEAD_DIM
A_IN = 2 * M_WIDTH + 3 * M_WIDTH + 2 * M_HEADS + 2 * MEM_WIDTH
B_IN = Q_LORA + B_WIDTH + 2 * MEM_WIDTH
A_MIX = M_WIDTH + MEM_WIDTH
B_MIX = B_WIDTH + MEM_WIDTH


def rmsnorm(t, g):
    tf = t.astype(jnp.float32)
    y = tf * lax.rsqrt(jnp.mean(tf * tf, axis=-1, keepdims=True) + EPS)
    return (y * g.astype(jnp.float32)).astype(t.dtype)

def split_cols(t, sizes):
    offs = np.cumsum(np.array(sizes))[:-1].tolist()
    return jnp.split(t, offs, axis=-1)

def rope(t, positions):
    half = QK_ROPE // 2
    inv = ROPE_THETA ** (-jnp.arange(0, QK_ROPE, 2, dtype=jnp.float32) / QK_ROPE)
    ang = positions.astype(jnp.float32)[..., None] * inv
    cos = jnp.cos(ang)[:, :, None, :]
    sin = jnp.sin(ang)[:, :, None, :]
    tf = t.astype(jnp.float32)
    t1, t2 = tf[..., :half], tf[..., half:]
    return jnp.concatenate([t1 * cos - t2 * sin, t1 * sin + t2 * cos], axis=-1).astype(t.dtype)

def causal_conv(u, w, b):
    out = lax.conv_general_dilated(
        u, w[:, None, :].astype(u.dtype), window_strides=(1,), padding=[(CONV_W - 1, 0)],
        dimension_numbers=("NWC", "WIO", "NWC"), feature_group_count=u.shape[-1])
    return out + b.astype(u.dtype)

def mlstm_chunkwise(q, k, v, i_pre, f_pre):
    bsz, s, h, dh = q.shape
    nc = s // CHUNK

    def to_chunks(t):
        return t.astype(jnp.float32).reshape(bsz, nc, CHUNK, h, -1).transpose(1, 0, 3, 2, 4)

    def gate_chunks(t):
        return t.astype(jnp.float32).reshape(bsz, nc, CHUNK, h).transpose(1, 0, 3, 2)

    qc = to_chunks(q) * (dh ** -0.5)
    kc = to_chunks(k)
    vc = to_chunks(v)
    ic = gate_chunks(i_pre)
    lfc = jax.nn.log_sigmoid(gate_chunks(f_pre))
    causal = jnp.tril(jnp.ones((CHUNK, CHUNK), dtype=bool))

    def step(carry, inp):
        c_mat, n_vec, m = carry
        qb, kb, vb, ib, fb = inp
        b = jnp.cumsum(fb, axis=-1)
        d = b[..., :, None] - b[..., None, :] + ib[..., None, :]
        d = jnp.where(causal, d, -jnp.inf)
        inter = b + m[..., None]
        m_t = jnp.maximum(inter, jnp.max(d, axis=-1))
        p = jnp.einsum("bhtd,bhsd->bhts", qb, kb) * jnp.exp(d - m_t[..., None])
        g = jnp.exp(inter - m_t)
        num = jnp.einsum("bhts,bhsv->bhtv", p, vb) + g[..., None] * jnp.einsum("bhvk,bhtk->bhtv", c_mat, qb)
        den = jnp.sum(p, axis=-1) + g * jnp.einsum("bhk,bhtk->bht", n_vec, qb)
        h_out = num / jnp.maximum(jnp.abs(den), jnp.exp(-m_t))[..., None]
        b_last = b[..., -1]
        a = b_last[..., None] - b + ib
        m_new = jnp.maximum(b_last + m, jnp.max(a, axis=-1))
        wa = jnp.exp(a - m_new[..., None])
        gs = jnp.exp(b_last + m - m_new)
        c_new = gs[..., None, None] * c_mat + jnp.einsum("bhs,bhsv,bhsk->bhvk", wa, vb, kb)
        n_new = gs[..., None] * n_vec + jnp.einsum("bhs,bhsk->bhk", wa, kb)
        return (c_new, n_new, m_new), h_out

    init = (jnp.zeros((bsz, h, dh, dh), jnp.float32), jnp.zeros((bsz, h, dh), jnp.float32),
            jnp.zeros((bsz, h), jnp.float32))
    _, hs = lax.scan(step, init, (qc, kc, vc, ic, lfc))
    return hs.transpose(1, 0, 3, 2, 4).reshape(bsz, s, h, dh)

def chunk_causal_attention(q, k, v):
    s = q.shape[1]
    scale = QK_HEAD ** -0.5
    outs = []
    for j in range(s // Q_BLOCK):
        qs = j * Q_BLOCK
        ke = qs + Q_BLOCK
        sc = jnp.einsum("bqhd,bkhd->bhqk", q[:, qs:ke], k[:, :ke],
                        preferred_element_type=jnp.float32) * scale
        q_chunk = (qs + jnp.arange(Q_BLOCK)) // CHUNK
        k_chunk = jnp.arange(ke) // CHUNK
        sc = jnp.where(k_chunk[None, :] <= q_chunk[:, None], sc, -jnp.inf)
        p = jax.nn.softmax(sc, axis=-1).astype(v.dtype)
        outs.append(jnp.einsum("bhqk,bkhd->bqhd", p, v[:, :ke]))
    return jnp.concatenate(outs, axis=1)

def memory_kv(mem_n, w_kv, k_gain):
    bsz, nm, _ = mem_n.shape
    mk, mv = split_cols(mem_n @ w_kv, [MEM_WIDTH, MEM_WIDTH])
    mk = rmsnorm(mk.reshape(bsz, nm, MEM_HEADS, MEM_HEAD_DIM), k_gain)
    return mk, mv.reshape(bsz, nm, MEM_HEADS, MEM_HEAD_DIM)

def memory_attention(mq, mz, mk, mv, q_gain):
    bsz, s, _ = mq.shape
    q = rmsnorm(mq.reshape(bsz, s, MEM_HEADS, MEM_HEAD_DIM), q_gain)
    sc = jnp.einsum("bqhd,bkhd->bhqk", q, mk, preferred_element_type=jnp.float32) * (MEM_HEAD_DIM ** -0.5)
    p = jax.nn.softmax(sc, axis=-1).astype(mv.dtype)
    out = jnp.einsum("bhqk,bkhd->bqhd", p, mv).reshape(bsz, s, MEM_WIDTH)
    return out * jax.nn.silu(mz)

def mlstm_layer(x, norm_g, w_in, conv_w, conv_b, ig_b, fg_b, h_g, w_out, mk, mv, mq_gain):
    bsz, s, _ = x.shape
    h = rmsnorm(x, norm_g)
    qk, v, o, z, i_pre, f_pre, mq, mz = split_cols(
        h @ w_in, [2 * M_WIDTH, M_WIDTH, M_WIDTH, M_WIDTH, M_HEADS, M_HEADS, MEM_WIDTH, MEM_WIDTH])
    qk = jax.nn.silu(causal_conv(qk, conv_w, conv_b))
    q, k = split_cols(qk, [M_WIDTH, M_WIDTH])
    heads = (bsz, s, M_HEADS, M_HEAD_DIM)
    ht = mlstm_chunkwise(q.reshape(heads), k.reshape(heads), v.reshape(heads),
                         i_pre + ig_b, f_pre + fg_b).astype(x.dtype)
    ht = rmsnorm(ht, h_g.reshape(M_HEADS, M_HEAD_DIM)).reshape(bsz, s, M_WIDTH)
    y_m = jax.nn.sigmoid(o) * ht * jax.nn.silu(z)
    y_mem = memory_attention(mq, mz, mk, mv, mq_gain)
    return x + jnp.concatenate([y_m, y_mem], axis=-1) @ w_out

def shared_kv(x, positions, kv_norm, w_kv_a, kv_lat_norm, w_kv_b, k_gain):
    bsz, s, _ = x.shape
    h = rmsnorm(x, kv_norm)
    c_kv, k_pe = split_cols(h @ w_kv_a, [KV_LORA, QK_ROPE])
    kv = (rmsnorm(c_kv, kv_lat_norm) @ w_kv_b).reshape(bsz, s, B_HEADS, QK_NOPE + V_HEAD)
    k_nope, v = kv[..., :QK_NOPE], kv[..., QK_NOPE:]
    k = jnp.concatenate([k_nope, jnp.broadcast_to(k_pe[:, :, None, :], (bsz, s, B_HEADS, QK_ROPE))], axis=-1)
    k = rmsnorm(k, k_gain)
    k = jnp.concatenate([k[..., :QK_NOPE], rope(k[..., QK_NOPE:], positions)], axis=-1)
    return k, v

def mla_layer(x, positions, k_sh, v_sh, norm_g, w_in, q_lat_g, w_q_up, q_gain, w_out, mk, mv, mq_gain):
    bsz, s, _ = x.shape
    h = rmsnorm(x, norm_g)
    q_lat, z, mq, mz = split_cols(h @ w_in, [Q_LORA, B_WIDTH, MEM_WIDTH, MEM_WIDTH])
    q = (rmsnorm(q_lat, q_lat_g) @ w_q_up).reshape(bsz, s, B_HEADS, QK_HEAD)
    q = rmsnorm(q, q_gain)
    q = jnp.concatenate([q[..., :QK_NOPE], rope(q[..., QK_NOPE:], positions)], axis=-1)
    attn = chunk_causal_attention(q, k_sh, v_sh).reshape(bsz, s, B_WIDTH)
    y_b = attn * jax.nn.silu(z)
    y_mem = memory_attention(mq, mz, mk, mv, mq_gain)
    return x + jnp.concatenate([y_b, y_mem], axis=-1) @ w_out

def second_inputs(seed: int = 0) -> dict:
    key = jax.random.key(seed)
    ks = jax.random.split(key, 32)

    def nrm(k, shape, scale):
        return jax.random.normal(k, shape, jnp.float32) * scale

    def gain(k, shape):
        return 1.0 + 0.02 * jax.random.normal(k, shape, jnp.float32)

    offsets = jax.random.randint(ks[2], (BATCH,), 0, 4096, dtype=jnp.int32)
    positions = (offsets[:, None] + jnp.arange(SEQ, dtype=jnp.int32)[None, :]).astype(jnp.int32)
    fg_base = jnp.linspace(3.0, 6.0, M_HEADS, dtype=jnp.float32)
    return {
        "x": nrm(ks[0], (BATCH, SEQ, D_MODEL), 1.0),
        "mem": nrm(ks[1], (BATCH, N_MEM, D_MODEL), 1.0),
        "positions": positions,
        "a_norm": gain(ks[3], (N_A_LAYERS, D_MODEL)),
        "a_w_in": nrm(ks[4], (N_A_LAYERS, D_MODEL, A_IN), D_MODEL ** -0.5),
        "a_conv_w": nrm(ks[5], (N_A_LAYERS, CONV_W, 2 * M_WIDTH), CONV_W ** -0.5),
        "a_conv_b": nrm(ks[6], (N_A_LAYERS, 2 * M_WIDTH), 0.01),
        "a_ig_bias": nrm(ks[7], (N_A_LAYERS, M_HEADS), 0.1),
        "a_fg_bias": fg_base[None, :] + nrm(ks[8], (N_A_LAYERS, M_HEADS), 0.1),
        "a_h_norm": gain(ks[9], (N_A_LAYERS, M_WIDTH)),
        "a_w_out": nrm(ks[10], (N_A_LAYERS, A_MIX, D_MODEL), A_MIX ** -0.5),
        "b_norm": gain(ks[11], (N_B_LAYERS, D_MODEL)),
        "b_w_in": nrm(ks[12], (N_B_LAYERS, D_MODEL, B_IN), D_MODEL ** -0.5),
        "b_q_lat_norm": gain(ks[13], (N_B_LAYERS, Q_LORA)),
        "b_w_q_up": nrm(ks[14], (N_B_LAYERS, Q_LORA, B_HEADS * QK_HEAD), Q_LORA ** -0.5),
        "b_q_gain": gain(ks[15], (N_B_LAYERS, QK_HEAD)),
        "b_w_out": nrm(ks[16], (N_B_LAYERS, B_MIX, D_MODEL), B_MIX ** -0.5),
        "kv_norm": gain(ks[17], (D_MODEL,)),
        "w_kv_a": nrm(ks[18], (D_MODEL, KV_LORA + QK_ROPE), D_MODEL ** -0.5),
        "kv_lat_norm": gain(ks[19], (KV_LORA,)),
        "w_kv_b": nrm(ks[20], (KV_LORA, B_HEADS * (QK_NOPE + V_HEAD)), KV_LORA ** -0.5),
        "k_gain": gain(ks[21], (QK_HEAD,)),
        "mem_norm": gain(ks[22], (D_MODEL,)),
        "mem_w_kv": nrm(ks[23], (DEPTH_2, D_MODEL, 2 * MEM_WIDTH), D_MODEL ** -0.5),
        "mem_q_gain": gain(ks[24], (DEPTH_2, MEM_HEAD_DIM)),
        "mem_k_gain": gain(ks[25], (DEPTH_2, MEM_HEAD_DIM)),
    }

def second_block(x, mem, positions, a_norm, a_w_in, a_conv_w, a_conv_b, a_ig_bias, a_fg_bias, a_h_norm, a_w_out,
              b_norm, b_w_in, b_q_lat_norm, b_w_q_up, b_q_gain, b_w_out,
              kv_norm, w_kv_a, kv_lat_norm, w_kv_b, k_gain,
              mem_norm, mem_w_kv, mem_q_gain, mem_k_gain):
    mem_n = rmsnorm(mem, mem_norm)
    k_sh = None
    v_sh = None
    for layer in range(DEPTH_2):
        mk, mv = memory_kv(mem_n, mem_w_kv[layer], mem_k_gain[layer])
        if layer < N_A_LAYERS:
            x = mlstm_layer(x, a_norm[layer], a_w_in[layer], a_conv_w[layer], a_conv_b[layer],
                            a_ig_bias[layer], a_fg_bias[layer], a_h_norm[layer], a_w_out[layer],
                            mk, mv, mem_q_gain[layer])
        else:
            if layer == N_A_LAYERS:
                k_sh, v_sh = shared_kv(x, positions, kv_norm, w_kv_a, kv_lat_norm, w_kv_b, k_gain)
            j = layer - N_A_LAYERS
            x = mla_layer(x, positions, k_sh, v_sh, b_norm[j], b_w_in[j], b_q_lat_norm[j], b_w_q_up[j],
                          b_q_gain[j], b_w_out[j], mk, mv, mem_q_gain[layer])
    return x


def setup_inputs(seed=0):
    out = dict(first_inputs(seed))
    for name, value in second_inputs(seed + 1).items():
        if name != "x":
            out[name + "_2"] = value
    return out


def reference(
    x, meta_tokens, mix_norm_g, w_in, conv_w, lambda_q1, lambda_k1, lambda_q2, lambda_k2,
    attn_subln_g, w_out, ffn_norm_g, w_router, w_gate, w_up, w_down, final_norm_g, mem_2,
    positions_2, a_norm_2, a_w_in_2, a_conv_w_2, a_conv_b_2, a_ig_bias_2, a_fg_bias_2,
    a_h_norm_2, a_w_out_2, b_norm_2, b_w_in_2, b_q_lat_norm_2, b_w_q_up_2, b_q_gain_2,
    b_w_out_2, kv_norm_2, w_kv_a_2, kv_lat_norm_2, w_kv_b_2, k_gain_2, mem_norm_2, mem_w_kv_2,
    mem_q_gain_2, mem_k_gain_2,
):
    x = first_block(
        x, meta_tokens, mix_norm_g, w_in, conv_w, lambda_q1, lambda_k1, lambda_q2, lambda_k2,
        attn_subln_g, w_out, ffn_norm_g, w_router, w_gate, w_up, w_down, final_norm_g,
    )
    return second_block(
        x, mem_2, positions_2, a_norm_2, a_w_in_2, a_conv_w_2, a_conv_b_2, a_ig_bias_2,
        a_fg_bias_2, a_h_norm_2, a_w_out_2, b_norm_2, b_w_in_2, b_q_lat_norm_2, b_w_q_up_2,
        b_q_gain_2, b_w_out_2, kv_norm_2, w_kv_a_2, kv_lat_norm_2, w_kv_b_2, k_gain_2,
        mem_norm_2, mem_w_kv_2, mem_q_gain_2, mem_k_gain_2,
    )


_drawn_inputs = setup_inputs


def setup_inputs(seed=0):
    import zlib

    import numpy as np

    out = dict(_drawn_inputs(seed))
    spreads = {}
    factors = {'lambda_q1': 8.0,
     'attn_subln_g': 4.578,
     'ffn_norm_g': 4.658,
     'a_norm_2': 6.581,
     'a_conv_b_2': 64.0,
     'a_ig_bias_2': 200.0,
     'a_h_norm_2': 8.0,
     'b_norm_2': 8.0,
     'b_q_lat_norm_2': 8.0,
     'b_q_gain_2': 8.0,
     'kv_norm_2': 8.0,
     'kv_lat_norm_2': 8.0,
     'k_gain_2': 8.0,
     'mem_norm_2': 8.0,
     'mem_q_gain_2': 8.0,
     'mem_k_gain_2': 8.0}
    for name, (base, spread) in spreads.items():
        noise = np.random.default_rng([zlib.crc32(name.encode()), seed]).standard_normal(out[name].shape)
        drawn = base * np.exp(spread * noise) if base else spread * noise
        out[name] = __import__('jax').numpy.asarray(drawn.astype(out[name].dtype))
    for name, factor in factors.items():
        out[name] = (out[name] * factor).astype(out[name].dtype)
    return out
```

```python
from contextlib import ExitStack

import numpy as np
import concourse.bass as bass
from concourse import mybir

F32 = mybir.dt.float32
F32R = mybir.dt.float32r
U32 = mybir.dt.uint32
ALU = mybir.AluOpType
ACT = mybir.ActivationFunctionType
AX = mybir.AxisListType

P = 128
D = 1024
KD = D // P
META = 16
SEQ = 512
L1 = META + SEQ
TILES1 = [(i * P, min(P, L1 - i * P)) for i in range(-(-L1 // P))]
TILES2 = [(i * P, P) for i in range(SEQ // P)]
HALF1 = L1 // 2
EPS = 1e-6
LAM_INIT = 0.2
AH, AV = 4, 128
NE = 16
CAP = 2 * L1 // NE
FF = 2 * D
FH = FF // 2
ROUNDS = -(-CAP // 8)
MEM = 256
MH, MDH = 4, 256
MW = MH * MDH
MEMH, MEMD = 4, 128
BH = 8
NOPE, ROPE = 128, 64
QKH = NOPE + ROPE
QL, KVL = 384, 256
NEG = -1.0e30
SLOT = 2048
NSLOT = 12
NPIECE, NSPLIT = 6, 3
TWO_PI = 2.0 * np.pi
PI_A = 6.28125
PI_B = float(np.float32(np.round((TWO_PI - PI_A) * 2 ** 19) / 2 ** 19))
PI_C = float(np.float32(TWO_PI - PI_A - PI_B))
ROUND = 12582912.0


def fixed_tables():
    i = np.arange(P)
    ident = np.eye(P)
    rot = np.zeros((P, P))
    for m in range(P):
        if m % 64 < 32:
            rot[m + 32, m] = -1.0
        else:
            rot[m - 32, m] = 1.0
    upto = (i[:, None] <= i[None, :])
    ones = np.ones((P, P))
    after = (i[:, None] > i[None, :])
    causal = np.where(i[None, :] > i[:, None], NEG, 0.0)
    chunk = np.where(i[None, :] // 64 > i[:, None] // 64, NEG, 0.0)
    freq = (np.float32(10000.0) ** (-np.arange(0, 64, 2, dtype=np.float32) / np.float32(64))).astype(np.float32)
    freqs = np.broadcast_to(freq[None, :], (P, 32))
    masks = np.concatenate([ident, rot, upto, after, causal, chunk, ones, freqs], axis=1).astype(np.float32)
    ang = (np.arange(L1, dtype=np.float32)[:, None] * freq[None, :]).astype(np.float32)
    ang = np.concatenate([ang] * 4, axis=1).T
    turns = np.stack([np.cos(ang), np.sin(ang)], axis=1).astype(np.float32)
    return np.ascontiguousarray(masks), np.ascontiguousarray(turns)


class Steps:

    def __init__(self, sem):
        self.sem, self.count = sem, 0

    def on(self, engine):
        def step(ins):
            self.count += 1
            ins.then_inc(self.sem, 1)
            engine.wait_ge(self.sem, self.count)
        return step


class Machine:

    def __init__(self, nc, ctx, dram):
        self.nc, self.ctx, self.dram = nc, ctx, dram
        self.stage, self.stage_sems, self.cooling = 0, [], []
        self.ps = ctx.enter_context(nc.psum_tensor("ps", [P, 8, 512], F32))
        self.ring_at = 16640
        self.keep_at = self.ring_at + NSLOT * SLOT * 4
        self.keep_end = self.keep_at
        self.ring = self.at("ring", [P, NSLOT, SLOT], self.ring_at)
        self.low_ring = self.ring_at + 6 * SLOT * 4
        self.pieces = self.at("pieces", [P, NPIECE, SLOT], self.low_ring)
        self.high = self.at("pieces_high", [P, NSPLIT, SLOT], self.ring_at, F32R)
        self.low_part = self.at("pieces_low", [P, NSPLIT, SLOT], self.ring_at + NSPLIT * SLOT * 4, F32R)
        self.masks = self.keep("masks", [P, 7 * P + 32])
        self.ident = self.masks[:, 0:P]
        self.rot = self.masks[:, P:2 * P]
        self.upto = self.masks[:, 2 * P:3 * P]
        self.after = self.masks[:, 3 * P:4 * P]
        self.causal = self.masks[:, 4 * P:5 * P]
        self.chunk = self.masks[:, 5 * P:6 * P]
        self.ones = self.masks[:, 6 * P:7 * P]
        self.freqs = self.masks[:, 7 * P:7 * P + 32]
        self.cols = self.keep("cols", [P, 2, P])
        self.eps = self.keep("eps", [P, 1])
        self.lam = self.keep("lam", [P, 1])
        self.gpe = self.keep("gpe", [P, 2, ROPE])
        self.gate_bias = self.keep("gate_bias", [P, 2 * MH])
        self.arena = self.keep_end
        self.dve_steps = Steps(self.lasting("dve_step"))
        self.act_steps = Steps(self.lasting("act_step"))
        self.pool_steps = Steps(self.lasting("pool_step"))
        self.block_loaded = [self.lasting("block_loaded0"), self.lasting("block_loaded1")]
        self.block_free = {}
        self.sent = 0
        self.taken = 0
        self.blocks = []
        self.experts_sent = 0
        self.expert_loaded = [self.lasting(f"expert_loaded{i}") for i in range(NPIECE)]

    def lasting(self, name):
        return self.ctx.enter_context(self.nc.semaphore(name))

    def sem(self, name):
        s = self.nc.alloc_semaphore(name)
        self.stage_sems.append(s)
        return s

    def close(self):
        for s in self.cooling:
            self.nc.release_semaphore(s)
        for s in self.stage_sems:
            self.nc.gpsimd.sem_clear(s)
        self.cooling, self.stage_sems = self.stage_sems, []
        self.stage += 1

    def at(self, name, shape, offset, dt=F32):
        return self.nc.alloc_sbuf_tensor_at(name, shape, dt, offset=offset)

    def keep(self, name, shape, dt=F32):
        t = self.at(name, shape, self.keep_end, dt)
        size = 4 * int(np.prod(shape[1:]))
        self.keep_end += -(-size // 32) * 32
        return t

    def area(self, name, shape, offset, dt=F32):
        assert self.arena + offset + 4 * int(np.prod(shape[1:])) <= 229344, name
        return self.at(name, shape, self.arena + offset, dt)

    def low(self, name, shape, offset):
        assert offset + 4 * int(np.prod(shape[1:])) <= 6 * SLOT * 4
        return self.at(name, shape, self.low_ring + offset)

    def col(self, name, k=0):
        n = self.col_of[name] + k
        return self.cols[:, n // P, n % P:n % P + 1]

    def colrange(self, name, k):
        n = self.col_of[name]
        assert n // P == (n + k - 1) // P, name
        return self.cols[:, n // P, n % P:n % P + k]

    def block_view(self, n):
        _, k, cols = self.blocks[n]
        flat = self.ring[:, 3 * (n % 2):3 * (n % 2) + 3, :].rearrange("p a b -> p (a b)")
        return flat[:, 0:k * cols].rearrange("p (k c) -> p k c", k=k)

    def send_blocks(self, sp, upto):
        while self.sent < min(upto, len(self.blocks)):
            n = self.sent
            src, k, cols = self.blocks[n]
            if n >= 2 and self.block_free[n - 2][0] == self.stage:
                sp.wait_ge(*self.block_free[n - 2][1:])
            sp.dma_start(self.block_view(n), src.rearrange("(k p) c -> p k c", p=P)).then_inc(
                self.block_loaded[n % 2], 16)
            self.sent += 1

    def expert_load(self, sp, j, e, slot):
        w_gate, w_up, w_down = self.dram["w_gate"], self.dram["w_up"], self.dram["w_down"]
        if j < 8 or 12 <= j < 20:
            half = 1 if j < 8 else 0
            i = j if j < 8 else j - 12
            w = w_up if i % 2 else w_gate
            src = w[0, e, 2 * P * (i // 2):2 * P * (i // 2 + 1), half * FH:(half + 1) * FH]
        else:
            half = 0 if j < 12 else 1
            i = j - 8 if j < 12 else j - 20
            src = w_down[0, e, half * FH + 2 * P * i:half * FH + 2 * P * (i + 1), :]
        if len(src.shape) == 3:
            src = src.rearrange("o (k p) c -> p (o k) c", p=P)
        else:
            src = src.rearrange("(k p) c -> p k c", p=P)
        sp.dma_start(self.pieces[:, slot, :].rearrange("p (k c) -> p k c", k=2), src).then_inc(
            self.expert_loaded[slot], 16)

    def send_experts(self, sp, upto):
        while self.experts_sent < upto:
            n = self.experts_sent
            self.expert_load(sp, 12 + n if n < 8 else n - 8, 0, n % NPIECE)
            self.experts_sent += 1

    def wait_block(self, pe, n):
        pe.wait_ge(self.block_loaded[n % 2], 16 * (n // 2 + 1))


def wait_counted(engine, sem, value, passed):
    engine.wait_ge(sem, value)
    engine.sem_inc(passed, 1)


def spread(ap, n):
    p, k = ap.shape
    return ap.unsqueeze(2).to_broadcast([p, k, n])


def norm_stage(m, name, x, tiles, outs, temp, tail=None):
    nc, ps = m.nc, m.ps
    nt = len(tiles)
    normed = m.at(f"{name}_normed", [P, 2, D], temp)
    junk = m.at(f"{name}_junk", [P, D], temp + 8 * D)
    ss = m.at(f"{name}_ss", [P, 3, nt], temp + 12 * D)
    squared = m.sem(f"{name}_squared")
    root_ready = m.sem(f"{name}_root")
    inverse_ready = m.sem(f"{name}_inverse")
    normed_ready = m.sem(f"{name}_normed")
    turned = m.sem(f"{name}_turned")
    evicted = m.sem(f"{name}_evicted")
    stored = [m.sem(f"{name}_stored{i}") for i in range(2)] if tail else None

    with nc.Block() as block:
        if tail:
            @block.sync
            def _(sp):
                tail(sp, normed, normed_ready, stored)

        @block.vector
        def _(dve):
            step = m.dve_steps.on(dve)
            step(nc.vector.memset(ss[:], 1.0))
            for t, (_, n) in enumerate(tiles):
                ins = nc.vector.tensor_tensor_reduce(
                    out=junk[0:n, :], in0=x[0:n, t, :], in1=x[0:n, t, :], scale=1.0 / D, scalar=0.0,
                    op0=ALU.mult, op1=ALU.add, accum_out=ss[0:n, 0, t:t + 1])
                ins.then_inc(squared, 1)
                dve.wait_ge(squared, t + 1)
            dve.wait_ge(root_ready, 1)
            nc.vector.reciprocal(ss[:, 2, :], ss[:, 1, :]).then_inc(inverse_ready, 1)
            u = 0
            for t, (t0, n) in enumerate(tiles):
                for half in range(2):
                    dve.wait_ge(turned, u + 1)
                    bank = ps[:, u % 8, :].rearrange("p (k c) -> p k c", k=4)[:, :, 0:n]
                    for out, gain in outs:
                        g = spread(m.colrange(gain, KD)[:, 4 * half:4 * half + 4], n)
                        ins = nc.vector.tensor_tensor(out[:, 4 * half:4 * half + 4, t0:t0 + n], bank, g, ALU.mult)
                    ins.then_inc(evicted, 1)
                    u += 1

        @block.scalar
        def _(act):
            act.wait_ge(squared, nt)
            nc.scalar.activation(ss[:, 1, :], ss[:, 0, :], ACT.Sqrt, bias=m.eps[:, 0:1]).then_inc(root_ready, 1)
            act.wait_ge(inverse_ready, 1)
            for t, (_, n) in enumerate(tiles):
                if t >= 2:
                    act.wait_ge(turned, 2 * (t - 1))
                    if stored is not None:
                        act.wait_ge(stored[t % 2], 16 * (t // 2))
                nc.scalar.activation(normed[0:n, t % 2, :], x[0:n, t, :], ACT.Copy,
                                     scale=ss[0:n, 2, t:t + 1]).then_inc(normed_ready, 1)

        @block.tensor
        def _(pe):
            u = 0
            for t, (_, n) in enumerate(tiles):
                pe.wait_ge(normed_ready, t + 1)
                for half in range(2):
                    if u >= 8:
                        pe.wait_ge(evicted, u - 7)
                    for k in range(4):
                        f = 4 * half + k
                        ins = pe.transpose(ps[:, u % 8, k * P:k * P + n],
                                           normed[0:n, t % 2, f * P:(f + 1) * P], m.ident[0:n, 0:n])
                    ins.then_inc(turned, 1)
                    u += 1


class Gemm:

    def __init__(self, m, name, jobs, pairs=4):
        self.m, self.name, self.jobs, self.pairs = m, name, jobs, pairs
        self.first = m.taken
        self.ready = m.sem(f"{name}_ready")
        self.out = {"act": m.sem(f"{name}_act_took"), "dve": m.sem(f"{name}_dve_took")}
        self.units = []
        count = {"act": 0, "dve": 0}
        for j, job in enumerate(jobs):
            _, k, cols = m.blocks[self.first + j]
            tiles = job["tiles"]
            n_units = cols // P if job["kind"] == "features" else len(tiles)
            for u in range(n_units):
                count[job["engine"]] += 1
                self.units.append((j, u, job["engine"], count[job["engine"]]))
            m.block_free[self.first + j] = (m.stage, self.ready, len(self.units))
        m.taken += len(jobs)

    def psum(self, n):
        j, u, _, _ = self.units[n]
        job = self.jobs[j]
        pair = 2 * (n % self.pairs)
        ps = self.m.ps
        if job["kind"] == "features":
            tokens = job["act"].shape[2]
            if tokens > 512:
                return ps[:, pair:pair + 2, 0:tokens // 2]
            return ps[:, pair, 0:tokens]
        cols = self.m.blocks[self.first + j][2]
        rows = job["tiles"][u][1]
        return ps[0:rows, pair, 0:cols]

    def products(self, pe, after=None):
        m = self.m
        for n, (j, u, _, _) in enumerate(self.units):
            job = self.jobs[j]
            w = m.block_view(self.first + j)
            k_tiles, cols = m.blocks[self.first + j][1:]
            if u == 0:
                m.wait_block(pe, self.first + j)
                if "needs" in job:
                    pe.wait_ge(*job["needs"])
            if n >= self.pairs:
                _, _, engine, count = self.units[n - self.pairs]
                pe.wait_ge(self.out[engine], count)
            act = job["act"]
            out = self.psum(n)
            if job["kind"] == "features":
                tokens = act.shape[2]
                halves = [(0, tokens)] if tokens <= 512 else [(0, tokens // 2), (tokens // 2, tokens)]
                for h, (a, b) in enumerate(halves):
                    to = out if len(halves) == 1 else out[:, h, :]
                    for k in range(k_tiles):
                        ins = pe.matmul(to, w[:, k, u * P:(u + 1) * P], act[:, k, a:b],
                                        start=(k == 0), stop=(k == k_tiles - 1))
            else:
                t0, rows = job["tiles"][u]
                for k in range(k_tiles):
                    ins = pe.matmul(out, act[:, k, t0:t0 + rows], w[:, k, :],
                                    start=(k == 0), stop=(k == k_tiles - 1))
            ins.then_inc(self.ready, 1)
            if after:
                after(pe, n)

    def take(self, which, engine, step):
        for n, (j, u, name, count) in enumerate(self.units):
            if name != which:
                continue
            engine.wait_ge(self.ready, n + 1)
            ins = self.jobs[j]["take"](step, u, self.psum(n))
            if ins is None:
                engine.sem_inc(self.out[which], 1)
            else:
                ins.then_inc(self.out[which], 1)

    def send(self, sp, ahead=2):
        self.m.send_blocks(sp, self.first + len(self.jobs) + ahead)


def setup_stage(m, h, turns, rows, names):
    nc, ps, dram = m.nc, m.ps, m.dram
    stage = m.area("gain_rows", [P, 2, P], rows)
    lq = m.area("lambda_rows", [P, 4, 64], rows + 1024)
    lw = m.area("lambda_work", [P, 2, 64], rows + 2048)
    ls = m.area("lambda_sums", [P, 4], rows + 2560)
    small = m.sem("small_loaded")
    cleared = m.sem("rows_cleared")
    turned = m.sem("gains_turned")
    sums = m.sem("lambda_sums_ready")
    exps = m.sem("lambda_exps_ready")
    m.tokens_loaded = m.sem("tokens_loaded")
    m.turns_loaded = m.sem("turns_loaded")
    at, m.col_of, loads = 0, {}, []
    for name, src in names:
        k = src.shape[0]
        if at < P and at + k > P:
            at = P
        m.col_of[name] = at
        loads.append((src, at // P, at % P, k))
        at += k
    assert at <= 2 * P
    n_small = 1 + len(loads) + 4 + 2 + 2

    with nc.Block() as block:
        @block.sync
        def _(sp):
            x = dram["x"][0]
            sp.dma_start(h[0:META, 0, :], dram["meta_tokens"]).then_inc(m.tokens_loaded, 16)
            sp.dma_start(h[META:P, 0, :], x[0:P - META, :]).then_inc(m.tokens_loaded, 16)
            for t, (t0, n) in enumerate(TILES1[1:], 1):
                sp.dma_start(h[0:n, t, :], x[t0 - META:t0 - META + n, :]).then_inc(m.tokens_loaded, 16)
            sp.dma_start(m.masks[:], dram["masks"]).then_inc(small, 16)
            sp.wait_ge(cleared, 1)
            for src, g, at, k in loads:
                sp.dma_start(stage[at:at + k, g, :], src).then_inc(small, 16)
            for i, name in enumerate(("lambda_q1", "lambda_k1", "lambda_q2", "lambda_k2")):
                sp.dma_start(lq[:, i, :], dram[name].to_broadcast([P, 64])).then_inc(small, 16)
            for i, src in enumerate((dram["b_q_gain_2"], dram["k_gain_2"].unsqueeze(0))):
                sp.dma_start(m.gpe[:, i, :], src[:, NOPE:].to_broadcast([P, ROPE])).then_inc(small, 16)
            for i, name in enumerate(("a_ig_bias_2", "a_fg_bias_2")):
                sp.dma_start(m.gate_bias[:, MH * i:MH * (i + 1)],
                             dram[name].to_broadcast([P, MH])).then_inc(small, 16)
            sp.dma_start(turns[:], dram["turns"]).then_inc(m.turns_loaded, 16)
            m.send_blocks(sp, 2)
            sp.wait_ge(m.tokens_loaded, 16 * (1 + len(TILES1)))
            sp.wait_ge(m.turns_loaded, 16)

        @block.tensor
        def _(pe):
            pe.wait_ge(small, 16 * n_small)
            for g in range(2):
                ins = pe.transpose(ps[:, g, 0:P], stage[:, g, :], m.ident)
            ins.then_inc(turned, 1)

        @block.vector
        def _(dve):
            step = m.dve_steps.on(dve)
            nc.vector.memset(stage[:], 0.0).then_inc(cleared, 1)
            nc.vector.memset(m.eps[:], EPS)
            dve.wait_ge(small, 16 * n_small)
            for i in range(2):
                ins = nc.vector.tensor_tensor_reduce(
                    out=lw[:, i, :], in0=lq[:, 2 * i, :], in1=lq[:, 2 * i + 1, :], scale=1.0, scalar=0.0,
                    op0=ALU.mult, op1=ALU.add, accum_out=ls[:, i:i + 1])
                ins.then_inc(sums, 1)
            dve.wait_ge(turned, 1)
            step(nc.vector.tensor_copy(m.cols[:], ps[:, 0:2, 0:P]))
            dve.wait_ge(exps, 1)
            step(nc.vector.tensor_tensor(m.lam[:], ls[:, 3:4], ls[:, 2:3], ALU.subtract))
            step(nc.vector.tensor_scalar(m.lam[:], m.lam[:], -LAM_INIT, None, ALU.add))

        @block.scalar
        def _(act):
            act.wait_ge(sums, 2)
            nc.scalar.activation(ls[:, 2:4], ls[:, 0:2], ACT.Exp).then_inc(exps, 1)


def projection_stage(m, hn, qk, v, raw, turns, rot_work):
    nc, ps = m.nc, m.ps
    halved = lambda t: t.rearrange("p (a b) -> p a b", a=2)
    scale = 64.0 ** -0.5

    def take_qk(block):
        def take(step, u, psum):
            return nc.scalar.activation(halved(qk[:, 4 * block + u, :]), psum, ACT.Copy,
                                        scale=scale if block == 0 else 1.0)
        return take

    def take_v(step, u, psum):
        return nc.scalar.activation(v[0:TILES1[u][1], u, :], psum, ACT.Copy)

    def take_raw(part):
        def take(step, u, psum):
            return nc.scalar.activation(halved(raw[:, 4 * part + u, :]), psum, ACT.Copy)
        return take

    takes = [("features", take_qk(0)), ("features", take_qk(1)), ("tokens", take_v)] + [
        ("features", take_raw(i)) for i in range(3)]
    jobs = [dict(kind=kind, act=hn, tiles=TILES1, engine="act", take=take) for kind, take in takes]
    g = Gemm(m, "in1", jobs, pairs=3)
    rotated = m.sem("in1_rotated")
    rot_taken = m.sem("in1_rot_taken")

    with nc.Block() as block:
        @block.sync
        def _(sp):
            g.send(sp)
            m.send_experts(sp, 4)

        @block.tensor
        def _(pe):
            def rotate(n):
                pe.wait_ge(g.out["act"], n + 1)
                if n >= 1:
                    pe.wait_ge(rot_taken, n)
                for a in range(2):
                    ins = pe.matmul(ps[:, 6 + a, 0:HALF1], m.rot, qk[:, n, a * HALF1:(a + 1) * HALF1],
                                    start=True, stop=True)
                ins.then_inc(rotated, 1)

            g.products(pe, lambda pe, n: rotate(n - 1) if 1 <= n <= 8 else None)

        @block.scalar
        def _(act):
            g.take("act", act, m.act_steps.on(act))

        @block.vector
        def _(dve):
            step = m.dve_steps.on(dve)
            for n in range(8):
                dve.wait_ge(rotated, n + 1)
                nc.vector.tensor_tensor(halved(rot_work[:, n % 2, :]), ps[:, 6:8, 0:HALF1],
                                        halved(turns[:, 1, :]), ALU.mult).then_inc(rot_taken, 1)
                step(nc.vector.tensor_tensor(qk[:, n, :], qk[:, n, :], turns[:, 0, :], ALU.mult))
                dve.wait_ge(rot_taken, n + 1)
                step(nc.vector.tensor_tensor(qk[:, n, :], qk[:, n, :], rot_work[:, n % 2, :], ALU.add))


def diff_attention_stage(m, qk, v, raw, mixed, at):
    nc, ps = m.nc, m.ps
    units = [(h, t) for h in range(AH) for t in range(len(TILES1))]
    e = m.area("da_e", [P, 2, 2, L1], at)
    pt = m.area("da_pt", [P, 2, len(TILES1), P], at + 16 * L1)
    at += 16 * L1 + 8 * len(TILES1) * P
    st = m.area("da_st", [P, 2, 8], at)
    ss = m.area("da_ss", [P, 3, len(TILES1) * AH], at + 64)
    qz = m.area("da_qz", [P, 3, 2, P], at + 64 + 256)
    spare = m.ring_at + 10 * SLOT * 4
    o = m.at("da_o", [P, len(TILES1), AH, AV], spare)
    cw = m.at("da_conv", [P, 2, L1], spare + 4 * len(TILES1) * AH * AV)
    junk = m.at("da_junk", [P, AV], spare + 4 * len(TILES1) * AH * AV + 8 * L1)
    scored = m.sem("da_scored")
    maxed = m.sem("da_maxed")
    q_ready = m.sem("da_q_ready")
    exped = m.sem("da_exped")
    mixed_ready = m.sem("da_weights")
    turned = m.sem("da_turned")
    pt_ready = m.sem("da_pt_ready")
    summed = m.sem("da_summed")
    o_ready = m.sem("da_o_ready")
    squared = m.sem("da_squared")
    root = m.sem("da_root")
    scaled = m.sem("da_scaled")
    o_turned = m.sem("da_o_turned")
    cleared = m.sem("da_cleared")
    mixed_taken = m.sem("da_mixed_taken")
    nt = len(TILES1)

    with nc.Block() as block:
        @block.tensor
        def _(pe):
            def scores(u):
                h, t = units[u]
                t0, n = TILES1[t]
                pe.wait_ge(q_ready, 2 * u + 3)
                if u >= 1:
                    pe.wait_ge(exped, 2 * u)
                for i in range(2):
                    for a in range(2):
                        ins = pe.matmul(ps[0:n, 2 * i + a, 0:HALF1], qz[:, u % 3, i, 0:n],
                                        qk[:, 4 + h, a * HALF1:(a + 1) * HALF1], start=True, stop=True)
                    ins.then_inc(scored, 1)

            def values(u):
                h, t = units[u]
                n = TILES1[t][1]
                pe.wait_ge(mixed_ready, u + 1)
                if u >= 1:
                    pe.wait_ge(pt_ready, u)
                for s, (s0, w) in enumerate(TILES1):
                    ins = pe.transpose(ps[0:w, 4 + s // 4, (s % 4) * P:(s % 4) * P + n],
                                       e[0:n, u % 2, 0, s0:s0 + w], m.ident[0:n, 0:n])
                ins.then_inc(turned, 1)
                pe.wait_ge(pt_ready, u + 1)
                if u >= 2:
                    pe.wait_ge(o_ready, u - 1)
                for s, (s0, w) in enumerate(TILES1):
                    ins = pe.matmul(ps[0:n, 6 + u % 2, 0:AV], pt[0:w, u % 2, s, 0:n],
                                    v[0:w, s, h * AV:(h + 1) * AV], start=(s == 0), stop=(s == nt - 1))
                ins.then_inc(summed, 1)

            for u in range(len(units)):
                scores(u)
                if u >= 1:
                    values(u - 1)
            values(len(units) - 1)
            for t, (_, n) in enumerate(TILES1):
                pe.wait_ge(scaled, t + 1)
                for h in range(AH):
                    ins = pe.transpose(ps[:, t % 4, h * P:h * P + n], o[0:n, t, h, :], m.ident[0:n, 0:n])
                ins.then_inc(o_turned, 1)
                if t == 3:
                    pe.wait_ge(mixed_taken, 1)

        @block.vector
        def _(dve):
            step = m.dve_steps.on(dve)
            nc.vector.memset(ss[:], 1.0).then_inc(cleared, 1)
            dve.wait_ge(cleared, 1)
            step(nc.vector.tensor_scalar(m.col("subln"), m.col("subln"), 1.0 - LAM_INIT, None, ALU.mult))

            def combine(u):
                n = TILES1[units[u][1]][1]
                b = u % 2
                dve.wait_ge(exped, 2 * u + 2)
                step(nc.vector.reciprocal(st[0:n, b, 4:6], st[0:n, b, 2:4]))
                step(nc.vector.tensor_tensor(st[0:n, b, 6:7], st[0:n, b, 5:6], m.lam[0:n, :], ALU.mult))
                step(nc.vector.tensor_scalar(e[0:n, b, 1, :], e[0:n, b, 1, :], st[0:n, b, 6:7], None, ALU.mult))
                nc.vector.scalar_tensor_tensor(out=e[0:n, b, 0, :], in0=e[0:n, b, 0, :], scalar=st[0:n, b, 4:5],
                                               in1=e[0:n, b, 1, :], op0=ALU.mult,
                                               op1=ALU.add).then_inc(mixed_ready, 1)

            def squares(u):
                h, t = units[u]
                n = TILES1[t][1]
                dve.wait_ge(o_ready, u + 1)
                nc.vector.tensor_tensor_reduce(
                    out=junk[0:n, :], in0=o[0:n, t, h, :], in1=o[0:n, t, h, :], scale=1.0 / AV, scalar=0.0,
                    op0=ALU.mult, op1=ALU.add,
                    accum_out=ss[0:n, 0, t * AH + h:t * AH + h + 1]).then_inc(squared, 1)
                dve.wait_ge(squared, u + 1)

            for u, (h, t) in enumerate(units):
                n = TILES1[t][1]
                for i in range(2):
                    dve.wait_ge(scored, 2 * u + i + 1)
                    nc.vector.tensor_reduce(st[0:n, u % 2, i:i + 1], ps[0:n, 2 * i:2 * i + 2, 0:HALF1],
                                            AX.XY, ALU.max, negate=True).then_inc(maxed, 1)
                combine(u)
                if u >= 2:
                    squares(u - 2)
            for u in (len(units) - 2, len(units) - 1):
                squares(u)
            dve.wait_ge(root, 1)
            step(nc.vector.reciprocal(ss[:, 2, :], ss[:, 1, :]))
            for t, (_, n) in enumerate(TILES1):
                nc.vector.tensor_tensor(o[0:n, t], o[0:n, t], spread(ss[0:n, 2, t * AH:(t + 1) * AH], AV),
                                        ALU.mult).then_inc(scaled, 1)
            for t, (t0, n) in enumerate(TILES1):
                dve.wait_ge(o_turned, t + 1)
                bank = ps[:, t % 4, :].rearrange("p (k c) -> p k c", k=4)[:, :, 0:n]
                nc.vector.tensor_scalar(mixed[:, 0:AH, t0:t0 + n], bank, m.col("subln"), None,
                                        ALU.mult).then_inc(mixed_taken, 1)

        def after_unit(act, u):
            h, t = units[u]
            n = TILES1[t][1]
            w = TILES1[-1][1]
            act.wait_ge(turned, u + 1)
            nc.scalar.activation(pt[:, u % 2, 0:4, 0:n], ps[:, 4, :].rearrange("p (k c) -> p k c", k=4)[:, :, 0:n],
                                 ACT.Copy)
            nc.scalar.activation(pt[0:w, u % 2, 4, 0:n], ps[0:w, 5, 0:n], ACT.Copy).then_inc(pt_ready, 1)
            act.wait_ge(summed, u + 1)
            nc.scalar.activation(o[0:n, t, h, :], ps[0:n, 6 + u % 2, 0:AV], ACT.Copy).then_inc(o_ready, 1)

        @block.scalar
        def _(act):
            for u, (h, t) in enumerate(units):
                n = TILES1[t][1]
                b = u % 2
                for i in range(2):
                    act.wait_ge(maxed, 2 * u + i + 1)
                    if u >= 2:
                        act.wait_ge(turned, u - 1)
                    nc.scalar.activation(e[0:n, b, i, :].rearrange("p (a c) -> p a c", a=2),
                                         ps[0:n, 2 * i:2 * i + 2, 0:HALF1], ACT.Exp, bias=st[0:n, b, i:i + 1],
                                         accum_out=st[0:n, b, 2 + i:3 + i]).then_inc(exped, 1)
                if u >= 1:
                    after_unit(act, u - 1)
            after_unit(act, len(units) - 1)
            act.wait_ge(squared, len(units))
            nc.scalar.activation(ss[:, 1, :], ss[:, 0, :], ACT.Sqrt, bias=m.eps[:, 0:1]).then_inc(root, 1)

        @block.gpsimd
        def _(pool):
            step = m.pool_steps.on(pool)
            g = nc.gpsimd
            g.memset(qz[:], 0.0).then_inc(q_ready, 1)
            pool.wait_ge(q_ready, 1)

            def queries(u):
                h, t = units[u]
                t0, n = TILES1[t]
                if u >= 3:
                    pool.wait_ge(scored, 2 * (u - 2))
                for i in range(2):
                    d = slice(64 * i, 64 * i + 64)
                    g.tensor_copy(qz[d, u % 3, i, 0:n], qk[d, h, t0:t0 + n]).then_inc(q_ready, 1)
                    pool.wait_ge(q_ready, 2 * u + i + 2)

            def convolution(c):
                cx, cb, cc = raw[:, c, :], raw[:, 4 + c, :], raw[:, 8 + c, :]
                yield g.tensor_tensor(cc, cc, cx, ALU.mult)
                yield g.tensor_scalar(cw[:, 0, :], cc, m.col("conv_w", 4 + c), None, ALU.mult)
                yield g.tensor_scalar(cw[:, 1, :], cc, m.col("conv_w", c), None, ALU.mult)
                yield g.tensor_tensor(cw[:, 0, 1:], cw[:, 0, 1:], cw[:, 1, 0:L1 - 1], ALU.add)
                yield g.tensor_scalar(cw[:, 1, :], cc, m.col("conv_w", 8 + c), None, ALU.mult)
                yield g.tensor_tensor(cw[:, 0, 0:L1 - 1], cw[:, 0, 0:L1 - 1], cw[:, 1, 1:], ALU.add)
                yield g.tensor_tensor(mixed[:, AH + c, :], cw[:, 0, :], cb, ALU.mult)

            conv = (ins for c in range(4) for ins in convolution(c))
            for u in range(len(units)):
                queries(u)
                if u >= 2:
                    for _ in range(2):
                        ins = next(conv, None)
                        if ins is not None:
                            step(ins)


def out_stage(m, name, mixed, x, tiles, ahead=2, tail=None):
    nc = m.nc

    def take(c):
        def f(step, u, psum):
            n = tiles[u][1]
            to = x[0:n, u, c * 512:(c + 1) * 512]
            return nc.vector.tensor_tensor(to, psum, to, ALU.add)
        return f

    jobs = [dict(kind="tokens", act=mixed, tiles=tiles, engine="dve", take=take(c)) for c in range(2)]
    g = Gemm(m, name, jobs)
    with nc.Block() as block:
        @block.sync
        def _(sp):
            g.send(sp, ahead)
            if tail:
                tail(sp, g)

        @block.tensor
        def _(pe):
            g.products(pe)

        @block.vector
        def _(dve):
            g.take("dve", dve, None)


def router_stage(m, hn, at):
    nc, ps = m.nc, m.ps
    nt = len(TILES1)
    w = m.area("router_w", [P, KD, NE], at)
    aff = m.area("router_aff", [P, nt, NE], at + 512)
    st = m.area("router_st", [P, 3, 8], at + 832)
    afft = m.area("router_afft", [NE, 2, L1], at + 960)
    vals = m.area("router_vals", [NE, 8 * ROUNDS], at + 960 + 8 * L1)
    idx = m.area("router_idx", [NE, 8 * ROUNDS], at + 1280 + 8 * L1, U32)
    idxf = m.area("router_idxf", [NE, 8 * ROUNDS], at + 1600 + 8 * L1)
    loaded = m.sem("router_loaded")
    scored = m.sem("router_scored")
    shifted = m.sem("router_shifted")
    exped = m.sem("router_exped")
    normed = m.sem("router_normed")
    turned = m.sem("router_turned")
    picked = m.sem("router_picked")
    picks_turned = m.sem("router_picks_turned")

    with nc.Block() as block:
        @block.sync
        def _(sp):
            sp.dma_start(w[:], m.dram["w_router"][0].rearrange("(k p) e -> p k e", p=P)).then_inc(loaded, 16)
            m.send_experts(sp, NPIECE)

        @block.tensor
        def _(pe):
            pe.wait_ge(loaded, 16)
            for t, (t0, n) in enumerate(TILES1):
                for k in range(KD):
                    ins = pe.matmul(ps[0:n, t, 0:NE], hn[:, k, t0:t0 + n], w[:, k, :],
                                    start=(k == 0), stop=(k == KD - 1))
                ins.then_inc(scored, 1)
            pe.wait_ge(normed, 1)
            for t, (_, n) in enumerate(TILES1):
                ins = pe.transpose(ps[0:NE, 6 + t // 4, (t % 4) * P:(t % 4) * P + n], aff[0:n, t, :],
                                   m.ident[0:n, 0:n])
            ins.then_inc(turned, 1)
            pe.wait_ge(picked, 1)
            pe.transpose(ps[0:CAP, 0, 0:NE], vals[:, 0:CAP], m.ident[0:NE, 0:NE])
            pe.transpose(ps[0:CAP, 0, NE:2 * NE], idxf[:, 0:CAP], m.ident[0:NE, 0:NE]).then_inc(picks_turned, 1)

        @block.vector
        def _(dve):
            step = m.dve_steps.on(dve)
            step(nc.vector.memset(aff[:], 0.0))
            for t, (_, n) in enumerate(TILES1):
                dve.wait_ge(scored, t + 1)
                step(nc.vector.tensor_copy(aff[0:n, t, :], ps[0:n, t, 0:NE]))
            step(nc.vector.tensor_reduce(st[:, 0, 0:nt], aff[:], AX.X, ALU.max))
            nc.vector.tensor_tensor(aff[:], aff[:], spread(st[:, 0, 0:nt], NE), ALU.subtract).then_inc(shifted, 1)
            dve.wait_ge(exped, 1)
            step(nc.vector.tensor_reduce(st[:, 1, 0:nt], aff[:], AX.X, ALU.add))
            step(nc.vector.reciprocal(st[:, 2, 0:nt], st[:, 1, 0:nt]))
            nc.vector.tensor_tensor(aff[:], aff[:], spread(st[:, 2, 0:nt], NE), ALU.mult).then_inc(normed, 1)
            dve.wait_ge(turned, 1)
            nc.vector.tensor_copy(afft[:, 0, 0:512], ps[0:NE, 6, :])
            step(nc.vector.tensor_copy(afft[:, 0, 512:L1], ps[0:NE, 7, 0:L1 - 512]))
            for r in range(ROUNDS):
                a = afft[:, r % 2, :]
                best = vals[:, 8 * r:8 * r + 8]
                step(nc.vector.max(best, a))
                step(nc.vector.max_index(idx[:, 8 * r:8 * r + 8], best, a))
                if r + 1 < ROUNDS:
                    step(nc.vector.match_replace(afft[:, (r + 1) % 2, :], best, a, -1.0))
            nc.vector.tensor_copy(idxf[:], idx[:]).then_inc(picked, 1)
            dve.wait_ge(picks_turned, 1)
            nc.vector.tensor_copy(m.gates[:], ps[0:CAP, 0, 0:NE])
            step(nc.vector.tensor_copy(m.rows[:], ps[0:CAP, 0, NE:2 * NE]))

        @block.scalar
        def _(act):
            act.wait_ge(shifted, 1)
            nc.scalar.activation(aff[:], aff[:], ACT.Exp).then_inc(exped, 1)


def experts_stage(m, at):
    nc, ps = m.nc, m.ps
    PIECES = 24
    FIRST = 8
    AHEAD = 2
    size = 4 * KD * CAP
    xg = m.area("ex_rows", [CAP, D], at)
    hid = m.area("ex_hidden", [CAP, FH], at + 4096)
    y = m.area("ex_y", [CAP, D], at + 8192)
    at += 12288
    x_part = [m.area(f"ex_x{i}", [P, KD, CAP], at + size * i, F32R) for i in range(2)]
    h_part = [m.area(f"ex_h{i}", [P, KD, CAP], at + size * (2 + i), F32R) for i in range(2)]
    xs = m.area("ex_x_scaled", [P, KD, CAP], at + size * 4)
    at += 5 * size
    rows_in = m.area("ex_rows_in", [CAP, 1], at, U32)
    rows_out = m.area("ex_rows_out", [CAP, 1], at + 32, U32)
    gate = m.area("ex_gate", [CAP, 1], at + 64)
    high_done = m.sem("ex_high_done")
    low_done = m.sem("ex_low_done")
    used = m.sem("ex_pieces_used")
    silu_done = m.sem("ex_silu_done")
    hid_done = m.sem("ex_hidden_done")
    turned = m.sem("ex_hidden_turned")
    h_high = m.sem("ex_h_high")
    h_done = m.sem("ex_h_split")
    rows_ready = m.sem("ex_rows_ready")
    gathered = m.lasting("ex_gathered")
    x_turned = m.sem("ex_x_turned")
    x_scaled = m.sem("ex_x_scaled")
    x_high = m.sem("ex_x_high")
    x_done = m.sem("ex_x_split")
    gate_ready = m.sem("ex_gate_ready")
    y_done = m.sem("ex_y_done")
    y_free = m.sem("ex_y_free")
    scattered = m.lasting("ex_scattered")
    sp_passed = m.sem("ex_sp_waits_passed")
    pool_passed = m.sem("ex_pool_waits_passed")
    quarter = lambda bank: bank[:, 0:4 * CAP].rearrange("p (k c) -> p k c", k=4)

    with nc.Block() as block:
        @block.sync
        def _(sp):
            for n in range(NPIECE, 12):
                sp.wait_ge(low_done, n - NPIECE + 1)
                m.expert_load(sp, 12 + n if n < FIRST else n - FIRST, 0, n % NPIECE)
            with sp.Fori(0, NE - 1) as e:
                for i in range(PIECES):
                    wait_counted(sp, low_done, e * PIECES + (12 - NPIECE + 1 + i), sp_passed)
                    j = (4 + i) % PIECES
                    ahead = (4 + i) // PIECES + (1 if 12 <= j < 20 else 0)
                    m.expert_load(sp, j, bass.ds(e + ahead, 1), i % NPIECE)
            n = 12 + PIECES * (NE - 1)
            for j in list(range(4, 12)) + list(range(20, 24)):
                sp.wait_ge(low_done, n - NPIECE + 1)
                m.expert_load(sp, j, NE - 1, n % NPIECE)
                n += 1

        @block.tensor
        def _(pe):
            first_unit = 0

            def products(n, e, banks, parts, k0, start, stop):
                pe.wait_ge(low_done, e * PIECES + (n + 1))
                w = [x[:, n % NSPLIT, :].rearrange("p (k c) -> p k c", k=2) for x in (m.high, m.low_part)]
                for k in range(2):
                    for a, b in ((0, 0), (0, 1), (1, 0)):
                        for c in range(2):
                            ins = pe.matmul(ps[0:CAP, banks + c, :], parts[a][:, k0 + k, :],
                                            w[b][:, k, c * 512:(c + 1) * 512],
                                            start=start and k == 0 and a == b == 0,
                                            stop=stop and k == 1 and a == 1)
                ins.then_inc(used, 1)

            def gate_up(n, e, unit, turn_unit=None):
                for i in range(8):
                    if i == 0 and unit is not first_unit:
                        pe.wait_ge(hid_done, unit)
                    products(n + i, e, 2 * (i % 2), x_part, 2 * (i // 2), i < 2, i >= 6)
                    if i == 3 and turn_unit is not None:
                        turn(turn_unit)

            def turn(unit):
                for k in range(KD):
                    ins = pe.transpose(ps[:, 6 + k // 4, (k % 4) * CAP:(k % 4 + 1) * CAP],
                                       hid[:, k * P:(k + 1) * P], m.ident[0:CAP, 0:CAP])
                ins.then_inc(turned, 1)

            def turn_x(count):
                pe.wait_ge(gathered, count * 16)
                for k in range(KD):
                    ins = pe.transpose(ps[:, 6 + k // 4, (k % 4) * CAP:(k % 4 + 1) * CAP],
                                       xg[:, k * P:(k + 1) * P], m.ident[0:CAP, 0:CAP])
                ins.then_inc(x_turned, 1)

            def down(n, e, unit, half, next_x=None):
                for i in range(4):
                    if i == 0:
                        pe.wait_ge(h_done, unit + 1)
                        if half == 0:
                            pe.wait_ge(y_free, e + 1)
                    products(n + i, e, 4, h_part, 2 * i, half == 0 and i == 0, half == 1 and i == 3)
                    if i == 0 and next_x is not None:
                        turn_x(next_x)

            turn_x(1)
            pe.wait_ge(x_done, 1)
            gate_up(0, 0, first_unit)
            with pe.Fori(0, NE - 1) as e:
                gate_up(FIRST, e, e * 2 + 1, turn_unit=e * 2)
                down(FIRST + 8, e, e * 2, 0, next_x=e + 2)
                pe.wait_ge(x_done, e + 2)
                gate_up(FIRST + 12, e, e * 2 + 2, turn_unit=e * 2 + 1)
                down(FIRST + 20, e, e * 2 + 1, 1)
            e = NE - 1
            gate_up(FIRST, e, e * 2 + 1, turn_unit=e * 2)
            down(FIRST + 8, e, e * 2, 0)
            pe.wait_ge(hid_done, e * 2 + 2)
            turn(e * 2 + 1)
            down(FIRST + 12, e, e * 2 + 1, 1)

        @block.scalar
        def _(act):
            def high(n, e=None):
                rounds = 16 * (n // NPIECE + 1)
                act.wait_ge(m.expert_loaded[n % NPIECE],
                            rounds if e is None else e * (16 * PIECES // NPIECE) + rounds)
                if e is not None:
                    act.wait_ge(used, e * PIECES + (n - NSPLIT + 1))
                elif n >= NSPLIT:
                    act.wait_ge(used, n - NSPLIT + 1)
                nc.scalar.activation(m.high[:, n % NSPLIT, :], m.pieces[:, n % NPIECE, :],
                                     ACT.Copy).then_inc(high_done, 1)

            def silu(pieces):
                act.wait_ge(used, pieces)
                nc.scalar.activation(hid[:].rearrange("p (a c) -> p a c", a=2), ps[0:CAP, 0:2, :],
                                     ACT.Silu).then_inc(silu_done, 1)

            def take_turned(unit):
                act.wait_ge(turned, unit + 1)
                nc.scalar.activation(h_part[0][:].rearrange("p (a k) c -> p a (k c)", a=2),
                                     ps[:, 6:8, 0:4 * CAP], ACT.Copy).then_inc(h_high, 1)

            for n in range(FIRST + AHEAD):
                high(n)
            silu(FIRST)
            with act.Fori(0, NE - 1) as e:
                for i in range(PIECES):
                    high(FIRST + AHEAD + i, e)
                    if i == 3:
                        take_turned(e * 2)
                    if i == 7:
                        silu(e * PIECES + (FIRST + 8))
                    if i == 15:
                        take_turned(e * 2 + 1)
                    if i == 19:
                        silu(e * PIECES + (FIRST + 20))
            base = PIECES * (NE - 1) + FIRST
            for i in range(16):
                if i + AHEAD < 16:
                    high(base + AHEAD + i)
                if i == 3:
                    take_turned(2 * NE - 2)
                if i == 7:
                    silu(base + 8)
                if i == 11:
                    take_turned(2 * NE - 1)

        @block.vector
        def _(dve):
            def low(n, e=None):
                dve.wait_ge(high_done, n + 1 if e is None else e * PIECES + (n + 1))
                nc.vector.tensor_tensor(m.low_part[:, n % NSPLIT, :], m.pieces[:, n % NPIECE, :],
                                        m.high[:, n % NSPLIT, :].bitcast(F32), ALU.subtract).then_inc(low_done, 1)

            def next_rows(e):
                nc.vector.tensor_copy(rows_in[:], m.rows[:, bass.ds(e, 1)]).then_inc(rows_ready, 1)

            def hidden(unit):
                dve.wait_ge(silu_done, unit + 1)
                h = hid[:].rearrange("p (a c) -> p a c", a=2)
                nc.vector.tensor_tensor(h, ps[0:CAP, 2:4, :], h, ALU.mult).then_inc(hid_done, 1)

            def split_hidden(unit):
                dve.wait_ge(h_high, unit + 1)
                for a in range(2):
                    ins = nc.vector.tensor_tensor(h_part[1][:, 4 * a:4 * a + 4, :], quarter(ps[:, 6 + a, :]),
                                                  h_part[0][:, 4 * a:4 * a + 4, :].bitcast(F32), ALU.subtract)
                ins.then_inc(h_done, 1)

            def take_x(count):
                dve.wait_ge(x_turned, count)
                for a in range(2):
                    ins = nc.vector.tensor_tensor(xs[:, 4 * a:4 * a + 4, :], quarter(ps[:, 6 + a, :]),
                                                  spread(m.colrange("ffn_g", KD)[:, 4 * a:4 * a + 4], CAP),
                                                  ALU.mult)
                ins.then_inc(x_scaled, 1)
                dve.wait_ge(x_scaled, count)
                nc.vector.tensor_copy(x_part[0][:], xs[:]).then_inc(x_high, 1)
                dve.wait_ge(x_high, count)
                nc.vector.tensor_tensor(x_part[1][:], xs[:], x_part[0][:].bitcast(F32),
                                        ALU.subtract).then_inc(x_done, 1)

            def take_y(e, pieces):
                dve.wait_ge(y_free, e + 1)
                nc.vector.tensor_copy(rows_out[:], m.rows[:, bass.ds(e, 1)])
                nc.vector.tensor_copy(gate[:], m.gates[:, bass.ds(e, 1)]).then_inc(gate_ready, 1)
                dve.wait_ge(gate_ready, e + 1)
                dve.wait_ge(used, pieces)
                nc.vector.tensor_scalar(y[:].rearrange("p (a c) -> p a c", a=2), ps[0:CAP, 4:6, :],
                                        gate[:, 0:1], None, ALU.mult).then_inc(y_done, 1)

            next_rows(0)
            for n in range(FIRST + AHEAD):
                low(n)
                if n == 0:
                    take_x(1)
            hidden(0)
            with dve.Fori(0, NE - 1) as e:
                for i in range(PIECES):
                    if i == 0:
                        dve.wait_ge(gathered, e * 16 + 16)
                        next_rows(e + 1)
                    low(FIRST + AHEAD + i, e)
                    if i == 3:
                        split_hidden(e * 2)
                    if i == 7:
                        hidden(e * 2 + 1)
                    if i == 8:
                        take_x(e + 2)
                    if i == 15:
                        split_hidden(e * 2 + 1)
                    if i == 19:
                        hidden(e * 2 + 2)
                    if i == 23:
                        take_y(e, e * PIECES + (FIRST + 24))
            base = PIECES * (NE - 1) + FIRST
            for i in range(16):
                if i + AHEAD < 16:
                    low(base + AHEAD + i)
                if i == 3:
                    split_hidden(2 * NE - 2)
                if i == 7:
                    hidden(2 * NE - 1)
                if i == 11:
                    split_hidden(2 * NE - 1)
            take_y(NE - 1, NE * PIECES)

        @block.gpsimd
        def _(pool):
            def gather(count):
                wait_counted(pool, rows_ready, count, pool_passed)
                nc.gpsimd.indirect_dma_start(
                    out=xg[:], out_offset=None, in_=m.xhat[:],
                    in_offset=bass.IndirectOffsetOnAxis(ap=rows_in[:, 0:1], axis=0)).then_inc(gathered, 16)

            def scatter(e):
                wait_counted(pool, y_done, e + 1, pool_passed)
                nc.gpsimd.indirect_dma_start(
                    out=m.resid[:], out_offset=bass.IndirectOffsetOnAxis(ap=rows_out[:, 0:1], axis=0),
                    in_=y[:], in_offset=None, compute_op=ALU.add).then_inc(scattered, 16)
                pool.wait_ge(scattered, e * 16 + 16)
                pool.sem_inc(y_free, 1)

            pool.sem_inc(y_free, 1)
            gather(1)
            with pool.Fori(0, NE - 1) as e:
                wait_counted(pool, x_turned, e + 1, pool_passed)
                gather(e + 2)
                scatter(e)
            scatter(NE - 1)


def final_norm_stage(m, x, at):
    nc = m.nc
    grow = m.area("fin_gain", [P, D], at)
    junk = m.area("fin_junk", [P, D], at + 4096)
    ss = m.area("fin_ss", [P, 3, 4], at + 8192)
    gain_loaded = m.sem("fin_gain_loaded")
    loaded = [m.sem(f"fin_loaded{t}") for t in range(4)]
    squared = m.sem("fin_squared")
    root = m.sem("fin_root")
    with nc.Block() as block:
        @block.sync
        def _(sp):
            for t in range(4):
                sp.dma_start(x[:, t, :], m.resid[META + t * P:META + (t + 1) * P, :]).then_inc(loaded[t], 16)
            sp.dma_start(grow[:], m.dram["final_norm_g"].unsqueeze(0).to_broadcast([P, D])).then_inc(gain_loaded, 16)
            m.send_blocks(sp, m.taken + 2)

        @block.vector
        def _(dve):
            step = m.dve_steps.on(dve)
            for t in range(4):
                dve.wait_ge(loaded[t], 16)
                nc.vector.tensor_tensor_reduce(
                    out=junk[:], in0=x[:, t, :], in1=x[:, t, :], scale=1.0 / D, scalar=0.0,
                    op0=ALU.mult, op1=ALU.add, accum_out=ss[:, 0, t:t + 1]).then_inc(squared, 1)
                dve.wait_ge(squared, t + 1)
            dve.wait_ge(root, 1)
            step(nc.vector.reciprocal(ss[:, 2, :], ss[:, 1, :]))
            dve.wait_ge(gain_loaded, 16)
            for t in range(4):
                step(nc.vector.scalar_tensor_tensor(out=x[:, t, :], in0=x[:, t, :], scalar=ss[:, 2, t:t + 1],
                                                    in1=grow[:], op0=ALU.mult, op1=ALU.mult))

        @block.scalar
        def _(act):
            act.wait_ge(squared, 4)
            nc.scalar.activation(ss[:, 1, :], ss[:, 0, :], ACT.Sqrt, bias=m.eps[:, 0:1]).then_inc(root, 1)


def group_norm_stage(m, name, jobs, at):
    nc, ps = m.nc, m.ps
    n_ss = sum(j["src"].shape[1] * j["src"].shape[2] for j in jobs)
    ss = m.area(f"{name}_ss", [P, 3, n_ss], at)
    junk = m.area(f"{name}_junk", [P, 512], at + -(-12 * n_ss // 32) * 32)
    squared = m.sem(f"{name}_squared")
    root = m.sem(f"{name}_root")
    scaled = m.sem(f"{name}_scaled")
    turned = m.sem(f"{name}_turned")
    taken = m.sem(f"{name}_taken")
    work, c = [], 0
    for j in jobs:
        _, nt, g, width = j["src"].shape
        for t in range(nt):
            work.append((j, t, g, width, c))
            c += g

    with nc.Block() as block:
        @block.vector
        def _(dve):
            step = m.dve_steps.on(dve)
            for j, t, g, width, c in work:
                x = j["src"][:, t]
                sq = junk[:, 0:g * width].rearrange("p (g w) -> p g w", g=g)
                step(nc.vector.tensor_tensor(sq, x, x, ALU.mult))
                step(nc.vector.tensor_reduce(ss[:, 0, c:c + g], sq, AX.X, ALU.add))
                step(nc.vector.tensor_scalar(ss[:, 0, c:c + g], ss[:, 0, c:c + g], 1.0 / width, None, ALU.mult))
            nc.vector.tensor_copy(ss[:, 2, :], ss[:, 0, :]).then_inc(squared, 1)
            dve.wait_ge(root, 1)
            step(nc.vector.reciprocal(ss[:, 2, :], ss[:, 1, :]))
            for j, t, g, width, c in work:
                x = j["src"][:, t]
                nc.vector.tensor_tensor(x, x, spread(ss[:, 2, c:c + g], width), ALU.mult).then_inc(scaled, 1)
            for n, (j, t, g, width, c) in enumerate(work):
                dve.wait_ge(turned, n + 1)
                per = width // P
                bank = ps[:, n % 8, :].rearrange("p (k c) -> p k c", k=4)
                for i in range(per):
                    ins = nc.vector.tensor_scalar(
                        j["dst"][:, i:g * per:per, t * P:(t + 1) * P], bank[:, i:g * per:per, :],
                        m.col(j["gain"][0], j["gain"][1] + i), j["factor"], ALU.mult, ALU.mult)
                ins.then_inc(taken, 1)

        @block.scalar
        def _(act):
            act.wait_ge(squared, 1)
            nc.scalar.activation(ss[:, 1, :], ss[:, 0, :], ACT.Sqrt, bias=m.eps[:, 0:1]).then_inc(root, 1)

        @block.tensor
        def _(pe):
            for n, (j, t, g, width, c) in enumerate(work):
                pe.wait_ge(scaled, n + 1)
                if n >= 8:
                    pe.wait_ge(taken, n - 7)
                x = j["src"][:, t].rearrange("p g w -> p (g w)")
                for i in range(g * width // P):
                    ins = pe.transpose(ps[:, n % 8, i * P:(i + 1) * P], x[:, i * P:(i + 1) * P], m.ident)
                ins.then_inc(turned, 1)


def attention_stage(m, name, units, at):
    nc, ps = m.nc, m.ps
    probs = m.area(f"{name}_probs", [P, 3, 512], at)
    pt = m.area(f"{name}_pt", [P, 2, 512], at + 6144)
    st = m.area(f"{name}_st", [P, 3, 4], at + 10240)
    scored = m.sem(f"{name}_scored")
    maxed = m.sem(f"{name}_maxed")
    exped = m.sem(f"{name}_exped")
    ready = m.sem(f"{name}_ready")
    turned = m.sem(f"{name}_turned")
    pt_ready = m.sem(f"{name}_pt_ready")
    summed = m.sem(f"{name}_summed")
    taken = m.sem(f"{name}_taken")
    nu = len(units)

    with nc.Block() as block:
        @block.tensor
        def _(pe):
            def scores(u):
                if u >= 2:
                    pe.wait_ge(exped, u - 1)
                for i, (lhs, rhs) in enumerate(units[u]["scores"]):
                    ins = pe.matmul(ps[:, u % 2, 0:units[u]["width"]], lhs, rhs,
                                    start=(i == 0), stop=(i == len(units[u]["scores"]) - 1))
                ins.then_inc(scored, 1)

            def turn(u):
                pe.wait_ge(ready, u + 1)
                if u >= 2:
                    pe.wait_ge(pt_ready, u - 1)
                for s in range(units[u]["width"] // P):
                    ins = pe.transpose(ps[:, 2 + u % 2, s * P:(s + 1) * P], probs[:, u % 3, s * P:(s + 1) * P],
                                       m.ident)
                ins.then_inc(turned, 1)

            def values(u):
                pe.wait_ge(pt_ready, u + 1)
                if u >= 2:
                    pe.wait_ge(taken, u - 1)
                vs = units[u]["values"]
                for s, v in enumerate(vs):
                    ins = pe.matmul(ps[:, 4 + u % 2, 0:P], v, pt[:, u % 2, s * P:(s + 1) * P],
                                    start=(s == 0), stop=(s == len(vs) - 1))
                ins.then_inc(summed, 1)

            for u in range(nu + 2):
                if u < nu:
                    scores(u)
                if 1 <= u <= nu:
                    turn(u - 1)
                if u >= 2:
                    values(u - 2)

        @block.vector
        def _(dve):
            step = m.dve_steps.on(dve)

            def head(u):
                w = units[u]["width"]
                dve.wait_ge(scored, u + 1)
                s = ps[:, u % 2, 0:w]
                if units[u]["mask"] is not None:
                    step(nc.vector.tensor_tensor(s[:, w - P:w], s[:, w - P:w], units[u]["mask"], ALU.add))
                nc.vector.tensor_reduce(st[:, u % 3, 0:1], s, AX.X, ALU.max, negate=True).then_inc(maxed, 1)

            def norm(u):
                w = units[u]["width"]
                dve.wait_ge(exped, u + 1)
                step(nc.vector.reciprocal(st[:, u % 3, 2:3], st[:, u % 3, 1:2]))
                p = probs[:, u % 3, 0:w]
                nc.vector.tensor_scalar(p, p, st[:, u % 3, 2:3], None, ALU.mult).then_inc(ready, 1)

            def take(u):
                dve.wait_ge(summed, u + 1)
                y = units[u]["y"]
                nc.vector.tensor_tensor(y, ps[:, 4 + u % 2, 0:P], y, ALU.mult).then_inc(taken, 1)

            for u in range(nu + 3):
                if u < nu:
                    head(u)
                if 1 <= u <= nu:
                    norm(u - 1)
                if u >= 3:
                    take(u - 3)

        @block.scalar
        def _(act):
            for u in range(nu + 1):
                if u < nu:
                    w = units[u]["width"]
                    act.wait_ge(maxed, u + 1)
                    if u >= 3:
                        act.wait_ge(turned, u - 2)
                    nc.scalar.activation(probs[:, u % 3, 0:w], ps[:, u % 2, 0:w], ACT.Exp,
                                         bias=st[:, u % 3, 0:1], accum_out=st[:, u % 3, 1:2]).then_inc(exped, 1)
                if u >= 1:
                    w = units[u - 1]["width"]
                    act.wait_ge(turned, u)
                    if u >= 3:
                        act.wait_ge(summed, u - 2)
                    nc.scalar.activation(pt[:, (u - 1) % 2, 0:w], ps[:, 2 + (u - 1) % 2, 0:w],
                                         ACT.Copy).then_inc(pt_ready, 1)


def memory_units(mq, mk, mv, y):
    return [dict(scores=[(mq[:, h, t * P:(t + 1) * P], mk[:, h, :])], width=MEM, mask=None,
                 values=[mv[:, s, h * P:(h + 1) * P] for s in range(MEM // P)],
                 y=y[:, 8 + h, t * P:(t + 1) * P])
            for h in range(MEMH) for t in range(4)]


def memory_stage(m, mem_t, mk_tok, mvs):
    nc = m.nc
    tiles = [(0, P), (P, P)]

    def take(dst):
        def f(step, u, psum):
            return nc.scalar.activation(dst[:, u, :], psum, ACT.Copy)
        return f

    jobs = [dict(kind="tokens", act=mem_t, tiles=tiles, engine="act", take=take(dst))
            for dst in (mk_tok[0], mvs[0], mk_tok[1], mvs[1])]
    g = Gemm(m, "mem", jobs)
    with nc.Block() as block:
        @block.sync
        def _(sp):
            g.send(sp)

        @block.tensor
        def _(pe):
            g.products(pe)

        @block.scalar
        def _(act):
            g.take("act", act, None)


def mlstm_in_stage(m, hn, qk, v, y, mq, gates, at):
    nc = m.nc
    raw = m.area("ml_raw", [P, 3, SEQ + 3], at)
    acc = m.area("ml_acc", [P, 2, SEQ], at + 6208)
    zs = m.area("ml_zs", [P, 2, SEQ], at + 6208 + 8 * SEQ)
    padded = m.sem("ml_padded")
    raw_ready = m.sem("ml_raw_ready")
    conv_done = m.sem("ml_conv_done")
    silu_done = m.sem("ml_silu_done")
    z_ready = m.sem("ml_z_ready")
    z_used = m.sem("ml_z_used")
    act = nc.scalar
    NQK = 2 * MW // P

    def finish(n):
        act.wait_ge(conv_done, n + 1)
        act.activation(qk[:, n, :], acc[:, n % 2, :], ACT.Silu,
                       bias=m.col("a_conv_b", n)).then_inc(silu_done, 1)

    def take_qk(block):
        def f(step, u, psum):
            n = 4 * block + u
            if n == 0:
                act.wait_ge(padded, 1)
            if n >= 2:
                finish(n - 2)
            act.activation(raw[:, n % 3, 3:], psum, ACT.Copy).then_inc(raw_ready, 1)
            act.wait_ge(raw_ready, n + 1)
            return None
        return f

    def take_v(block):
        def f(step, u, psum):
            if block == 0 and u < 2:
                finish(NQK - 2 + u)
            return act.activation(v[:, u, 512 * block:512 * (block + 1)], psum, ACT.Copy)
        return f

    def take_o(block):
        return lambda step, u, psum: act.activation(y[:, 4 * block + u, :], psum, ACT.Tanh, scale=0.5)

    def take_z(block):
        def f(step, u, psum):
            n = 4 * block + u
            if n >= 2:
                act.wait_ge(z_used, n - 1)
            act.activation(zs[:, n % 2, :], psum, ACT.Silu).then_inc(z_ready, 1)
            act.wait_ge(z_ready, n + 1)
            return None
        return f

    def take_gates(step, u, psum):
        return act.activation(gates[:, u, :], psum, ACT.Copy)

    def take_mq(step, u, psum):
        return act.activation(mq[:, u, :], psum, ACT.Copy)

    def take_mz(step, u, psum):
        return act.activation(y[:, 8 + u, :], psum, ACT.Silu)

    takes = [("features", take_qk(b)) for b in range(4)] + [("tokens", take_v(b)) for b in range(2)] + \
        [("features", take_o(b)) for b in range(2)] + [("features", take_z(b)) for b in range(2)] + \
        [("tokens", take_gates), ("tokens", take_mq), ("features", take_mz)]
    jobs = [dict(kind=k, act=hn, tiles=TILES2, engine="act", take=t) for k, t in takes]
    g = Gemm(m, "in2", jobs)

    with nc.Block() as block:
        @block.sync
        def _(sp):
            g.send(sp)

        @block.tensor
        def _(pe):
            g.products(pe)

        @block.scalar
        def _(act):
            g.take("act", act, None)

        @block.vector
        def _(dve):
            step = m.dve_steps.on(dve)
            nc.vector.memset(raw[:, :, 0:3], 0.0).then_inc(padded, 1)
            for n in range(NQK):
                dve.wait_ge(raw_ready, n + 1)
                if n >= 2:
                    dve.wait_ge(silu_done, n - 1)
                r, a = raw[:, n % 3, :], acc[:, n % 2, :]
                step(nc.vector.tensor_scalar(a, r[:, 3:], m.col("a_conv_w", 3 * NQK + n), None, ALU.mult))
                for j in (2, 1, 0):
                    ins = nc.vector.scalar_tensor_tensor(out=a, in0=r[:, j:j + SEQ],
                                                         scalar=m.col("a_conv_w", j * NQK + n), in1=a,
                                                         op0=ALU.mult, op1=ALU.add)
                    if j:
                        step(ins)
                ins.then_inc(conv_done, 1)
            for n in range(MW // P):
                dve.wait_ge(z_ready, n + 1)
                nc.vector.scalar_tensor_tensor(out=y[:, n, :], in0=y[:, n, :], scalar=1.0, in1=zs[:, n % 2, :],
                                               op0=ALU.add, op1=ALU.mult).then_inc(z_used, 1)


def mlstm_stage(m, qk, v, gates, ht, y, at):
    nc, ps = m.nc, m.ps
    units = [(h, t) for h in range(MH) for t in range(4)]
    b = m.area("xl_b", [P, 4, SEQ], at)
    e = m.area("xl_e", [P, 2, SEQ], at + 8192)
    p = m.area("xl_p", [P, 2, SEQ], at + 12288)
    pt = m.area("xl_pt", [P, 2, SEQ], at + 16384)
    at += 20480
    lf = m.area("xl_lf", [P, 4, MH], at)
    ig = m.area("xl_ig", [P, 4, MH], at + 64)
    tmp = m.area("xl_tmp", [P, 2, 4 * MH], at + 128)
    nb = m.area("xl_nb", [P, 4, MH], at + 256)
    st = m.area("xl_st", [P, 3, 8], at + 320)
    ss = m.area("xl_ss", [P, 3, 4 * MH], at + 416)
    junk = m.area("xl_junk", [P, MDH], at + 608)
    abs_ready = m.sem("xl_abs")
    exp_ready = m.sem("xl_exp")
    one_ready = m.sem("xl_one")
    ln_ready = m.sem("xl_ln")
    lf_ready = m.sem("xl_lf")
    total_ready = m.sem("xl_totals")
    b_ready = m.sem("xl_b_ready")
    decayed = m.sem("xl_decays")
    scored = m.sem("xl_scored")
    maxed = m.sem("xl_maxed")
    exped = m.sem("xl_exped")
    p_ready = m.sem("xl_p_ready")
    den_ready = m.sem("xl_den_ready")
    turned = m.sem("xl_turned")
    pt_ready = m.sem("xl_pt_ready")
    summed = m.sem("xl_summed")
    h_ready = m.sem("xl_h_ready")
    squared = m.sem("xl_squared")
    root = m.sem("xl_root")
    scaled = m.sem("xl_scaled")
    h_turned = m.sem("xl_h_turned")
    y_taken = m.sem("xl_y_taken")
    nu = len(units)
    QS = MDH ** -0.5

    with nc.Block() as block:
        @block.tensor
        def _(pe):
            pe.wait_ge(lf_ready, 1)
            for t in range(4):
                for u in range(t + 1):
                    ins = pe.matmul(ps[:, 6, t * MH:(t + 1) * MH], m.upto if u == t else m.ones, lf[:, u, :],
                                    start=(u == 0), stop=(u == t))
            ins.then_inc(total_ready, 1)

            def scores(u):
                h, t = units[u]
                w = (t + 1) * P
                if u >= 2:
                    pe.wait_ge(p_ready, u - 1)
                pe.wait_ge(b_ready, h + 1)
                for i in range(t, -1, -1):
                    ins = pe.matmul(ps[:, u % 2, 0:(i + 1) * P], m.upto if i == t else m.ones,
                                    b[:, i, 0:(i + 1) * P], start=(i == t), stop=(i == 0))
                ins.then_inc(decayed, 1)
                for k in range(2):
                    ins = pe.matmul(ps[:, 2 + u % 2, 0:w], qk[:, 2 * h + k, t * P:(t + 1) * P],
                                    qk[:, 8 + 2 * h + k, 0:w], start=(k == 0), stop=(k == 1))
                ins.then_inc(scored, 1)

            def turn(u):
                t = units[u][1]
                pe.wait_ge(p_ready, u + 1)
                if u >= 1:
                    pe.wait_ge(pt_ready, u)
                for s in range(t + 1):
                    ins = pe.transpose(ps[:, 4, s * P:(s + 1) * P], p[:, u % 2, s * P:(s + 1) * P], m.ident)
                ins.then_inc(turned, 1)

            def values(u):
                h, t = units[u]
                pe.wait_ge(pt_ready, u + 1)
                if u == 0:
                    pe.wait_ge(b_ready, 1)
                if u >= 2:
                    pe.wait_ge(h_ready, u - 1)
                for s in range(t + 1):
                    ins = pe.matmul(ps[:, 6 + u % 2, 0:MDH], pt[:, u % 2, s * P:(s + 1) * P],
                                    v[:, s, h * MDH:(h + 1) * MDH], start=(s == 0), stop=(s == t))
                ins.then_inc(summed, 1)

            for u in range(nu):
                scores(u)
                if u >= 1:
                    turn(u - 1)
                    values(u - 1)
            turn(nu - 1)
            values(nu - 1)
            pe.wait_ge(scaled, 4)
            for f in range(MW // P):
                if f >= 4:
                    pe.wait_ge(y_taken, f - 3)
                for t in range(4):
                    ins = pe.transpose(ps[:, f % 4, t * P:(t + 1) * P], ht[:, t, f * P:(f + 1) * P], m.ident)
                ins.then_inc(h_turned, 1)

        @block.vector
        def _(dve):
            step = m.dve_steps.on(dve)
            gb = lambda k: m.gate_bias[:, MH * k:MH * (k + 1)].unsqueeze(1).to_broadcast([P, 4, MH])
            flat = lambda x: x.rearrange("p a b -> p (a b)")
            step(nc.vector.tensor_tensor(ig[:], gates[:, :, 0:MH], gb(0), ALU.add))
            step(nc.vector.tensor_tensor(lf[:], gates[:, :, MH:2 * MH], gb(1), ALU.add))
            step(nc.vector.tensor_scalar(tmp[:, 0, :], flat(lf[:]), -1.0, None, ALU.mult))
            nc.vector.tensor_tensor(tmp[:, 0, :], tmp[:, 0, :], flat(lf[:]), ALU.max).then_inc(abs_ready, 1)
            dve.wait_ge(exp_ready, 1)
            nc.vector.tensor_scalar(tmp[:, 1, :], tmp[:, 1, :], 1.0, None, ALU.add).then_inc(one_ready, 1)
            dve.wait_ge(ln_ready, 1)
            nc.vector.scalar_tensor_tensor(out=flat(lf[:]), in0=flat(lf[:]), scalar=0.0, in1=tmp[:, 0, :],
                                           op0=ALU.min, op1=ALU.subtract).then_inc(lf_ready, 1)
            dve.wait_ge(lf_ready, 1)
            dve.wait_ge(total_ready, 1)
            step(nc.vector.tensor_scalar(flat(nb[:]), ps[:, 6, 0:4 * MH], -1.0, None, ALU.mult))
            step(nc.vector.tensor_scalar(m.colrange("a_h_norm", 8), m.colrange("a_h_norm", 8), 0.5, None,
                                         ALU.mult))

            def build(h):
                if h:
                    dve.wait_ge(decayed, 4 * h)
                for u in range(4):
                    c = slice(u * P, (u + 1) * P)
                    if u:
                        nc.vector.tensor_scalar(b[:, u, 0:u * P], m.masks[:, 0:u * P], 0.0,
                                                lf[:, u, h:h + 1], ALU.mult, ALU.add)
                    step(nc.vector.tensor_scalar(b[:, u, c], m.after, lf[:, u, h:h + 1], None, ALU.mult))
                    ins = nc.vector.scalar_tensor_tensor(out=b[:, u, c], in0=m.ident, scalar=ig[:, u, h:h + 1],
                                                         in1=b[:, u, c], op0=ALU.mult, op1=ALU.add)
                ins.then_inc(b_ready, 1)

            def head(u):
                h, t = units[u]
                w = (t + 1) * P
                x = ps[:, u % 2, 0:w]
                dve.wait_ge(decayed, u + 1)
                step(nc.vector.tensor_tensor(x[:, t * P:w], x[:, t * P:w], m.causal, ALU.add))
                step(nc.vector.tensor_reduce(st[:, u % 3, 0:1], x, AX.X, ALU.max, negate=True))
                nc.vector.tensor_tensor(st[:, u % 3, 1:2], st[:, u % 3, 0:1], nb[:, t, h:h + 1],
                                        ALU.min).then_inc(maxed, 1)

            def weigh(u):
                h, t = units[u]
                w = (t + 1) * P
                s = st[:, u % 3, :]
                dve.wait_ge(exped, u + 1)
                dve.wait_ge(scored, u + 1)
                if u >= 2:
                    dve.wait_ge(turned, u - 1)
                nc.vector.scalar_tensor_tensor(out=p[:, u % 2, 0:w], in0=ps[:, 2 + u % 2, 0:w], scalar=QS,
                                               in1=e[:, u % 2, 0:w], op0=ALU.mult, op1=ALU.mult,
                                               accum_out=s[:, 3:4]).then_inc(p_ready, 1)
                dve.wait_ge(p_ready, u + 1)
                step(nc.vector.tensor_scalar(s[:, 4:5], s[:, 3:4], -1.0, None, ALU.mult))
                step(nc.vector.tensor_tensor(s[:, 4:5], s[:, 4:5], s[:, 3:4], ALU.max))
                step(nc.vector.tensor_tensor(s[:, 4:5], s[:, 4:5], s[:, 2:3], ALU.max))
                nc.vector.reciprocal(s[:, 5:6], s[:, 4:5]).then_inc(den_ready, 1)

            def squares(u):
                h, t = units[u]
                dve.wait_ge(h_ready, u + 1)
                x = ht[:, t, h * MDH:(h + 1) * MDH]
                nc.vector.tensor_tensor_reduce(
                    out=junk[:], in0=x, in1=x, scale=1.0 / MDH, scalar=0.0, op0=ALU.mult, op1=ALU.add,
                    accum_out=ss[:, 0, t * MH + h:t * MH + h + 1]).then_inc(squared, 1)
                dve.wait_ge(squared, u + 1)

            build(0)
            for u in range(nu):
                head(u)
                if u % 4 == 3 and u + 1 < nu:
                    build((u + 1) // 4)
                weigh(u)
                if u >= 2:
                    squares(u - 2)
            squares(nu - 2)
            squares(nu - 1)
            dve.wait_ge(root, 1)
            step(nc.vector.reciprocal(ss[:, 2, :], ss[:, 1, :]))
            for t in range(4):
                x = ht[:, t, :].rearrange("p (h w) -> p h w", h=MH)
                nc.vector.tensor_tensor(x, x, spread(ss[:, 2, t * MH:(t + 1) * MH], MDH),
                                        ALU.mult).then_inc(scaled, 1)
            for f in range(MW // P):
                dve.wait_ge(h_turned, f + 1)
                nc.vector.scalar_tensor_tensor(out=y[:, f, :], in0=ps[:, f % 4, :], scalar=m.col("a_h_norm", f),
                                               in1=y[:, f, :], op0=ALU.mult, op1=ALU.mult).then_inc(y_taken, 1)

        @block.scalar
        def _(act):
            act.wait_ge(abs_ready, 1)
            nc.scalar.activation(tmp[:, 1, :], tmp[:, 0, :], ACT.Exp, scale=-1.0).then_inc(exp_ready, 1)
            act.wait_ge(one_ready, 1)
            nc.scalar.activation(tmp[:, 0, :], tmp[:, 1, :], ACT.Ln).then_inc(ln_ready, 1)

            def exps(u):
                h, t = units[u]
                w = (t + 1) * P
                act.wait_ge(maxed, u + 1)
                if u >= 2:
                    act.wait_ge(p_ready, u - 1)
                if u >= 3:
                    act.wait_ge(den_ready, u - 2)
                nc.scalar.activation(st[:, u % 3, 2:3], st[:, u % 3, 1:2], ACT.Exp)
                nc.scalar.activation(e[:, u % 2, 0:w], ps[:, u % 2, 0:w], ACT.Exp,
                                     bias=st[:, u % 3, 1:2]).then_inc(exped, 1)

            def takes(u):
                h, t = units[u]
                w = (t + 1) * P
                act.wait_ge(turned, u + 1)
                nc.scalar.activation(pt[:, u % 2, 0:w], ps[:, 4, 0:w], ACT.Copy).then_inc(pt_ready, 1)
                act.wait_ge(summed, u + 1)
                act.wait_ge(den_ready, u + 1)
                nc.scalar.activation(ht[:, t, h * MDH:(h + 1) * MDH], ps[:, 6 + u % 2, 0:MDH], ACT.Copy,
                                     scale=st[:, u % 3, 5:6]).then_inc(h_ready, 1)

            for u in range(nu):
                exps(u)
                if u >= 1:
                    takes(u - 1)
            takes(nu - 1)
            act.wait_ge(squared, nu)
            nc.scalar.activation(ss[:, 1, :], ss[:, 0, :], ACT.Sqrt, bias=m.eps[:, 0:1]).then_inc(root, 1)


def copy_stage(m, name, jobs, tail=None):
    g = Gemm(m, name, jobs)
    with m.nc.Block() as block:
        @block.sync
        def _(sp):
            g.send(sp)

        @block.tensor
        def _(pe):
            g.products(pe)

        @block.scalar
        def _(act):
            g.take("act", act, None)


def rotary_stage(m, turn, at):
    nc = m.nc
    pos = m.area("ro_pos", [P, 4], at, mybir.dt.int32)
    posf = m.area("ro_posf", [P, 4], at + 32)
    ang = m.area("ro_ang", [P, 4, 32], at + 64)
    k = m.area("ro_k", [P, 4, 32], at + 64 + 512)
    loaded = m.sem("ro_loaded")
    reduced = m.sem("ro_reduced")
    sines = m.sem("ro_sines")
    with nc.Block() as block:
        @block.sync
        def _(sp):
            for t in range(4):
                sp.dma_start(pos[:, t:t + 1], m.dram["positions_2"][0, t * P:(t + 1) * P].unsqueeze(1)).then_inc(
                    loaded, 16)

        @block.vector
        def _(dve):
            step = m.dve_steps.on(dve)
            dve.wait_ge(loaded, 64)
            step(nc.vector.tensor_copy(posf[:], pos[:]))
            step(nc.vector.tensor_tensor(ang[:], spread(posf[:], 32),
                                         m.freqs.unsqueeze(1).to_broadcast([P, 4, 32]), ALU.mult))
            step(nc.vector.tensor_scalar(k[:], ang[:], 1.0 / TWO_PI, None, ALU.mult))
            step(nc.vector.tensor_scalar(k[:], k[:], ROUND, None, ALU.add))
            step(nc.vector.tensor_scalar(k[:], k[:], -ROUND, None, ALU.add))
            for part in (PI_A, PI_B, PI_C):
                step(nc.vector.scalar_tensor_tensor(out=ang[:], in0=k[:], scalar=-part, in1=ang[:],
                                                    op0=ALU.mult, op1=ALU.add))
            nc.vector.tensor_scalar(ang[:], ang[:], 3.1415925, -3.1415925, ALU.min, ALU.max).then_inc(reduced, 1)
            dve.wait_ge(sines, 1)
            step(nc.vector.tensor_tensor(turn[:, 0], turn[:, 0], turn[:, 0], ALU.mult))
            step(nc.vector.tensor_scalar(turn[:, 0], turn[:, 0], -2.0, 1.0, ALU.mult, ALU.add))

        @block.scalar
        def _(act):
            act.wait_ge(reduced, 1)
            nc.scalar.activation(turn[:, 0], ang[:], ACT.Sin, scale=0.5)
            nc.scalar.activation(turn[:, 1], ang[:], ACT.Sin).then_inc(sines, 1)


def finish_stage(m, name, nope, pe_part, gpe, gain, factor, turn, nope_t, pe_t, at, x_at, padded=False):
    nc, ps = m.nc, m.ps
    junk = m.area(f"{name}_junk", [P, BH, NOPE], at)
    x = m.at(f"{name}_pe", [P, 2, BH, ROPE], x_at)
    w = m.area(f"{name}_work", [P, BH, ROPE], at + 4096)
    ss = m.area(f"{name}_ss", [P, 4, 4, BH], at + 6144)
    cleared = m.sem(f"{name}_cleared")
    squared = m.sem(f"{name}_squared")
    root = m.sem(f"{name}_root")
    ready = m.sem(f"{name}_ready")
    turned = m.sem(f"{name}_turned")
    taken = m.sem(f"{name}_taken")

    with nc.Block() as block:
        @block.vector
        def _(dve):
            step = m.dve_steps.on(dve)
            tt, ts = nc.vector.tensor_tensor, nc.vector.tensor_scalar
            if padded:
                nc.vector.memset(pe_t[:], 0.0).then_inc(cleared, 1)
            for t in range(4):
                step(tt(junk[:], nope(t), nope(t), ALU.mult))
                step(nc.vector.tensor_reduce(ss[:, 0, t, :], junk[:], AX.X, ALU.add))
                step(tt(w[:], pe_part(t), pe_part(t), ALU.mult))
                step(nc.vector.tensor_reduce(ss[:, 3, t, :], w[:], AX.X, ALU.add))
            step(tt(ss[:, 0], ss[:, 0], ss[:, 3], ALU.add))
            ts(ss[:, 0], ss[:, 0], 1.0 / QKH, None, ALU.mult).then_inc(squared, 1)
            dve.wait_ge(root, 1)
            step(nc.vector.reciprocal(ss[:, 2], ss[:, 1]))
            step(ts(ss[:, 2], ss[:, 2], factor, None, ALU.mult))
            for t in range(4):
                r = ss[:, 2, t, :]
                if t >= 2:
                    dve.wait_ge(turned, t - 1)
                step(tt(nope(t), nope(t), spread(r, NOPE), ALU.mult))
                g = gpe.unsqueeze(1).to_broadcast([P, BH, ROPE])
                c = turn[:, 0, t, :].unsqueeze(1).to_broadcast([P, BH, 32])
                s = turn[:, 1, t, :].unsqueeze(1).to_broadcast([P, BH, 32])
                o = x[:, t % 2]
                step(tt(w[:], pe_part(t), g, ALU.mult))
                step(tt(w[:], w[:], spread(r, ROPE), ALU.mult))
                j = junk[:, :, 0:32]
                step(tt(j, w[:, :, 32:64], s, ALU.mult))
                step(tt(o[:, :, 0:32], w[:, :, 0:32], c, ALU.mult))
                step(tt(o[:, :, 0:32], o[:, :, 0:32], j, ALU.subtract))
                step(tt(j, w[:, :, 0:32], s, ALU.mult))
                step(tt(o[:, :, 32:64], w[:, :, 32:64], c, ALU.mult))
                tt(o[:, :, 32:64], o[:, :, 32:64], j, ALU.add).then_inc(ready, 1)
                dve.wait_ge(ready, t + 1)

        @block.scalar
        def _(act):
            act.wait_ge(squared, 1)
            nc.scalar.activation(ss[:, 1], ss[:, 0], ACT.Sqrt, bias=m.eps[:, 0:1]).then_inc(root, 1)
            for t in range(4):
                c = slice(t * P, (t + 1) * P)
                b = 4 * (t % 2)
                act.wait_ge(turned, t + 1)
                for half in range(2):
                    nc.scalar.activation(nope_t[:, 4 * half:4 * half + 4, c],
                                         ps[:, b + half, :].rearrange("p (k c) -> p k c", k=4), ACT.Copy,
                                         scale=m.col(gain))
                stacked = ps[:, b + 2, :].rearrange("p (k c) -> p k c", k=4)
                if padded:
                    if t == 0:
                        act.wait_ge(cleared, 1)
                    for i in range(2):
                        r = slice(64 * i, 64 * i + 64)
                        ins = nc.scalar.activation(pe_t[r, i:BH:2, c], stacked[r], ACT.Copy)
                else:
                    ins = nc.scalar.activation(pe_t[:, :, c], stacked, ACT.Copy)
                ins.then_inc(taken, 1)

        @block.tensor
        def _(pe):
            for t in range(4):
                b = 4 * (t % 2)
                pe.wait_ge(ready, t + 1)
                if t >= 2:
                    pe.wait_ge(taken, t - 1)
                for h in range(BH):
                    pe.transpose(ps[:, b + h // 4, (h % 4) * P:(h % 4 + 1) * P], nope(t)[:, h, :], m.ident)
                for h in range(BH // 2):
                    ins = pe.transpose(ps[:, b + 2, h * P:(h + 1) * P],
                                       x[:, t % 2, 2 * h:2 * h + 2, :].rearrange("p a b -> p (a b)"), m.ident)
                ins.then_inc(turned, 1)


def two_blocks(nc, dram):
    with ExitStack() as ctx:
        ctx.enter_context(nc.allow_non_contiguous_dma("short rows of gains and gate weights"))
        m = Machine(nc, ctx, dram)
        m.gates = m.keep("gates", [CAP, NE])
        m.rows = m.keep("rows", [CAP, NE], U32)
        m.arena = m.keep_end
        m.xhat = nc.dram_tensor("xhat_scratch", [L1, D], F32, kind="Internal").ap()
        m.resid = nc.dram_tensor("resid_scratch", [L1, D], F32, kind="Internal").ap()

        def columns(w, widths, start=0):
            k = w.shape[0] // P
            for c in widths:
                m.blocks.append((w[:, start:start + c], k, c))
                start += c

        columns(dram["w_in"][0], [512] * 6)
        columns(dram["w_out"][0], [512] * 2)
        for l in range(2):
            columns(dram["mem_w_kv_2"][l], [512] * 2)
        columns(dram["a_w_in_2"][0], [512] * 10 + [8, 512, 512])
        columns(dram["a_w_out_2"][0], [512] * 2)
        columns(dram["w_kv_a_2"], [KVL + ROPE])
        columns(dram["w_kv_b_2"], [512] * 4)
        columns(dram["b_w_in_2"][0], [QL] + [512] * 4)
        columns(dram["b_w_q_up_2"][0], [512] * 3)
        columns(dram["b_w_out_2"][0], [512] * 2)

        def rows(name, n, flat=None):
            a = dram[name] if flat is None else flat
            return a.rearrange("(k p) -> k p", p=P)

        names = [
            ("mix_g", rows(None, 8, dram["mix_norm_g"][0])),
            ("conv_w", dram["conv_w"][0].rearrange("j (k p) -> (j k) p", p=P)),
            ("subln", rows(None, 1, dram["attn_subln_g"][0])),
            ("ffn_g", rows(None, 8, dram["ffn_norm_g"][0])),
            ("a_norm", rows(None, 8, dram["a_norm_2"][0])),
            ("a_conv_b", rows(None, 16, dram["a_conv_b_2"][0])),
            ("a_h_norm", rows(None, 8, dram["a_h_norm_2"][0])),
            ("b_norm", rows(None, 8, dram["b_norm_2"][0])),
            ("q_lat", rows(None, 3, dram["b_q_lat_norm_2"][0])),
            ("kv_norm", rows(None, 8, dram["kv_norm_2"])),
            ("kv_lat", rows(None, 2, dram["kv_lat_norm_2"])),
            ("q_nope", rows(None, 1, dram["b_q_gain_2"][0, 0:NOPE])),
            ("k_nope", rows(None, 1, dram["k_gain_2"][0:NOPE])),
            ("mem_norm", rows(None, 8, dram["mem_norm_2"])),
            ("mem_q", dram["mem_q_gain_2"]),
            ("mem_k", dram["mem_k_gain_2"]),
            ("a_conv_w", dram["a_conv_w_2"][0].rearrange("j (k p) -> (j k) p", p=P)),
        ]

        feat = 4 * KD * L1
        h = m.area("h", [P, len(TILES1), D], 0)
        hn = m.area("hn1", [P, KD, L1], 20480)
        qk = m.area("qk1", [P, KD, L1], 20480 + feat)
        v = m.area("v1", [P, len(TILES1), AH * AV], 20480 + 2 * feat)
        at = 20480 + 2 * feat + 10240
        raw = m.area("raw1", [P, 12, L1], at)
        turns = m.area("turns1", [P, 2, L1], at + 48 * L1)
        work = at + 56 * L1
        setup_stage(m, h, turns, work, names)
        m.close()
        norm_stage(m, "n1", h, TILES1, [(hn, "mix_g")], m.arena + work)
        m.close()
        rot_work = m.area("rot_work", [P, 2, L1], work)
        projection_stage(m, hn, qk, v, raw, turns, rot_work)
        m.close()
        diff_attention_stage(m, qk, v, raw, hn, at + 48 * L1)
        m.close()
        out_stage(m, "out1", hn, h, TILES1, ahead=0)
        m.close()

        def store_tokens(sp, normed, ready, stored):
            for t, (t0, n) in enumerate(TILES1):
                sp.dma_start(m.resid[t0:t0 + n, :], h[0:n, t, :]).then_inc(m.resid_stored, 16)
            for t, (t0, n) in enumerate(TILES1):
                sp.wait_ge(ready, t + 1)
                sp.dma_start(m.xhat[t0:t0 + n, :], normed[0:n, t % 2, :]).then_inc(stored[t % 2], 16)
            sp.wait_ge(m.resid_stored, 16 * len(TILES1))
            for i in range(2):
                sp.wait_ge(stored[i], 16 * len(range(i, len(TILES1), 2)))

        m.resid_stored = m.sem("resid_stored")
        norm_stage(m, "n2", h, TILES1, [(hn, "ffn_g")], m.arena + work, tail=store_tokens)
        m.close()
        router_stage(m, hn, work)
        m.close()
        experts_stage(m, 0)
        m.close()

        x = m.area("x", [P, 4, D], 0)
        mk = [m.area(f"mk{l}", [P, MEMH, MEM], 16384 + 8192 * l) for l in range(2)]
        mv = [m.area(f"mv{l}", [P, 2, 512], 16384 + 8192 * l + 4096) for l in range(2)]
        final_norm_stage(m, x, 32768)
        m.close()
        mem_x = m.area("mem_x", [P, 2, D], 32768)
        mem_t = m.area("mem_t", [P, KD, MEM], 40960)
        mk_tok = [m.area(f"mk_tok{l}", [P, 2, 512], 49152 + 4096 * l) for l in range(2)]
        mem_load_stage(m, mem_x)
        m.close()
        norm_stage(m, "nm", mem_x, TILES2[:2], [(mem_t, "mem_norm")], m.arena + 57344)
        m.close()
        memory_stage(m, mem_t, mk_tok, mv)
        m.close()

        hn = m.low("hn2", [P, KD, SEQ], 0)
        qk = m.low("qk2", [P, 16, SEQ], 16384)
        v = m.area("v2", [P, 4, MW], 32768)
        y = m.area("y2", [P, 12, SEQ], 49152)
        mq = m.area("mq2", [P, 4, MEMH * MEMD], 73728)
        work = 81920
        gates = m.area("ml_gates", [P, 4, 2 * MH], 106496)
        mqt = m.low("mqt2", [P, MEMH, SEQ], 16384)
        by_head = lambda t: t.rearrange("p t (g w) -> p t g w", g=MEMH)
        group_norm_stage(m, "gm", [dict(src=by_head(mk_tok[l][:]), dst=mk[l], gain=("mem_k", l), factor=1.0)
                                   for l in range(2)], work)
        m.close()
        norm_stage(m, "n3", x, TILES2, [(hn, "a_norm")], m.arena + work)
        m.close()
        mlstm_in_stage(m, hn, qk, v, y, mq, gates, work)
        m.close()
        ht = m.low("ht", [P, 4, MW], 0)
        mlstm_stage(m, qk, v, gates, ht, y, work)
        m.close()
        group_norm_stage(m, "gq1", [dict(src=by_head(mq[:]), dst=mqt, gain=("mem_q", 0),
                                         factor=MEMD ** -0.5)], work)
        m.close()
        attention_stage(m, "ma1", memory_units(mqt, mk[0], mv[0], y), work)
        m.close()
        out_stage(m, "out2", y, x, TILES2)
        m.close()

        hb = m.low("hb", [P, KD, SEQ], 0)
        hkv = m.low("hkv", [P, KD, SEQ], 16384)
        qt = m.low("qt3", [P, BH, SEQ], 16384)
        kt = m.low("kt3", [P, BH, SEQ], 32768)
        v = m.area("v3", [P, 4, BH, NOPE], 32768)
        y = m.area("y3", [P, 12, SEQ], 49152)
        kn = m.area("kn", [P, 4, BH, NOPE], 49152)
        lat = m.area("lat", [P, 4, KVL + ROPE], 65536)
        kpt = m.area("kpt", [P, BH // 2, SEQ], 73728)
        qpt = m.area("qpt", [P, BH, SEQ], 81920)
        mq = m.area("mq3", [P, 4, MEMH * MEMD], 90112)
        latt = m.area("latt", [P, KVL // P, SEQ], 81920)
        turn = m.area("turn3", [P, 2, 4, 32], 106496)
        norm_stage(m, "n4", x, TILES2, [(hb, "b_norm"), (hkv, "kv_norm")], m.arena + 49152)
        m.close()

        def copies(*dsts):
            act = m.nc.scalar
            return [lambda step, u, psum, f=f: f(act, u, psum) for f in dsts]

        def job(kind, src, take):
            return dict(kind=kind, act=src, tiles=TILES2, engine="act", take=take)

        take_lat, = copies(lambda act, u, ps: act.activation(lat[:, u, :], ps, ACT.Copy))
        copy_stage(m, "kva", [job("tokens", hkv, take_lat)])
        m.close()
        one_group = lambda t: t.unsqueeze(2)
        group_norm_stage(m, "gkv", [dict(src=one_group(lat[:, :, 0:KVL]), dst=latt, gain=("kv_lat", 0),
                                         factor=1.0)], 90112)
        m.close()
        rotary_stage(m, turn, 90112)
        m.close()

        def take_kv(c):
            def f(step, u, psum):
                act = m.nc.scalar
                pair = psum.rearrange("p (h w) -> p h w", h=2)
                act.activation(kn[:, u, 2 * c:2 * c + 2, :], pair[:, :, 0:NOPE], ACT.Copy)
                return act.activation(v[:, u, 2 * c:2 * c + 2, :], pair[:, :, NOPE:], ACT.Copy)
            return f

        copy_stage(m, "kvb", [job("tokens", latt, take_kv(c)) for c in range(4)])
        m.close()
        finish_stage(m, "fk", lambda t: kn[:, t],
                     lambda t: lat[:, t, KVL:].unsqueeze(1).to_broadcast([P, BH, ROPE]), m.gpe[:, 1, :],
                     "k_nope", 1.0, turn, kt, kpt, 90112, m.arena + 98304)
        m.close()

        qlat = m.area("qlat", [P, 4, QL], 81920)
        take_ql, take_mq = copies(lambda act, u, ps: act.activation(qlat[:, u, :], ps, ACT.Copy),
                                  lambda act, u, ps: act.activation(mq[:, u, :], ps, ACT.Copy))
        take_z = copies(*[lambda act, u, ps, c=c: act.activation(y[:, c + u, :], ps, ACT.Silu)
                          for c in (0, 4, 8)])
        copy_stage(m, "in3", [job("tokens", hb, take_ql), job("features", hb, take_z[0]),
                              job("features", hb, take_z[1]), job("tokens", hb, take_mq),
                              job("features", hb, take_z[2])])
        m.close()
        qlt = m.low("qlt", [P, QL // P, SEQ], 16384)
        mqt = m.low("mqt3", [P, MEMH, SEQ], 16384 + 6144)
        group_norm_stage(m, "gq2", [dict(src=one_group(qlat[:]), dst=qlt, gain=("q_lat", 0), factor=1.0),
                                    dict(src=by_head(mq[:]), dst=mqt, gain=("mem_q", 1),
                                         factor=MEMD ** -0.5)], 98304)
        m.close()
        attention_stage(m, "ma2", memory_units(mqt, mk[1], mv[1], y), 90112)
        m.close()
        q_low = m.area("q_low", [P, 2, BH, QKH], 16384)
        q_high = m.low("q_high", [P, 2, BH, QKH], 0)
        q_of = lambda t: (q_low if t < 2 else q_high)[:, t % 2]

        def take_q(c):
            def f(step, u, psum):
                flat = q_of(u).rearrange("p h w -> p (h w)")
                return m.nc.scalar.activation(flat[:, 512 * c:512 * (c + 1)], psum, ACT.Copy)
            return f

        copy_stage(m, "qup", [job("tokens", qlt, take_q(c)) for c in range(3)])
        m.close()
        finish_stage(m, "fq", lambda t: q_of(t)[:, :, 0:NOPE], lambda t: q_of(t)[:, :, NOPE:], m.gpe[:, 0, :],
                     "q_nope", QKH ** -0.5, turn, qt, qpt, 98304, m.low_ring + 12288, padded=True)
        m.close()
        units = []
        for hd in range(BH):
            for t in range(4):
                c, w = slice(t * P, (t + 1) * P), (t + 1) * P
                units.append(dict(scores=[(qt[:, hd, c], kt[:, hd, 0:w]), (qpt[:, hd, c], kpt[:, hd // 2, 0:w])],
                                  width=w, mask=m.chunk, values=[v[:, s, hd, :] for s in range(t + 1)],
                                  y=y[:, hd, c]))
        attention_stage(m, "ba", units, 98304)
        m.close()
        out_stage(m, "out3", y, x, TILES2)
        m.close()
        result_stage(m, x)
        m.close()


def mem_load_stage(m, mem_x):
    loaded = m.sem("mem_loaded")
    with m.nc.Block() as block:
        @block.sync
        def _(sp):
            sp.dma_start(mem_x[:], m.dram["mem_2"][0].rearrange("(t p) d -> p t d", p=P)).then_inc(loaded, 16)
            sp.wait_ge(loaded, 16)


def result_stage(m, x):
    stored = m.sem("result_stored")
    with m.nc.Block() as block:
        @block.sync
        def _(sp):
            sp.dma_start(m.dram["out"][0].rearrange("(t p) d -> p t d", p=P), x[:]).then_inc(stored, 16)
            sp.wait_ge(stored, 16)


INPUTS = ["x", "meta_tokens", "mix_norm_g", "w_in", "conv_w", "lambda_q1", "lambda_k1", "lambda_q2", "lambda_k2",
          "attn_subln_g", "w_out", "ffn_norm_g", "w_router", "w_gate", "w_up", "w_down", "final_norm_g", "mem_2",
          "positions_2", "a_norm_2", "a_w_in_2", "a_conv_w_2", "a_conv_b_2", "a_ig_bias_2", "a_fg_bias_2",
          "a_h_norm_2", "a_w_out_2", "b_norm_2", "b_w_in_2", "b_q_lat_norm_2", "b_w_q_up_2", "b_q_gain_2",
          "b_w_out_2", "kv_norm_2", "w_kv_a_2", "kv_lat_norm_2", "w_kv_b_2", "k_gain_2", "mem_norm_2",
          "mem_w_kv_2", "mem_q_gain_2", "mem_k_gain_2"]


def kernel(**inputs):
    import numpy as _np
    import concourse.bacc as _bacc
    from concourse import mybir as _mybir
    from concourse.bass_utils import run_bass_kernel_spmd as _run

    nc = _bacc.Bacc("TRN2", target_bir_lowering=False, num_devices=1)
    arrays, dram = {}, {}
    masks, turns = fixed_tables()
    given = {name: _np.ascontiguousarray(inputs[name]) for name in INPUTS}
    given["masks"], given["turns"] = masks, turns
    for name, a in given.items():
        arrays[f"in_{name}"] = a
        dram[name] = nc.dram_tensor(f"in_{name}", a.shape, _mybir.dt.from_np(a.dtype), kind="ExternalInput").ap()
    dram["out"] = nc.dram_tensor("out_0", (1, SEQ, D), _mybir.dt.float32, kind="ExternalOutput").ap()
    two_blocks(nc, dram)
    r = _run(nc, [arrays], core_ids=[0])
    return r.results[0]["out_0"]
```

```python
from contextlib import ExitStack

import numpy as np
import concourse.bass as bass
from concourse import mybir

F32 = mybir.dt.float32
F32R = mybir.dt.float32r
U32 = mybir.dt.uint32
ALU = mybir.AluOpType
ACT = mybir.ActivationFunctionType
AX = mybir.AxisListType

P = 128
D = 1024
KD = D // P
META = 16
SEQ = 512
L1 = META + SEQ
TILES1 = [(i * P, min(P, L1 - i * P)) for i in range(-(-L1 // P))]
TILES2 = [(i * P, P) for i in range(SEQ // P)]
HALF1 = L1 // 2
EPS = 1e-6
LAM_INIT = 0.2
AH, AV = 4, 128
NE = 16
CAP = 2 * L1 // NE
FF = 2 * D
FH = FF // 2
ROUNDS = -(-CAP // 8)
MEM = 256
MH, MDH = 4, 256
MW = MH * MDH
MEMH, MEMD = 4, 128
BH = 8
NOPE, ROPE = 128, 64
QKH = NOPE + ROPE
QL, KVL = 384, 256
NEG = -1.0e30
SLOT = 2048
NSLOT = 12
NPIECE, NSPLIT = 6, 3
MLSTM_IN = [("gates", 0, 5120, 8), ("qk", 0, 0, 512), ("v", 0, 2048, 512), ("qk", 1, 512, 512), ("v", 1, 2560, 512),
            ("qk", 2, 1024, 512), ("o", 0, 3072, 512), ("qk", 3, 1536, 512), ("o", 1, 3584, 512),
            ("z", 0, 4096, 512), ("z", 1, 4608, 512), ("mq", 0, 5128, 512),
            ("mz", 0, 5640, 512)]
TWO_PI = 2.0 * np.pi
PI_A = 6.28125
PI_B = float(np.float32(np.round((TWO_PI - PI_A) * 2 ** 19) / 2 ** 19))
PI_C = float(np.float32(TWO_PI - PI_A - PI_B))
ROUND = 12582912.0


def fixed_tables():
    i = np.arange(P)
    ident = np.eye(P)
    rot = np.zeros((P, P))
    for m in range(P):
        if m % 64 < 32:
            rot[m + 32, m] = -1.0
        else:
            rot[m - 32, m] = 1.0
    upto = (i[:, None] <= i[None, :])
    ones = np.ones((P, P))
    after = (i[:, None] > i[None, :])
    causal = np.where(i[None, :] > i[:, None], NEG, 0.0)
    chunk = np.where(i[None, :] // 64 > i[:, None] // 64, NEG, 0.0)
    freq = (np.float32(10000.0) ** (-np.arange(0, 64, 2, dtype=np.float32) / np.float32(64))).astype(np.float32)
    freqs = np.broadcast_to(freq[None, :], (P, 32))
    masks = np.concatenate([ident, rot, upto, after, causal, chunk, ones, freqs], axis=1).astype(np.float32)
    ang = (np.arange(L1, dtype=np.float32)[:, None] * freq[None, :]).astype(np.float32)
    ang = np.concatenate([ang] * 4, axis=1).T
    turns = np.stack([np.cos(ang), np.sin(ang)], axis=1).astype(np.float32)
    return np.ascontiguousarray(masks), np.ascontiguousarray(turns)


class Steps:

    def __init__(self, sem):
        self.sem, self.count = sem, 0

    def on(self, engine):
        def step(ins):
            self.count += 1
            ins.then_inc(self.sem, 1)
            engine.wait_ge(self.sem, self.count)
        return step


class Machine:

    def __init__(self, nc, ctx, dram):
        self.nc, self.ctx, self.dram = nc, ctx, dram
        self.stage, self.stage_sems, self.cooling = 0, [], []
        self.ps = ctx.enter_context(nc.psum_tensor("ps", [P, 8, 512], F32))
        self.ring_at = 16640
        self.keep_at = self.ring_at + NSLOT * SLOT * 4
        self.keep_end = self.keep_at
        self.ring = self.at("ring", [P, NSLOT, SLOT], self.ring_at)
        self.low_ring = self.ring_at + 6 * SLOT * 4
        self.pieces = self.at("pieces", [P, NPIECE, SLOT], self.low_ring)
        self.high = self.at("pieces_high", [P, NSPLIT, SLOT], self.ring_at, F32R)
        self.low_part = self.at("pieces_low", [P, NSPLIT, SLOT], self.ring_at + NSPLIT * SLOT * 4, F32R)
        self.gaps = [self.ring_at + 3 * SLOT * 4 * i + 2 * SLOT * 4 for i in range(2)]
        self.masks = self.keep("masks", [P, 7 * P + 32])
        self.ident = self.masks[:, 0:P]
        self.rot = self.masks[:, P:2 * P]
        self.upto = self.masks[:, 2 * P:3 * P]
        self.after = self.masks[:, 3 * P:4 * P]
        self.causal = self.masks[:, 4 * P:5 * P]
        self.chunk = self.masks[:, 5 * P:6 * P]
        self.ones = self.masks[:, 6 * P:7 * P]
        self.freqs = self.masks[:, 7 * P:7 * P + 32]
        self.cols = self.keep("cols", [P, 2, P])
        self.eps = self.keep("eps", [P, 1])
        self.lam = self.keep("lam", [P, 1])
        self.gpe = self.keep("gpe", [P, 2, ROPE])
        self.gate_bias = self.keep("gate_bias", [P, 2 * MH])
        self.arena = self.keep_end
        self.dve_steps = Steps(self.lasting("dve_step"))
        self.act_steps = Steps(self.lasting("act_step"))
        self.pool_steps = Steps(self.lasting("pool_step"))
        self.block_loaded = [self.lasting("block_loaded0"), self.lasting("block_loaded1")]
        self.block_free = {}
        self.sent = 0
        self.taken = 0
        self.blocks = []
        self.experts_sent = 0
        self.expert_loaded = [self.lasting(f"expert_loaded{i}") for i in range(NPIECE)]

    def lasting(self, name):
        return self.ctx.enter_context(self.nc.semaphore(name))

    def sem(self, name):
        s = self.nc.alloc_semaphore(name)
        self.stage_sems.append(s)
        return s

    def close(self):
        for s in self.cooling:
            self.nc.release_semaphore(s)
        for s in self.stage_sems:
            self.nc.gpsimd.sem_clear(s)
        self.cooling, self.stage_sems = self.stage_sems, []
        self.stage += 1

    def at(self, name, shape, offset, dt=F32):
        return self.nc.alloc_sbuf_tensor_at(name, shape, dt, offset=offset)

    def keep(self, name, shape, dt=F32):
        t = self.at(name, shape, self.keep_end, dt)
        size = 4 * int(np.prod(shape[1:]))
        self.keep_end += -(-size // 32) * 32
        return t

    def area(self, name, shape, offset, dt=F32):
        assert self.arena + offset + 4 * int(np.prod(shape[1:])) <= 229344, name
        return self.at(name, shape, self.arena + offset, dt)

    def low(self, name, shape, offset):
        assert offset + 4 * int(np.prod(shape[1:])) <= 6 * SLOT * 4
        return self.at(name, shape, self.low_ring + offset)

    def col(self, name, k=0):
        n = self.col_of[name] + k
        return self.cols[:, n // P, n % P:n % P + 1]

    def colrange(self, name, k):
        n = self.col_of[name]
        assert n // P == (n + k - 1) // P, name
        return self.cols[:, n // P, n % P:n % P + k]

    def block_view(self, n):
        _, k, cols = self.blocks[n]
        flat = self.ring[:, 3 * (n % 2):3 * (n % 2) + 3, :].rearrange("p a b -> p (a b)")
        return flat[:, 0:k * cols].rearrange("p (k c) -> p k c", k=k)

    def send_blocks(self, sp, upto):
        while self.sent < min(upto, len(self.blocks)):
            n = self.sent
            src, k, cols = self.blocks[n]
            if n >= 2 and self.block_free[n - 2][0] == self.stage:
                sp.wait_ge(*self.block_free[n - 2][1:])
            sp.dma_start(self.block_view(n), src.rearrange("(k p) c -> p k c", p=P)).then_inc(
                self.block_loaded[n % 2], 16)
            self.sent += 1

    def expert_load(self, sp, j, e, slot):
        w_gate, w_up, w_down = self.dram["w_gate"], self.dram["w_up"], self.dram["w_down"]
        if j < 8 or 12 <= j < 20:
            half = 1 if j < 8 else 0
            i = j if j < 8 else j - 12
            w = w_up if i % 2 else w_gate
            src = w[0, e, 2 * P * (i // 2):2 * P * (i // 2 + 1), half * FH:(half + 1) * FH]
        else:
            half = 0 if j < 12 else 1
            i = j - 8 if j < 12 else j - 20
            src = w_down[0, e, half * FH + 2 * P * i:half * FH + 2 * P * (i + 1), :]
        if len(src.shape) == 3:
            src = src.rearrange("o (k p) c -> p (o k) c", p=P)
        else:
            src = src.rearrange("(k p) c -> p k c", p=P)
        sp.dma_start(self.pieces[:, slot, :].rearrange("p (k c) -> p k c", k=2), src).then_inc(
            self.expert_loaded[slot], 16)

    def send_experts(self, sp, upto):
        while self.experts_sent < upto:
            n = self.experts_sent
            self.expert_load(sp, 12 + n if n < 8 else n - 8, 0, n % NPIECE)
            self.experts_sent += 1

    def wait_block(self, pe, n):
        pe.wait_ge(self.block_loaded[n % 2], 16 * (n // 2 + 1))


def wait_counted(engine, sem, value, passed):
    engine.wait_ge(sem, value)
    engine.sem_inc(passed, 1)


def spread(ap, n):
    p, k = ap.shape
    return ap.unsqueeze(2).to_broadcast([p, k, n])


def norm_stage(m, name, x, tiles, outs, temp, tail=None):
    nc, ps = m.nc, m.ps
    nt = len(tiles)
    normed = m.at(f"{name}_normed", [P, 2, D], temp)
    junk = m.at(f"{name}_junk", [P, D], temp + 8 * D)
    ss = m.at(f"{name}_ss", [P, 3, nt], temp + 12 * D)
    squared = m.sem(f"{name}_squared")
    root_ready = m.sem(f"{name}_root")
    inverse_ready = m.sem(f"{name}_inverse")
    normed_ready = m.sem(f"{name}_normed")
    turned = m.sem(f"{name}_turned")
    evicted = m.sem(f"{name}_evicted")
    stored = [m.sem(f"{name}_stored{i}") for i in range(2)] if tail else None

    with nc.Block() as block:
        if tail:
            @block.sync
            def _(sp):
                tail(sp, normed, normed_ready, stored)

        @block.vector
        def _(dve):
            step = m.dve_steps.on(dve)
            step(nc.vector.memset(ss[:], 1.0))
            for t, (_, n) in enumerate(tiles):
                ins = nc.vector.tensor_tensor_reduce(
                    out=junk[0:n, :], in0=x[0:n, t, :], in1=x[0:n, t, :], scale=1.0 / D, scalar=0.0,
                    op0=ALU.mult, op1=ALU.add, accum_out=ss[0:n, 0, t:t + 1])
                ins.then_inc(squared, 1)
                dve.wait_ge(squared, t + 1)
            dve.wait_ge(root_ready, 1)
            nc.vector.reciprocal(ss[:, 2, :], ss[:, 1, :]).then_inc(inverse_ready, 1)
            u = 0
            for t, (t0, n) in enumerate(tiles):
                for half in range(2):
                    dve.wait_ge(turned, u + 1)
                    bank = ps[:, u % 8, :].rearrange("p (k c) -> p k c", k=4)[:, :, 0:n]
                    for out, gain in outs:
                        g = spread(m.colrange(gain, KD)[:, 4 * half:4 * half + 4], n)
                        ins = nc.vector.tensor_tensor(out[:, 4 * half:4 * half + 4, t0:t0 + n], bank, g, ALU.mult)
                    ins.then_inc(evicted, 1)
                    u += 1

        @block.scalar
        def _(act):
            act.wait_ge(squared, nt)
            nc.scalar.activation(ss[:, 1, :], ss[:, 0, :], ACT.Sqrt, bias=m.eps[:, 0:1]).then_inc(root_ready, 1)
            act.wait_ge(inverse_ready, 1)
            for t, (_, n) in enumerate(tiles):
                if t >= 2:
                    act.wait_ge(turned, 2 * (t - 1))
                    if stored is not None:
                        act.wait_ge(stored[t % 2], 16 * (t // 2))
                nc.scalar.activation(normed[0:n, t % 2, :], x[0:n, t, :], ACT.Copy,
                                     scale=ss[0:n, 2, t:t + 1]).then_inc(normed_ready, 1)

        @block.tensor
        def _(pe):
            u = 0
            for t, (_, n) in enumerate(tiles):
                pe.wait_ge(normed_ready, t + 1)
                for half in range(2):
                    if u >= 8:
                        pe.wait_ge(evicted, u - 7)
                    for k in range(4):
                        f = 4 * half + k
                        ins = pe.transpose(ps[:, u % 8, k * P:k * P + n],
                                           normed[0:n, t % 2, f * P:(f + 1) * P], m.ident[0:n, 0:n])
                    ins.then_inc(turned, 1)
                    u += 1


class Gemm:

    def __init__(self, m, name, jobs, pairs=4):
        self.m, self.name, self.jobs, self.pairs = m, name, jobs, pairs
        self.first = m.taken
        self.ready = m.sem(f"{name}_ready")
        self.out = {"act": m.sem(f"{name}_act_took"), "dve": m.sem(f"{name}_dve_took")}
        self.units = []
        count = {"act": 0, "dve": 0}
        for j, job in enumerate(jobs):
            _, k, cols = m.blocks[self.first + j]
            tiles = job["tiles"]
            n_units = cols // P if job["kind"] == "features" else len(tiles)
            for u in range(n_units):
                count[job["engine"]] += 1
                self.units.append((j, u, job["engine"], count[job["engine"]]))
            m.block_free[self.first + j] = (m.stage, self.ready, len(self.units))
        m.taken += len(jobs)

    def psum(self, n):
        j, u, _, _ = self.units[n]
        job = self.jobs[j]
        pair = 2 * (n % self.pairs)
        ps = self.m.ps
        if job["kind"] == "features":
            tokens = job["act"].shape[2]
            if tokens > 512:
                return ps[:, pair:pair + 2, 0:tokens // 2]
            return ps[:, pair, 0:tokens]
        cols = self.m.blocks[self.first + j][2]
        rows = job["tiles"][u][1]
        return ps[0:rows, pair, 0:cols]

    def products(self, pe, after=None):
        m = self.m
        for n, (j, u, _, _) in enumerate(self.units):
            job = self.jobs[j]
            w = m.block_view(self.first + j)
            k_tiles, cols = m.blocks[self.first + j][1:]
            if u == 0:
                m.wait_block(pe, self.first + j)
                if "needs" in job:
                    pe.wait_ge(*job["needs"])
            if n >= self.pairs:
                _, _, engine, count = self.units[n - self.pairs]
                pe.wait_ge(self.out[engine], count)
            act = job["act"]
            out = self.psum(n)
            if job["kind"] == "features":
                tokens = act.shape[2]
                halves = [(0, tokens)] if tokens <= 512 else [(0, tokens // 2), (tokens // 2, tokens)]
                for h, (a, b) in enumerate(halves):
                    to = out if len(halves) == 1 else out[:, h, :]
                    for k in range(k_tiles):
                        ins = pe.matmul(to, w[:, k, u * P:(u + 1) * P], act[:, k, a:b],
                                        start=(k == 0), stop=(k == k_tiles - 1))
            else:
                t0, rows = job["tiles"][u]
                for k in range(k_tiles):
                    ins = pe.matmul(out, act[:, k, t0:t0 + rows], w[:, k, :],
                                    start=(k == 0), stop=(k == k_tiles - 1))
            ins.then_inc(self.ready, 1)
            if after:
                after(pe, n)

    def take(self, which, engine, step):
        for n, (j, u, name, count) in enumerate(self.units):
            if name != which:
                continue
            engine.wait_ge(self.ready, n + 1)
            ins = self.jobs[j]["take"](step, u, self.psum(n))
            if ins is None:
                engine.sem_inc(self.out[which], 1)
            else:
                ins.then_inc(self.out[which], 1)

    def send(self, sp, ahead=2):
        self.m.send_blocks(sp, self.first + len(self.jobs) + ahead)


class SplitGemm:

    def __init__(self, m, name, jobs, slots):
        self.m, self.name, self.jobs = m, name, jobs
        self.first, self.ns = m.taken, len(slots)
        tokens = max(job["act"].shape[2] for job in jobs)
        self.w_split = [m.at(f"{name}_w{i}", [P, 2, 512], at, F32R) for i, at in enumerate(slots)]
        self.a_split = [m.at(f"{name}_a{i}", [P, 2, tokens], at + 4096, F32R) for i, at in enumerate(slots)]
        self.high = m.sem(f"{name}_high")
        self.low = m.sem(f"{name}_low")
        self.used = m.sem(f"{name}_used")
        self.ready = m.sem(f"{name}_ready")
        self.out = {"act": m.sem(f"{name}_act_took"), "dve": m.sem(f"{name}_dve_took")}
        self.steps, self.units, self.first_unit, self.first_step = [], [], [], []
        count, n_ready = {"act": 0, "dve": 0}, 0
        for j, job in enumerate(jobs):
            _, k, cols = m.blocks[self.first + j]
            n_units = cols // P if job["kind"] == "features" else len(job["tiles"])
            self.first_unit.append(len(self.units))
            self.first_step.append(len(self.steps))
            for n in range(len(self.units) - 8 + 1, len(self.units) - 8 + n_units + 1):
                assert n < 1 or self.units[n - 1][5] <= len(self.steps) + self.ns - 1, name
            if not job.get("plain"):
                self.steps += [(j, i) for i in range(k)]
            for u in range(n_units):
                count[job["engine"]] += 1
                if u == n_units - 1 and not job.get("plain"):
                    done = (self.used, len(self.steps))
                else:
                    n_ready += 1
                    done = (self.ready, n_ready)
                place = len(self.steps) + self.ns - 1 + job.get("spread", 0) * u
                if self.units:
                    place = max(place, self.units[-1][5])
                self.units.append((j, u, job["engine"], count[job["engine"]], done, place))
            free = (self.ready, n_ready) if job.get("plain") else (self.low, 2 * len(self.steps) - 1)
            m.block_free[self.first + j] = (m.stage,) + free
        m.taken += len(jobs)

    def psum(self, n):
        j, u = self.units[n][0:2]
        bank = self.m.ps[:, n % 8, :]
        job = self.jobs[j]
        if job["kind"] == "features":
            return bank[:, 0:job["act"].shape[2]]
        return bank[0:job["tiles"][u][1], 0:self.m.blocks[self.first + j][2]]

    def wait_bank(self, pe, n):
        if n >= 8:
            engine, count = self.units[n - 8][2:4]
            pe.wait_ge(self.out[engine], count)

    def plain(self, pe, j):
        m, job = self.m, self.jobs[j]
        w = m.block_view(self.first + j)
        k_tiles = m.blocks[self.first + j][1]
        m.wait_block(pe, self.first + j)
        for u, (t0, rows) in enumerate(job["tiles"]):
            n = self.first_unit[j] + u
            self.wait_bank(pe, n)
            for k in range(k_tiles):
                ins = pe.matmul(self.psum(n), job["act"][:, k, t0:t0 + rows], w[:, k, :],
                                start=(k == 0), stop=(k == k_tiles - 1))
            ins.then_inc(self.ready, 1)

    def products(self, pe):
        m, s = self.m, 0
        for j, job in enumerate(self.jobs):
            if job.get("plain"):
                self.plain(pe, j)
                continue
            k_tiles, cols = m.blocks[self.first + j][1:]
            n_units = cols // P if job["kind"] == "features" else len(job["tiles"])
            tokens = job["act"].shape[2]
            for k in range(k_tiles):
                w, a = self.w_split[s % self.ns], self.a_split[s % self.ns]
                pe.wait_ge(self.low, 2 * s + 2)
                for u in range(n_units):
                    n = self.first_unit[j] + u
                    if k == 0:
                        self.wait_bank(pe, n)
                    for i, (x, y) in enumerate(((0, 0), (0, 1), (1, 0))):
                        if job["kind"] == "features":
                            lhs, rhs = w[:, x, u * P:(u + 1) * P], a[:, y, 0:tokens]
                        else:
                            t0, rows = job["tiles"][u]
                            lhs, rhs = a[:, x, t0:t0 + rows], w[:, y, 0:cols]
                        ins = pe.matmul(self.psum(n), lhs, rhs, start=(k == 0 and i == 0),
                                        stop=(k == k_tiles - 1 and i == 2))
                    if k == k_tiles - 1 and u < n_units - 1:
                        ins.then_inc(self.ready, 1)
                ins.then_inc(self.used, 1)
                s += 1

    def operands(self, s):
        j, k = self.steps[s]
        cols = self.m.blocks[self.first + j][2]
        act = self.jobs[j]["act"]
        tokens = act.shape[2]
        return ((self.m.block_view(self.first + j)[:, k, :], self.w_split[s % self.ns][:, :, 0:cols]),
                (act[:, k, :], self.a_split[s % self.ns][:, :, 0:tokens]))

    def highs(self, act, s):
        j, k = self.steps[s]
        if k == 0:
            self.m.wait_block(act, self.first + j)
        if s >= self.ns:
            act.wait_ge(self.used, s - self.ns + 1)
        for x, parts in self.operands(s):
            self.m.nc.scalar.activation(parts[:, 0, :], x, ACT.Copy).then_inc(self.high, 1)

    def lows(self, dve, s):
        for i, (x, parts) in enumerate(self.operands(s)):
            dve.wait_ge(self.high, 2 * s + i + 1)
            self.m.nc.vector.tensor_tensor(parts[:, 1, :], x, parts[:, 0, :].bitcast(F32),
                                           ALU.subtract).then_inc(self.low, 1)

    def take(self, which, engine, n):
        j, u, _, _, done, _ = self.units[n]
        engine.wait_ge(*done)
        ins = self.jobs[j]["take"](None, u, self.psum(n))
        if ins is None:
            engine.sem_inc(self.out[which], 1)
        else:
            ins.then_inc(self.out[which], 1)

    def split(self, which, engine, after=None):
        last = max(len(self.steps) - 1, self.units[-1][5], max(after) if after else 0)
        for s in range(last + 1):
            if s < len(self.steps):
                if which == "act":
                    self.highs(engine, s)
                else:
                    self.lows(engine, s)
            for n, unit in enumerate(self.units):
                if unit[5] == s and unit[2] == which:
                    self.take(which, engine, n)
            for work in (after or {}).get(s, []):
                work()

    def send(self, sp, ahead=2):
        self.m.send_blocks(sp, self.first + len(self.jobs) + ahead)

    def stage(self, ahead=2, tail=None):
        with self.m.nc.Block() as block:
            @block.sync
            def _(sp):
                self.send(sp, ahead)
                if tail:
                    tail(sp)

            @block.tensor
            def _(pe):
                self.products(pe)

            @block.scalar
            def _(act):
                self.split("act", act)

            @block.vector
            def _(dve):
                self.split("dve", dve)


def setup_stage(m, h, turns, rows, names):
    nc, ps, dram = m.nc, m.ps, m.dram
    stage = m.area("gain_rows", [P, 2, P], rows)
    lq = m.area("lambda_rows", [P, 4, 64], rows + 1024)
    lw = m.area("lambda_work", [P, 2, 64], rows + 2048)
    ls = m.area("lambda_sums", [P, 4], rows + 2560)
    small = m.sem("small_loaded")
    cleared = m.sem("rows_cleared")
    turned = m.sem("gains_turned")
    sums = m.sem("lambda_sums_ready")
    exps = m.sem("lambda_exps_ready")
    m.tokens_loaded = m.sem("tokens_loaded")
    m.turns_loaded = m.sem("turns_loaded")
    at, m.col_of, loads = 0, {}, []
    for name, src in names:
        k = src.shape[0]
        if at < P and at + k > P:
            at = P
        m.col_of[name] = at
        loads.append((src, at // P, at % P, k))
        at += k
    assert at <= 2 * P
    n_small = 1 + len(loads) + 4 + 2 + 2

    with nc.Block() as block:
        @block.sync
        def _(sp):
            x = dram["x"][0]
            sp.dma_start(h[0:META, 0, :], dram["meta_tokens"]).then_inc(m.tokens_loaded, 16)
            sp.dma_start(h[META:P, 0, :], x[0:P - META, :]).then_inc(m.tokens_loaded, 16)
            for t, (t0, n) in enumerate(TILES1[1:], 1):
                sp.dma_start(h[0:n, t, :], x[t0 - META:t0 - META + n, :]).then_inc(m.tokens_loaded, 16)
            sp.dma_start(m.masks[:], dram["masks"]).then_inc(small, 16)
            sp.wait_ge(cleared, 1)
            for src, g, at, k in loads:
                sp.dma_start(stage[at:at + k, g, :], src).then_inc(small, 16)
            for i, name in enumerate(("lambda_q1", "lambda_k1", "lambda_q2", "lambda_k2")):
                sp.dma_start(lq[:, i, :], dram[name].to_broadcast([P, 64])).then_inc(small, 16)
            for i, src in enumerate((dram["b_q_gain_2"], dram["k_gain_2"].unsqueeze(0))):
                sp.dma_start(m.gpe[:, i, :], src[:, NOPE:].to_broadcast([P, ROPE])).then_inc(small, 16)
            for i, name in enumerate(("a_ig_bias_2", "a_fg_bias_2")):
                sp.dma_start(m.gate_bias[:, MH * i:MH * (i + 1)],
                             dram[name].to_broadcast([P, MH])).then_inc(small, 16)
            sp.dma_start(turns[:], dram["turns"]).then_inc(m.turns_loaded, 16)
            m.send_blocks(sp, 2)
            sp.wait_ge(m.tokens_loaded, 16 * (1 + len(TILES1)))
            sp.wait_ge(m.turns_loaded, 16)

        @block.tensor
        def _(pe):
            pe.wait_ge(small, 16 * n_small)
            for g in range(2):
                ins = pe.transpose(ps[:, g, 0:P], stage[:, g, :], m.ident)
            ins.then_inc(turned, 1)

        @block.vector
        def _(dve):
            step = m.dve_steps.on(dve)
            nc.vector.memset(stage[:], 0.0).then_inc(cleared, 1)
            nc.vector.memset(m.eps[:], EPS)
            dve.wait_ge(small, 16 * n_small)
            for i in range(2):
                ins = nc.vector.tensor_tensor_reduce(
                    out=lw[:, i, :], in0=lq[:, 2 * i, :], in1=lq[:, 2 * i + 1, :], scale=1.0, scalar=0.0,
                    op0=ALU.mult, op1=ALU.add, accum_out=ls[:, i:i + 1])
                ins.then_inc(sums, 1)
            dve.wait_ge(turned, 1)
            step(nc.vector.tensor_copy(m.cols[:], ps[:, 0:2, 0:P]))
            dve.wait_ge(exps, 1)
            step(nc.vector.tensor_tensor(m.lam[:], ls[:, 3:4], ls[:, 2:3], ALU.subtract))
            step(nc.vector.tensor_scalar(m.lam[:], m.lam[:], -LAM_INIT, None, ALU.add))

        @block.scalar
        def _(act):
            act.wait_ge(sums, 2)
            nc.scalar.activation(ls[:, 2:4], ls[:, 0:2], ACT.Exp).then_inc(exps, 1)


def projection_stage(m, hn, qk, v, raw, turns, rot_work):
    nc, ps = m.nc, m.ps
    halved = lambda t: t.rearrange("p (a b) -> p a b", a=2)
    scale = 64.0 ** -0.5

    def take_qk(block):
        def take(step, u, psum):
            return nc.scalar.activation(halved(qk[:, 4 * block + u, :]), psum, ACT.Copy,
                                        scale=scale if block == 0 else 1.0)
        return take

    def take_v(step, u, psum):
        return nc.scalar.activation(v[0:TILES1[u][1], u, :], psum, ACT.Copy)

    def take_raw(part):
        def take(step, u, psum):
            return nc.scalar.activation(halved(raw[:, 4 * part + u, :]), psum, ACT.Copy)
        return take

    takes = [("features", take_qk(0)), ("features", take_qk(1)), ("tokens", take_v)] + [
        ("features", take_raw(i)) for i in range(3)]
    jobs = [dict(kind=kind, act=hn, tiles=TILES1, engine="act", take=take) for kind, take in takes]
    g = Gemm(m, "in1", jobs, pairs=3)
    rotated = m.sem("in1_rotated")
    rot_taken = m.sem("in1_rot_taken")

    with nc.Block() as block:
        @block.sync
        def _(sp):
            g.send(sp)
            m.send_experts(sp, 3)

        @block.tensor
        def _(pe):
            def rotate(n):
                pe.wait_ge(g.out["act"], n + 1)
                if n >= 1:
                    pe.wait_ge(rot_taken, n)
                for a in range(2):
                    ins = pe.matmul(ps[:, 6 + a, 0:HALF1], m.rot, qk[:, n, a * HALF1:(a + 1) * HALF1],
                                    start=True, stop=True)
                ins.then_inc(rotated, 1)

            g.products(pe, lambda pe, n: rotate(n - 1) if 1 <= n <= 8 else None)

        @block.scalar
        def _(act):
            g.take("act", act, m.act_steps.on(act))

        @block.vector
        def _(dve):
            step = m.dve_steps.on(dve)
            for n in range(8):
                dve.wait_ge(rotated, n + 1)
                nc.vector.tensor_tensor(halved(rot_work[:, n % 2, :]), ps[:, 6:8, 0:HALF1],
                                        halved(turns[:, 1, :]), ALU.mult).then_inc(rot_taken, 1)
                step(nc.vector.tensor_tensor(qk[:, n, :], qk[:, n, :], turns[:, 0, :], ALU.mult))
                dve.wait_ge(rot_taken, n + 1)
                step(nc.vector.tensor_tensor(qk[:, n, :], qk[:, n, :], rot_work[:, n % 2, :], ALU.add))


def diff_attention_stage(m, qk, v, raw, mixed, at):
    nc, ps = m.nc, m.ps
    units = [(h, t) for h in range(AH) for t in range(len(TILES1))]
    e = m.area("da_e", [P, 3, 2, L1], at)
    at += 24 * L1
    st = m.area("da_st", [P, 3, 8], at)
    ss = m.area("da_ss", [P, 3, len(TILES1) * AH], at + 96)
    qz = m.area("da_qz", [P, 3, 2, P], at + 96 + 256)
    spare = m.ring_at + 9 * SLOT * 4
    pt = m.at("da_pt", [P, 2, len(TILES1), P], spare)
    spare += 8 * len(TILES1) * P
    o = m.at("da_o", [P, len(TILES1), AH, AV], spare)
    cw = m.at("da_conv", [P, 2, L1], spare + 4 * len(TILES1) * AH * AV)
    junk = m.at("da_junk", [P, AV], spare + 4 * len(TILES1) * AH * AV + 8 * L1)
    scored = m.sem("da_scored")
    maxed = m.sem("da_maxed")
    q_ready = m.sem("da_q_ready")
    exped = m.sem("da_exped")
    mixed_ready = m.sem("da_weights")
    turned = m.sem("da_turned")
    pt_ready = m.sem("da_pt_ready")
    summed = m.sem("da_summed")
    o_ready = m.sem("da_o_ready")
    squared = m.sem("da_squared")
    root = m.sem("da_root")
    scaled = m.sem("da_scaled")
    o_turned = m.sem("da_o_turned")
    cleared = m.sem("da_cleared")
    mixed_taken = m.sem("da_mixed_taken")
    nt, nu = len(TILES1), len(units)

    def pair(u, i):
        return (0, 2, 6)[(2 * u + i) % 3]

    with nc.Block() as block:
        @block.tensor
        def _(pe):
            def scores(u):
                h, t = units[u]
                t0, n = TILES1[t]
                pe.wait_ge(q_ready, 2 * u + 3)
                for i in range(2):
                    if 2 * u + i >= 3:
                        pe.wait_ge(exped, 2 * u + i - 2)
                    for a in range(2):
                        ins = pe.matmul(ps[0:n, pair(u, i) + a, 0:HALF1], qz[:, u % 3, i, 0:n],
                                        qk[:, 4 + h, a * HALF1:(a + 1) * HALF1], start=True, stop=True)
                    ins.then_inc(scored, 1)

            def turn(u):
                n = TILES1[units[u][1]][1]
                pe.wait_ge(mixed_ready, u + 1)
                for s, (s0, w) in enumerate(TILES1):
                    if s == 4 and u >= 1:
                        pe.wait_ge(o_ready, u)
                    ins = pe.transpose(ps[0:w, 4 + s // 4, (s % 4) * P:(s % 4) * P + n],
                                       e[0:n, u % 3, 0, s0:s0 + w], m.ident[0:n, 0:n])
                ins.then_inc(turned, 1)

            def values(u):
                h, t = units[u]
                n = TILES1[t][1]
                pe.wait_ge(pt_ready, u + 1)
                for s, (s0, w) in enumerate(TILES1):
                    ins = pe.matmul(ps[0:n, 5, 0:AV], pt[0:w, u % 2, s, 0:n],
                                    v[0:w, s, h * AV:(h + 1) * AV], start=(s == 0), stop=(s == nt - 1))
                ins.then_inc(summed, 1)

            for u in range(nu + 2):
                if u >= 2:
                    turn(u - 2)
                if u < nu:
                    scores(u)
                if u >= 2:
                    values(u - 2)
            for t, (_, n) in enumerate(TILES1):
                pe.wait_ge(scaled, t + 1)
                for h in range(AH):
                    ins = pe.transpose(ps[:, t % 4, h * P:h * P + n], o[0:n, t, h, :], m.ident[0:n, 0:n])
                ins.then_inc(o_turned, 1)
                if t == 3:
                    pe.wait_ge(mixed_taken, 1)

        @block.vector
        def _(dve):
            step = m.dve_steps.on(dve)
            nc.vector.memset(ss[:], 1.0).then_inc(cleared, 1)
            dve.wait_ge(cleared, 1)
            step(nc.vector.tensor_scalar(m.col("subln"), m.col("subln"), 1.0 - LAM_INIT, None, ALU.mult))

            def combine(u):
                n = TILES1[units[u][1]][1]
                b = u % 3
                dve.wait_ge(exped, 2 * u + 2)
                step(nc.vector.reciprocal(st[0:n, b, 4:6], st[0:n, b, 2:4]))
                step(nc.vector.tensor_tensor(st[0:n, b, 6:7], st[0:n, b, 5:6], m.lam[0:n, :], ALU.mult))
                step(nc.vector.tensor_scalar(e[0:n, b, 1, :], e[0:n, b, 1, :], st[0:n, b, 6:7], None, ALU.mult))
                nc.vector.scalar_tensor_tensor(out=e[0:n, b, 0, :], in0=e[0:n, b, 0, :], scalar=st[0:n, b, 4:5],
                                               in1=e[0:n, b, 1, :], op0=ALU.mult,
                                               op1=ALU.add).then_inc(mixed_ready, 1)

            def squares(u):
                h, t = units[u]
                n = TILES1[t][1]
                dve.wait_ge(o_ready, u + 1)
                nc.vector.tensor_tensor_reduce(
                    out=junk[0:n, :], in0=o[0:n, t, h, :], in1=o[0:n, t, h, :], scale=1.0 / AV, scalar=0.0,
                    op0=ALU.mult, op1=ALU.add,
                    accum_out=ss[0:n, 0, t * AH + h:t * AH + h + 1]).then_inc(squared, 1)
                dve.wait_ge(squared, u + 1)

            def maxima(u):
                n = TILES1[units[u][1]][1]
                for i in range(2):
                    dve.wait_ge(scored, 2 * u + i + 1)
                    nc.vector.tensor_reduce(st[0:n, u % 3, i:i + 1], ps[0:n, pair(u, i):pair(u, i) + 2, 0:HALF1],
                                            AX.XY, ALU.max, negate=True).then_inc(maxed, 1)

            for u in range(nu + 4):
                if u < nu:
                    maxima(u)
                if 1 <= u <= nu:
                    combine(u - 1)
                if u >= 4:
                    squares(u - 4)
            dve.wait_ge(root, 1)
            step(nc.vector.reciprocal(ss[:, 2, :], ss[:, 1, :]))
            for t, (_, n) in enumerate(TILES1):
                nc.vector.tensor_tensor(o[0:n, t], o[0:n, t], spread(ss[0:n, 2, t * AH:(t + 1) * AH], AV),
                                        ALU.mult).then_inc(scaled, 1)
            for t, (t0, n) in enumerate(TILES1):
                dve.wait_ge(o_turned, t + 1)
                bank = ps[:, t % 4, :].rearrange("p (k c) -> p k c", k=4)[:, :, 0:n]
                nc.vector.tensor_scalar(mixed[:, 0:AH, t0:t0 + n], bank, m.col("subln"), None,
                                        ALU.mult).then_inc(mixed_taken, 1)

        def take_turned(act, u):
            n = TILES1[units[u][1]][1]
            w = TILES1[-1][1]
            act.wait_ge(turned, u + 1)
            nc.scalar.activation(pt[:, u % 2, 0:4, 0:n], ps[:, 4, :].rearrange("p (k c) -> p k c", k=4)[:, :, 0:n],
                                 ACT.Copy)
            nc.scalar.activation(pt[0:w, u % 2, 4, 0:n], ps[0:w, 5, 0:n], ACT.Copy).then_inc(pt_ready, 1)

        def take_values(act, u):
            h, t = units[u]
            n = TILES1[t][1]
            act.wait_ge(summed, u + 1)
            nc.scalar.activation(o[0:n, t, h, :], ps[0:n, 5, 0:AV], ACT.Copy).then_inc(o_ready, 1)

        @block.scalar
        def _(act):
            def exps(u, i):
                n = TILES1[units[u][1]][1]
                b = u % 3
                act.wait_ge(maxed, 2 * u + i + 1)
                if u >= 3:
                    act.wait_ge(turned, u - 2)
                nc.scalar.activation(e[0:n, b, i, :].rearrange("p (a c) -> p a c", a=2),
                                     ps[0:n, pair(u, i):pair(u, i) + 2, 0:HALF1], ACT.Exp, bias=st[0:n, b, i:i + 1],
                                     accum_out=st[0:n, b, 2 + i:3 + i]).then_inc(exped, 1)

            for u in range(nu + 2):
                if u >= 2:
                    take_turned(act, u - 2)
                if u < nu:
                    exps(u, 0)
                if u >= 2:
                    take_values(act, u - 2)
                if u < nu:
                    exps(u, 1)
            act.wait_ge(squared, len(units))
            nc.scalar.activation(ss[:, 1, :], ss[:, 0, :], ACT.Sqrt, bias=m.eps[:, 0:1]).then_inc(root, 1)

        @block.gpsimd
        def _(pool):
            step = m.pool_steps.on(pool)
            g = nc.gpsimd
            g.memset(qz[:], 0.0).then_inc(q_ready, 1)
            pool.wait_ge(q_ready, 1)

            def queries(u):
                h, t = units[u]
                t0, n = TILES1[t]
                if u >= 3:
                    pool.wait_ge(scored, 2 * (u - 2))
                for i in range(2):
                    d = slice(64 * i, 64 * i + 64)
                    g.tensor_copy(qz[d, u % 3, i, 0:n], qk[d, h, t0:t0 + n]).then_inc(q_ready, 1)
                    pool.wait_ge(q_ready, 2 * u + i + 2)

            def convolution(c):
                cx, cb, cc = raw[:, c, :], raw[:, 4 + c, :], raw[:, 8 + c, :]
                yield g.tensor_tensor(cc, cc, cx, ALU.mult)
                yield g.tensor_scalar(cw[:, 0, :], cc, m.col("conv_w", 4 + c), None, ALU.mult)
                yield g.tensor_scalar(cw[:, 1, :], cc, m.col("conv_w", c), None, ALU.mult)
                yield g.tensor_tensor(cw[:, 0, 1:], cw[:, 0, 1:], cw[:, 1, 0:L1 - 1], ALU.add)
                yield g.tensor_scalar(cw[:, 1, :], cc, m.col("conv_w", 8 + c), None, ALU.mult)
                yield g.tensor_tensor(cw[:, 0, 0:L1 - 1], cw[:, 0, 0:L1 - 1], cw[:, 1, 1:], ALU.add)
                yield g.tensor_tensor(mixed[:, AH + c, :], cw[:, 0, :], cb, ALU.mult)

            conv = (ins for c in range(4) for ins in convolution(c))
            for u in range(len(units)):
                queries(u)
                if u >= 2:
                    for _ in range(2):
                        ins = next(conv, None)
                        if ins is not None:
                            step(ins)


def out_stage(m, name, mixed, x, tiles, slots, ahead=2):
    def take(c):
        def f(step, u, psum):
            to = x[0:tiles[u][1], u, c * 512:(c + 1) * 512]
            return m.nc.vector.tensor_tensor(to, psum, to, ALU.add)
        return f

    SplitGemm(m, name, [dict(kind="tokens", act=mixed, tiles=tiles, engine="dve", take=take(c))
                        for c in range(2)], slots).stage(ahead)


def router_stage(m, hn, at):
    nc, ps = m.nc, m.ps
    nt = len(TILES1)
    w = m.area("router_w", [P, KD, NE], at)
    aff = m.area("router_aff", [P, nt, NE], at + 512)
    st = m.area("router_st", [P, 3, 8], at + 832)
    afft = m.area("router_afft", [NE, 2, L1], at + 960)
    vals = m.area("router_vals", [NE, 8 * ROUNDS], at + 960 + 8 * L1)
    idx = m.area("router_idx", [NE, 8 * ROUNDS], at + 1280 + 8 * L1, U32)
    idxf = m.area("router_idxf", [NE, 8 * ROUNDS], at + 1600 + 8 * L1)
    loaded = m.sem("router_loaded")
    scored = m.sem("router_scored")
    shifted = m.sem("router_shifted")
    exped = m.sem("router_exped")
    normed = m.sem("router_normed")
    turned = m.sem("router_turned")
    picked = m.sem("router_picked")
    picks_turned = m.sem("router_picks_turned")

    with nc.Block() as block:
        @block.sync
        def _(sp):
            sp.dma_start(w[:], m.dram["w_router"][0].rearrange("(k p) e -> p k e", p=P)).then_inc(loaded, 16)
            m.send_experts(sp, NPIECE)

        @block.tensor
        def _(pe):
            pe.wait_ge(loaded, 16)
            for t, (t0, n) in enumerate(TILES1):
                for k in range(KD):
                    ins = pe.matmul(ps[0:n, t, 0:NE], hn[:, k, t0:t0 + n], w[:, k, :],
                                    start=(k == 0), stop=(k == KD - 1))
                ins.then_inc(scored, 1)
            pe.wait_ge(normed, 1)
            for t, (_, n) in enumerate(TILES1):
                ins = pe.transpose(ps[0:NE, 6 + t // 4, (t % 4) * P:(t % 4) * P + n], aff[0:n, t, :],
                                   m.ident[0:n, 0:n])
            ins.then_inc(turned, 1)
            pe.wait_ge(picked, 1)
            pe.transpose(ps[0:CAP, 0, 0:NE], vals[:, 0:CAP], m.ident[0:NE, 0:NE])
            pe.transpose(ps[0:CAP, 0, NE:2 * NE], idxf[:, 0:CAP], m.ident[0:NE, 0:NE]).then_inc(picks_turned, 1)

        @block.vector
        def _(dve):
            step = m.dve_steps.on(dve)
            step(nc.vector.memset(aff[:], 0.0))
            for t, (_, n) in enumerate(TILES1):
                dve.wait_ge(scored, t + 1)
                step(nc.vector.tensor_copy(aff[0:n, t, :], ps[0:n, t, 0:NE]))
            step(nc.vector.tensor_reduce(st[:, 0, 0:nt], aff[:], AX.X, ALU.max))
            nc.vector.tensor_tensor(aff[:], aff[:], spread(st[:, 0, 0:nt], NE), ALU.subtract).then_inc(shifted, 1)
            dve.wait_ge(exped, 1)
            step(nc.vector.tensor_reduce(st[:, 1, 0:nt], aff[:], AX.X, ALU.add))
            step(nc.vector.reciprocal(st[:, 2, 0:nt], st[:, 1, 0:nt]))
            nc.vector.tensor_tensor(aff[:], aff[:], spread(st[:, 2, 0:nt], NE), ALU.mult).then_inc(normed, 1)
            dve.wait_ge(turned, 1)
            nc.vector.tensor_copy(afft[:, 0, 0:512], ps[0:NE, 6, :])
            step(nc.vector.tensor_copy(afft[:, 0, 512:L1], ps[0:NE, 7, 0:L1 - 512]))
            for r in range(ROUNDS):
                a = afft[:, r % 2, :]
                best = vals[:, 8 * r:8 * r + 8]
                step(nc.vector.max(best, a))
                step(nc.vector.max_index(idx[:, 8 * r:8 * r + 8], best, a))
                if r + 1 < ROUNDS:
                    step(nc.vector.match_replace(afft[:, (r + 1) % 2, :], best, a, -1.0))
            nc.vector.tensor_copy(idxf[:], idx[:]).then_inc(picked, 1)
            dve.wait_ge(picks_turned, 1)
            nc.vector.tensor_copy(m.gates[:], ps[0:CAP, 0, 0:NE])
            step(nc.vector.tensor_copy(m.rows[:], ps[0:CAP, 0, NE:2 * NE]))

        @block.scalar
        def _(act):
            act.wait_ge(shifted, 1)
            nc.scalar.activation(aff[:], aff[:], ACT.Exp).then_inc(exped, 1)


def experts_stage(m, at):
    nc, ps = m.nc, m.ps
    PIECES = 24
    FIRST = 8
    AHEAD = 2
    size = 4 * KD * CAP
    xg = m.area("ex_rows", [CAP, D], at)
    hid = m.area("ex_hidden", [CAP, FH], at + 4096)
    y = m.area("ex_y", [CAP, D], at + 8192)
    at += 12288
    x_part = [m.area(f"ex_x{i}", [P, KD, CAP], at + size * i, F32R) for i in range(2)]
    h_part = [m.area(f"ex_h{i}", [P, KD, CAP], at + size * (2 + i), F32R) for i in range(2)]
    xs = m.area("ex_x_scaled", [P, KD, CAP], at + size * 4)
    at += 5 * size
    rows_in = m.area("ex_rows_in", [CAP, 1], at, U32)
    rows_out = m.area("ex_rows_out", [CAP, 1], at + 32, U32)
    gate = m.area("ex_gate", [CAP, 1], at + 64)
    high_done = m.sem("ex_high_done")
    low_done = m.sem("ex_low_done")
    used = m.sem("ex_pieces_used")
    silu_done = m.sem("ex_silu_done")
    hid_done = m.sem("ex_hidden_done")
    turned = m.sem("ex_hidden_turned")
    h_high = m.sem("ex_h_high")
    h_done = m.sem("ex_h_split")
    rows_ready = m.sem("ex_rows_ready")
    gathered = m.lasting("ex_gathered")
    x_turned = m.sem("ex_x_turned")
    x_scaled = m.sem("ex_x_scaled")
    x_high = m.sem("ex_x_high")
    x_done = m.sem("ex_x_split")
    gate_ready = m.sem("ex_gate_ready")
    y_done = m.sem("ex_y_done")
    y_free = m.sem("ex_y_free")
    scattered = m.lasting("ex_scattered")
    sp_passed = m.sem("ex_sp_waits_passed")
    pool_passed = m.sem("ex_pool_waits_passed")
    quarter = lambda bank: bank[:, 0:4 * CAP].rearrange("p (k c) -> p k c", k=4)

    with nc.Block() as block:
        @block.sync
        def _(sp):
            for n in range(NPIECE, 12):
                sp.wait_ge(low_done, n - NPIECE + 1)
                m.expert_load(sp, 12 + n if n < FIRST else n - FIRST, 0, n % NPIECE)
            with sp.Fori(0, NE - 1) as e:
                for i in range(PIECES):
                    wait_counted(sp, low_done, e * PIECES + (12 - NPIECE + 1 + i), sp_passed)
                    j = (4 + i) % PIECES
                    ahead = (4 + i) // PIECES + (1 if 12 <= j < 20 else 0)
                    m.expert_load(sp, j, bass.ds(e + ahead, 1), i % NPIECE)
            n = 12 + PIECES * (NE - 1)
            for j in list(range(4, 12)) + list(range(20, 24)):
                sp.wait_ge(low_done, n - NPIECE + 1)
                m.expert_load(sp, j, NE - 1, n % NPIECE)
                n += 1

        @block.tensor
        def _(pe):
            first_unit = 0

            def products(n, e, banks, parts, k0, start, stop):
                pe.wait_ge(low_done, e * PIECES + (n + 1))
                w = [x[:, n % NSPLIT, :].rearrange("p (k c) -> p k c", k=2) for x in (m.high, m.low_part)]
                for k in range(2):
                    for a, b in ((0, 0), (0, 1), (1, 0)):
                        for c in range(2):
                            ins = pe.matmul(ps[0:CAP, banks + c, :], parts[a][:, k0 + k, :],
                                            w[b][:, k, c * 512:(c + 1) * 512],
                                            start=start and k == 0 and a == b == 0,
                                            stop=stop and k == 1 and a == 1)
                ins.then_inc(used, 1)

            def gate_up(n, e, unit, turn_unit=None):
                for i in range(8):
                    if i == 0 and unit is not first_unit:
                        pe.wait_ge(hid_done, unit)
                    products(n + i, e, 2 * (i % 2), x_part, 2 * (i // 2), i < 2, i >= 6)
                    if i == 3 and turn_unit is not None:
                        turn(turn_unit)

            def turn(unit):
                for k in range(KD):
                    ins = pe.transpose(ps[:, 6 + k // 4, (k % 4) * CAP:(k % 4 + 1) * CAP],
                                       hid[:, k * P:(k + 1) * P], m.ident[0:CAP, 0:CAP])
                ins.then_inc(turned, 1)

            def turn_x(count):
                pe.wait_ge(gathered, count * 16)
                for k in range(KD):
                    ins = pe.transpose(ps[:, 6 + k // 4, (k % 4) * CAP:(k % 4 + 1) * CAP],
                                       xg[:, k * P:(k + 1) * P], m.ident[0:CAP, 0:CAP])
                ins.then_inc(x_turned, 1)

            def down(n, e, unit, half, next_x=None):
                for i in range(4):
                    if i == 0:
                        pe.wait_ge(h_done, unit + 1)
                        if half == 0:
                            pe.wait_ge(y_free, e + 1)
                    products(n + i, e, 4, h_part, 2 * i, half == 0 and i == 0, half == 1 and i == 3)
                    if i == 0 and next_x is not None:
                        turn_x(next_x)

            turn_x(1)
            pe.wait_ge(x_done, 1)
            gate_up(0, 0, first_unit)
            with pe.Fori(0, NE - 1) as e:
                gate_up(FIRST, e, e * 2 + 1, turn_unit=e * 2)
                down(FIRST + 8, e, e * 2, 0, next_x=e + 2)
                pe.wait_ge(x_done, e + 2)
                gate_up(FIRST + 12, e, e * 2 + 2, turn_unit=e * 2 + 1)
                down(FIRST + 20, e, e * 2 + 1, 1)
            e = NE - 1
            gate_up(FIRST, e, e * 2 + 1, turn_unit=e * 2)
            down(FIRST + 8, e, e * 2, 0)
            pe.wait_ge(hid_done, e * 2 + 2)
            turn(e * 2 + 1)
            down(FIRST + 12, e, e * 2 + 1, 1)

        @block.scalar
        def _(act):
            def high(n, e=None):
                rounds = 16 * (n // NPIECE + 1)
                act.wait_ge(m.expert_loaded[n % NPIECE],
                            rounds if e is None else e * (16 * PIECES // NPIECE) + rounds)
                if e is not None:
                    act.wait_ge(used, e * PIECES + (n - NSPLIT + 1))
                elif n >= NSPLIT:
                    act.wait_ge(used, n - NSPLIT + 1)
                nc.scalar.activation(m.high[:, n % NSPLIT, :], m.pieces[:, n % NPIECE, :],
                                     ACT.Copy).then_inc(high_done, 1)

            def silu(pieces):
                act.wait_ge(used, pieces)
                nc.scalar.activation(hid[:].rearrange("p (a c) -> p a c", a=2), ps[0:CAP, 0:2, :],
                                     ACT.Silu).then_inc(silu_done, 1)

            def take_turned(unit):
                act.wait_ge(turned, unit + 1)
                nc.scalar.activation(h_part[0][:].rearrange("p (a k) c -> p a (k c)", a=2),
                                     ps[:, 6:8, 0:4 * CAP], ACT.Copy).then_inc(h_high, 1)

            for n in range(FIRST + AHEAD):
                high(n)
            silu(FIRST)
            with act.Fori(0, NE - 1) as e:
                for i in range(PIECES):
                    high(FIRST + AHEAD + i, e)
                    if i == 3:
                        take_turned(e * 2)
                    if i == 7:
                        silu(e * PIECES + (FIRST + 8))
                    if i == 15:
                        take_turned(e * 2 + 1)
                    if i == 19:
                        silu(e * PIECES + (FIRST + 20))
            base = PIECES * (NE - 1) + FIRST
            for i in range(16):
                if i + AHEAD < 16:
                    high(base + AHEAD + i)
                if i == 3:
                    take_turned(2 * NE - 2)
                if i == 7:
                    silu(base + 8)
                if i == 11:
                    take_turned(2 * NE - 1)

        @block.vector
        def _(dve):
            def low(n, e=None):
                dve.wait_ge(high_done, n + 1 if e is None else e * PIECES + (n + 1))
                nc.vector.tensor_tensor(m.low_part[:, n % NSPLIT, :], m.pieces[:, n % NPIECE, :],
                                        m.high[:, n % NSPLIT, :].bitcast(F32), ALU.subtract).then_inc(low_done, 1)

            def next_rows(e):
                nc.vector.tensor_copy(rows_in[:], m.rows[:, bass.ds(e, 1)]).then_inc(rows_ready, 1)

            def hidden(unit):
                dve.wait_ge(silu_done, unit + 1)
                h = hid[:].rearrange("p (a c) -> p a c", a=2)
                nc.vector.tensor_tensor(h, ps[0:CAP, 2:4, :], h, ALU.mult).then_inc(hid_done, 1)

            def split_hidden(unit):
                dve.wait_ge(h_high, unit + 1)
                for a in range(2):
                    ins = nc.vector.tensor_tensor(h_part[1][:, 4 * a:4 * a + 4, :], quarter(ps[:, 6 + a, :]),
                                                  h_part[0][:, 4 * a:4 * a + 4, :].bitcast(F32), ALU.subtract)
                ins.then_inc(h_done, 1)

            def take_x(count):
                dve.wait_ge(x_turned, count)
                for a in range(2):
                    ins = nc.vector.tensor_tensor(xs[:, 4 * a:4 * a + 4, :], quarter(ps[:, 6 + a, :]),
                                                  spread(m.colrange("ffn_g", KD)[:, 4 * a:4 * a + 4], CAP),
                                                  ALU.mult)
                ins.then_inc(x_scaled, 1)
                dve.wait_ge(x_scaled, count)
                nc.vector.tensor_copy(x_part[0][:], xs[:]).then_inc(x_high, 1)
                dve.wait_ge(x_high, count)
                nc.vector.tensor_tensor(x_part[1][:], xs[:], x_part[0][:].bitcast(F32),
                                        ALU.subtract).then_inc(x_done, 1)

            def take_y(e, pieces):
                dve.wait_ge(y_free, e + 1)
                nc.vector.tensor_copy(rows_out[:], m.rows[:, bass.ds(e, 1)])
                nc.vector.tensor_copy(gate[:], m.gates[:, bass.ds(e, 1)]).then_inc(gate_ready, 1)
                dve.wait_ge(gate_ready, e + 1)
                dve.wait_ge(used, pieces)
                nc.vector.tensor_scalar(y[:].rearrange("p (a c) -> p a c", a=2), ps[0:CAP, 4:6, :],
                                        gate[:, 0:1], None, ALU.mult).then_inc(y_done, 1)

            next_rows(0)
            for n in range(FIRST + AHEAD):
                low(n)
                if n == 0:
                    take_x(1)
            hidden(0)
            with dve.Fori(0, NE - 1) as e:
                for i in range(PIECES):
                    if i == 0:
                        dve.wait_ge(gathered, e * 16 + 16)
                        next_rows(e + 1)
                    low(FIRST + AHEAD + i, e)
                    if i == 3:
                        split_hidden(e * 2)
                    if i == 7:
                        hidden(e * 2 + 1)
                    if i == 8:
                        take_x(e + 2)
                    if i == 15:
                        split_hidden(e * 2 + 1)
                    if i == 19:
                        hidden(e * 2 + 2)
                    if i == 23:
                        take_y(e, e * PIECES + (FIRST + 24))
            base = PIECES * (NE - 1) + FIRST
            for i in range(16):
                if i + AHEAD < 16:
                    low(base + AHEAD + i)
                if i == 3:
                    split_hidden(2 * NE - 2)
                if i == 7:
                    hidden(2 * NE - 1)
                if i == 11:
                    split_hidden(2 * NE - 1)
            take_y(NE - 1, NE * PIECES)

        @block.gpsimd
        def _(pool):
            def gather(count):
                wait_counted(pool, rows_ready, count, pool_passed)
                nc.gpsimd.indirect_dma_start(
                    out=xg[:], out_offset=None, in_=m.xhat[:],
                    in_offset=bass.IndirectOffsetOnAxis(ap=rows_in[:, 0:1], axis=0)).then_inc(gathered, 16)

            def scatter(e):
                wait_counted(pool, y_done, e + 1, pool_passed)
                nc.gpsimd.indirect_dma_start(
                    out=m.resid[:], out_offset=bass.IndirectOffsetOnAxis(ap=rows_out[:, 0:1], axis=0),
                    in_=y[:], in_offset=None, compute_op=ALU.add).then_inc(scattered, 16)
                pool.wait_ge(scattered, e * 16 + 16)
                pool.sem_inc(y_free, 1)

            pool.sem_inc(y_free, 1)
            gather(1)
            with pool.Fori(0, NE - 1) as e:
                wait_counted(pool, x_turned, e + 1, pool_passed)
                gather(e + 2)
                scatter(e)
            scatter(NE - 1)


def final_norm_stage(m, x, at):
    nc = m.nc
    grow = m.area("fin_gain", [P, D], at)
    junk = m.area("fin_junk", [P, D], at + 4096)
    ss = m.area("fin_ss", [P, 3, 4], at + 8192)
    gain_loaded = m.sem("fin_gain_loaded")
    loaded = [m.sem(f"fin_loaded{t}") for t in range(4)]
    squared = m.sem("fin_squared")
    root = m.sem("fin_root")
    with nc.Block() as block:
        @block.sync
        def _(sp):
            for t in range(4):
                sp.dma_start(x[:, t, :], m.resid[META + t * P:META + (t + 1) * P, :]).then_inc(loaded[t], 16)
            sp.dma_start(grow[:], m.dram["final_norm_g"].unsqueeze(0).to_broadcast([P, D])).then_inc(gain_loaded, 16)
            m.send_blocks(sp, m.taken + 2)

        @block.vector
        def _(dve):
            step = m.dve_steps.on(dve)
            for t in range(4):
                dve.wait_ge(loaded[t], 16)
                nc.vector.tensor_tensor_reduce(
                    out=junk[:], in0=x[:, t, :], in1=x[:, t, :], scale=1.0 / D, scalar=0.0,
                    op0=ALU.mult, op1=ALU.add, accum_out=ss[:, 0, t:t + 1]).then_inc(squared, 1)
                dve.wait_ge(squared, t + 1)
            dve.wait_ge(root, 1)
            step(nc.vector.reciprocal(ss[:, 2, :], ss[:, 1, :]))
            dve.wait_ge(gain_loaded, 16)
            for t in range(4):
                step(nc.vector.scalar_tensor_tensor(out=x[:, t, :], in0=x[:, t, :], scalar=ss[:, 2, t:t + 1],
                                                    in1=grow[:], op0=ALU.mult, op1=ALU.mult))

        @block.scalar
        def _(act):
            act.wait_ge(squared, 4)
            nc.scalar.activation(ss[:, 1, :], ss[:, 0, :], ACT.Sqrt, bias=m.eps[:, 0:1]).then_inc(root, 1)


def group_norm_stage(m, name, jobs, at):
    nc, ps = m.nc, m.ps
    n_ss = sum(j["src"].shape[1] * j["src"].shape[2] for j in jobs)
    ss = m.area(f"{name}_ss", [P, 3, n_ss], at)
    junk = m.area(f"{name}_junk", [P, 512], at + -(-12 * n_ss // 32) * 32)
    squared = m.sem(f"{name}_squared")
    root = m.sem(f"{name}_root")
    scaled = m.sem(f"{name}_scaled")
    turned = m.sem(f"{name}_turned")
    taken = m.sem(f"{name}_taken")
    work, c = [], 0
    for j in jobs:
        _, nt, g, width = j["src"].shape
        for t in range(nt):
            work.append((j, t, g, width, c))
            c += g

    with nc.Block() as block:
        @block.vector
        def _(dve):
            step = m.dve_steps.on(dve)
            for j, t, g, width, c in work:
                x = j["src"][:, t]
                sq = junk[:, 0:g * width].rearrange("p (g w) -> p g w", g=g)
                step(nc.vector.tensor_tensor(sq, x, x, ALU.mult))
                step(nc.vector.tensor_reduce(ss[:, 0, c:c + g], sq, AX.X, ALU.add))
                step(nc.vector.tensor_scalar(ss[:, 0, c:c + g], ss[:, 0, c:c + g], 1.0 / width, None, ALU.mult))
            nc.vector.tensor_copy(ss[:, 2, :], ss[:, 0, :]).then_inc(squared, 1)
            dve.wait_ge(root, 1)
            step(nc.vector.reciprocal(ss[:, 2, :], ss[:, 1, :]))
            for j, t, g, width, c in work:
                x = j["src"][:, t]
                nc.vector.tensor_tensor(x, x, spread(ss[:, 2, c:c + g], width), ALU.mult).then_inc(scaled, 1)
            for n, (j, t, g, width, c) in enumerate(work):
                dve.wait_ge(turned, n + 1)
                per = width // P
                bank = ps[:, n % 8, :].rearrange("p (k c) -> p k c", k=4)
                for i in range(per):
                    ins = nc.vector.tensor_scalar(
                        j["dst"][:, i:g * per:per, t * P:(t + 1) * P], bank[:, i:g * per:per, :],
                        m.col(j["gain"][0], j["gain"][1] + i), j["factor"], ALU.mult, ALU.mult)
                ins.then_inc(taken, 1)

        @block.scalar
        def _(act):
            act.wait_ge(squared, 1)
            nc.scalar.activation(ss[:, 1, :], ss[:, 0, :], ACT.Sqrt, bias=m.eps[:, 0:1]).then_inc(root, 1)

        @block.tensor
        def _(pe):
            for n, (j, t, g, width, c) in enumerate(work):
                pe.wait_ge(scaled, n + 1)
                if n >= 8:
                    pe.wait_ge(taken, n - 7)
                x = j["src"][:, t].rearrange("p g w -> p (g w)")
                for i in range(g * width // P):
                    ins = pe.transpose(ps[:, n % 8, i * P:(i + 1) * P], x[:, i * P:(i + 1) * P], m.ident)
                ins.then_inc(turned, 1)


def attention_stage(m, name, units, at):
    nc, ps = m.nc, m.ps
    probs = m.area(f"{name}_probs", [P, 4, 512], at)
    pt = m.area(f"{name}_pt", [P, 2, 512], at + 8192)
    st = m.area(f"{name}_st", [P, 4, 4], at + 12288)
    scored = m.sem(f"{name}_scored")
    maxed = m.sem(f"{name}_maxed")
    exped = m.sem(f"{name}_exped")
    ready = m.sem(f"{name}_ready")
    turned = m.sem(f"{name}_turned")
    pt_ready = m.sem(f"{name}_pt_ready")
    summed = m.sem(f"{name}_summed")
    taken = m.sem(f"{name}_taken")
    nu = len(units)

    with nc.Block() as block:
        @block.tensor
        def _(pe):
            def scores(u):
                if u >= 3:
                    pe.wait_ge(exped, u - 2)
                for i, (lhs, rhs) in enumerate(units[u]["scores"]):
                    ins = pe.matmul(ps[:, u % 3, 0:units[u]["width"]], lhs, rhs,
                                    start=(i == 0), stop=(i == len(units[u]["scores"]) - 1))
                ins.then_inc(scored, 1)

            def turn(u):
                pe.wait_ge(ready, u + 1)
                if u >= 2:
                    pe.wait_ge(pt_ready, u - 1)
                for s in range(units[u]["width"] // P):
                    ins = pe.transpose(ps[:, 3 + u % 2, s * P:(s + 1) * P], probs[:, u % 4, s * P:(s + 1) * P],
                                       m.ident)
                ins.then_inc(turned, 1)

            def values(u):
                pe.wait_ge(pt_ready, u + 1)
                if u >= 2:
                    pe.wait_ge(taken, u - 1)
                vs = units[u]["values"]
                for s, v in enumerate(vs):
                    ins = pe.matmul(ps[:, 5 + u % 2, 0:P], v, pt[:, u % 2, s * P:(s + 1) * P],
                                    start=(s == 0), stop=(s == len(vs) - 1))
                ins.then_inc(summed, 1)

            for u in range(nu + 3):
                if u < nu:
                    scores(u)
                if 2 <= u < nu + 2:
                    turn(u - 2)
                if u >= 3:
                    values(u - 3)

        @block.vector
        def _(dve):
            step = m.dve_steps.on(dve)

            def head(u):
                w = units[u]["width"]
                dve.wait_ge(scored, u + 1)
                s = ps[:, u % 3, 0:w]
                if units[u]["mask"] is not None:
                    step(nc.vector.tensor_tensor(s[:, w - P:w], s[:, w - P:w], units[u]["mask"], ALU.add))
                nc.vector.tensor_reduce(st[:, u % 4, 0:1], s, AX.X, ALU.max, negate=True).then_inc(maxed, 1)

            def norm(u):
                w = units[u]["width"]
                dve.wait_ge(exped, u + 1)
                step(nc.vector.reciprocal(st[:, u % 4, 2:3], st[:, u % 4, 1:2]))
                p = probs[:, u % 4, 0:w]
                nc.vector.tensor_scalar(p, p, st[:, u % 4, 2:3], None, ALU.mult).then_inc(ready, 1)

            def take(u):
                dve.wait_ge(summed, u + 1)
                y = units[u]["y"]
                nc.vector.tensor_tensor(y, ps[:, 5 + u % 2, 0:P], y, ALU.mult).then_inc(taken, 1)

            for u in range(nu + 4):
                if u < nu:
                    head(u)
                if 1 <= u <= nu:
                    norm(u - 1)
                if u >= 4:
                    take(u - 4)

        @block.scalar
        def _(act):
            for u in range(nu + 2):
                if u < nu:
                    w = units[u]["width"]
                    act.wait_ge(maxed, u + 1)
                    if u >= 4:
                        act.wait_ge(turned, u - 3)
                    nc.scalar.activation(probs[:, u % 4, 0:w], ps[:, u % 3, 0:w], ACT.Exp,
                                         bias=st[:, u % 4, 0:1], accum_out=st[:, u % 4, 1:2]).then_inc(exped, 1)
                if u >= 2:
                    w = units[u - 2]["width"]
                    act.wait_ge(turned, u - 1)
                    if u >= 4:
                        act.wait_ge(summed, u - 3)
                    nc.scalar.activation(pt[:, u % 2, 0:w], ps[:, 3 + u % 2, 0:w],
                                         ACT.Copy).then_inc(pt_ready, 1)


def memory_units(mq, mk, mv, y):
    return [dict(scores=[(mq[:, h, t * P:(t + 1) * P], mk[:, h, :])], width=MEM, mask=None,
                 values=[mv[:, s, h * P:(h + 1) * P] for s in range(MEM // P)],
                 y=y[:, 8 + h, t * P:(t + 1) * P])
            for h in range(MEMH) for t in range(4)]


def memory_stage(m, mem_t, mk_tok, mvs, slots):
    nc = m.nc
    tiles = [(0, P), (P, P)]

    def take(dst):
        def f(step, u, psum):
            return nc.scalar.activation(dst[:, u, :], psum, ACT.Copy)
        return f

    jobs = [dict(kind="tokens", act=mem_t, tiles=tiles, engine="act", take=take(dst))
            for dst in (mk_tok[0], mvs[0], mk_tok[1], mvs[1])]
    SplitGemm(m, "mem", jobs, slots).stage()


def mlstm_in_stage(m, hn, qk, v, y, mq, gates, at):
    nc = m.nc
    raw = m.area("ml_raw", [P, 3, SEQ + 3], at)
    acc = m.area("ml_acc", [P, 2, SEQ], at + 6208)
    zs = m.area("ml_zs", [P, 2, SEQ], at + 6208 + 8 * SEQ)
    slots = m.gaps + [m.arena + at + 6208 + 16 * SEQ]
    padded = m.sem("ml_padded")
    raw_ready = m.sem("ml_raw_ready")
    conv_done = m.sem("ml_conv_done")
    silu_done = m.sem("ml_silu_done")
    z_ready = m.sem("ml_z_ready")
    z_used = m.sem("ml_z_used")
    act = nc.scalar
    NQK = 2 * MW // P

    def finish(n):
        act.wait_ge(conv_done, n + 1)
        act.activation(qk[:, n, :], acc[:, n % 2, :], ACT.Silu,
                       bias=m.col("a_conv_b", n)).then_inc(silu_done, 1)

    def take_qk(block):
        def f(step, u, psum):
            n = 4 * block + u
            if n == 0:
                act.wait_ge(padded, 1)
            if n >= 2:
                finish(n - 2)
            act.activation(raw[:, n % 3, 3:], psum, ACT.Copy).then_inc(raw_ready, 1)
            act.wait_ge(raw_ready, n + 1)
            return None
        return f

    def take_v(block):
        def f(step, u, psum):
            return act.activation(v[:, u, 512 * block:512 * (block + 1)], psum, ACT.Copy)
        return f

    def take_o(block):
        def f(step, u, psum):
            if block == 1 and u < 2:
                finish(NQK - 2 + u)
            return act.activation(y[:, 4 * block + u, :], psum, ACT.Tanh, scale=0.5)
        return f

    def take_z(block):
        def f(step, u, psum):
            n = 4 * block + u
            if n >= 2:
                act.wait_ge(z_used, n - 1)
            act.activation(zs[:, n % 2, :], psum, ACT.Silu).then_inc(z_ready, 1)
            act.wait_ge(z_ready, n + 1)
            return None
        return f

    def take_gates(step, u, psum):
        return act.activation(gates[:, u, :], psum, ACT.Copy)

    def take_mq(step, u, psum):
        return act.activation(mq[:, u, :], psum, ACT.Copy)

    def take_mz(step, u, psum):
        return act.activation(y[:, 8 + u, :], psum, ACT.Silu)

    takes = {"qk": ("features", take_qk), "v": ("tokens", take_v), "o": ("features", take_o),
             "z": ("features", take_z), "gates": ("tokens", lambda _: take_gates),
             "mq": ("tokens", lambda _: take_mq), "mz": ("features", lambda _: take_mz)}
    jobs = [dict(kind=takes[part][0], act=hn, tiles=TILES2, engine="act", take=takes[part][1](block),
                 plain=(part == "gates"), spread=1)
            for part, block, _, _ in MLSTM_IN]
    g = SplitGemm(m, "in2", jobs, slots)

    def convolve(step, n):
        nc.vector.wait_ge(raw_ready, n + 1)
        if n >= 2:
            nc.vector.wait_ge(silu_done, n - 1)
        r, a = raw[:, n % 3, :], acc[:, n % 2, :]
        step(nc.vector.tensor_scalar(a, r[:, 3:], m.col("a_conv_w", 3 * NQK + n), None, ALU.mult))
        for j in (2, 1, 0):
            ins = nc.vector.scalar_tensor_tensor(out=a, in0=r[:, j:j + SEQ],
                                                 scalar=m.col("a_conv_w", j * NQK + n), in1=a,
                                                 op0=ALU.mult, op1=ALU.add)
            if j:
                step(ins)
        ins.then_inc(conv_done, 1)

    def open_gate(n):
        nc.vector.wait_ge(z_ready, n + 1)
        nc.vector.scalar_tensor_tensor(out=y[:, n, :], in0=y[:, n, :], scalar=1.0, in1=zs[:, n % 2, :],
                                       op0=ALU.add, op1=ALU.mult).then_inc(z_used, 1)

    with nc.Block() as block:
        @block.sync
        def _(sp):
            g.send(sp, ahead=0)

        @block.tensor
        def _(pe):
            g.products(pe)

        @block.scalar
        def _(act):
            g.split("act", act)

        @block.vector
        def _(dve):
            step = m.dve_steps.on(dve)
            nc.vector.memset(raw[:, :, 0:3], 0.0).then_inc(padded, 1)
            after = {}
            for j, u, _, _, _, place in g.units:
                part, b = MLSTM_IN[j][0:2]
                work = {"qk": lambda n: convolve(step, n), "z": open_gate}.get(part)
                if work:
                    after.setdefault(place + 1, []).append(lambda n=4 * b + u, f=work: f(n))
            g.split("dve", dve, after)


def mlstm_stage(m, qk, v, gates, ht, y, at):
    nc, ps = m.nc, m.ps
    units = [(h, t) for h in range(MH) for t in range(4)]
    b = m.area("xl_b", [P, 4, SEQ], at)
    e = m.area("xl_e", [P, 2, SEQ], at + 8192)
    p = m.area("xl_p", [P, 3, SEQ], at + 12288)
    pt = m.area("xl_pt", [P, 2, SEQ], at + 18432)
    at += 22528
    lf = m.area("xl_lf", [P, 4, MH], at)
    ig = m.area("xl_ig", [P, 4, MH], at + 64)
    tmp = m.area("xl_tmp", [P, 2, 4 * MH], at + 128)
    nb = m.area("xl_nb", [P, 4, MH], at + 256)
    st = m.area("xl_st", [P, 6, 8], at + 320)
    ss = m.area("xl_ss", [P, 3, 4 * MH], at + 512)
    junk = m.area("xl_junk", [P, MDH], at + 704)
    abs_ready = m.sem("xl_abs")
    exp_ready = m.sem("xl_exp")
    one_ready = m.sem("xl_one")
    ln_ready = m.sem("xl_ln")
    lf_ready = m.sem("xl_lf")
    total_ready = m.sem("xl_totals")
    b_ready = m.sem("xl_b_ready")
    decayed = m.sem("xl_decays")
    scored = m.sem("xl_scored")
    maxed = m.sem("xl_maxed")
    exped = m.sem("xl_exped")
    p_ready = m.sem("xl_p_ready")
    den_ready = m.sem("xl_den_ready")
    turned = m.sem("xl_turned")
    pt_ready = m.sem("xl_pt_ready")
    summed = m.sem("xl_summed")
    h_ready = m.sem("xl_h_ready")
    squared = m.sem("xl_squared")
    root = m.sem("xl_root")
    scaled = m.sem("xl_scaled")
    h_turned = m.sem("xl_h_turned")
    y_taken = m.sem("xl_y_taken")
    nu = len(units)
    QS = MDH ** -0.5

    with nc.Block() as block:
        @block.sync
        def _(sp):
            m.send_blocks(sp, m.taken + 2)

        @block.tensor
        def _(pe):
            pe.wait_ge(lf_ready, 1)
            for t in range(4):
                for u in range(t + 1):
                    ins = pe.matmul(ps[:, 6, t * MH:(t + 1) * MH], m.upto if u == t else m.ones, lf[:, u, :],
                                    start=(u == 0), stop=(u == t))
            ins.then_inc(total_ready, 1)

            def scores(u):
                h, t = units[u]
                w = (t + 1) * P
                if u >= 2:
                    pe.wait_ge(p_ready, u - 1)
                pe.wait_ge(b_ready, h + 1)
                for i in range(t, -1, -1):
                    ins = pe.matmul(ps[:, u % 2, 0:(i + 1) * P], m.upto if i == t else m.ones,
                                    b[:, i, 0:(i + 1) * P], start=(i == t), stop=(i == 0))
                ins.then_inc(decayed, 1)
                for k in range(2):
                    ins = pe.matmul(ps[:, 2 + u % 2, 0:w], qk[:, 2 * h + k, t * P:(t + 1) * P],
                                    qk[:, 8 + 2 * h + k, 0:w], start=(k == 0), stop=(k == 1))
                ins.then_inc(scored, 1)

            def turn(u):
                t = units[u][1]
                pe.wait_ge(p_ready, u + 1)
                if u >= 2:
                    pe.wait_ge(pt_ready, u - 1)
                for s in range(t + 1):
                    ins = pe.transpose(ps[:, 4 + u % 2, s * P:(s + 1) * P], p[:, u % 3, s * P:(s + 1) * P], m.ident)
                ins.then_inc(turned, 1)

            def values(u):
                h, t = units[u]
                pe.wait_ge(pt_ready, u + 1)
                if u == 0:
                    pe.wait_ge(b_ready, 1)
                if u >= 2:
                    pe.wait_ge(h_ready, u - 1)
                for s in range(t + 1):
                    ins = pe.matmul(ps[:, 6 + u % 2, 0:MDH], pt[:, u % 2, s * P:(s + 1) * P],
                                    v[:, s, h * MDH:(h + 1) * MDH], start=(s == 0), stop=(s == t))
                ins.then_inc(summed, 1)

            for u in range(nu + 3):
                if u < nu:
                    scores(u)
                if 2 <= u < nu + 2:
                    turn(u - 2)
                if u >= 3:
                    values(u - 3)
            pe.wait_ge(scaled, 4)
            for f in range(MW // P):
                if f >= 4:
                    pe.wait_ge(y_taken, f - 3)
                for t in range(4):
                    ins = pe.transpose(ps[:, f % 4, t * P:(t + 1) * P], ht[:, t, f * P:(f + 1) * P], m.ident)
                ins.then_inc(h_turned, 1)

        @block.vector
        def _(dve):
            step = m.dve_steps.on(dve)
            gb = lambda k: m.gate_bias[:, MH * k:MH * (k + 1)].unsqueeze(1).to_broadcast([P, 4, MH])
            flat = lambda x: x.rearrange("p a b -> p (a b)")
            step(nc.vector.tensor_tensor(ig[:], gates[:, :, 0:MH], gb(0), ALU.add))
            step(nc.vector.tensor_tensor(lf[:], gates[:, :, MH:2 * MH], gb(1), ALU.add))
            step(nc.vector.tensor_scalar(tmp[:, 0, :], flat(lf[:]), -1.0, None, ALU.mult))
            nc.vector.tensor_tensor(tmp[:, 0, :], tmp[:, 0, :], flat(lf[:]), ALU.max).then_inc(abs_ready, 1)
            dve.wait_ge(exp_ready, 1)
            nc.vector.tensor_scalar(tmp[:, 1, :], tmp[:, 1, :], 1.0, None, ALU.add).then_inc(one_ready, 1)
            dve.wait_ge(ln_ready, 1)
            nc.vector.scalar_tensor_tensor(out=flat(lf[:]), in0=flat(lf[:]), scalar=0.0, in1=tmp[:, 0, :],
                                           op0=ALU.min, op1=ALU.subtract).then_inc(lf_ready, 1)
            dve.wait_ge(lf_ready, 1)
            dve.wait_ge(total_ready, 1)
            step(nc.vector.tensor_scalar(flat(nb[:]), ps[:, 6, 0:4 * MH], -1.0, None, ALU.mult))
            step(nc.vector.tensor_scalar(m.colrange("a_h_norm", 8), m.colrange("a_h_norm", 8), 0.5, None,
                                         ALU.mult))

            def build(h):
                if h:
                    dve.wait_ge(decayed, 4 * h)
                for u in range(4):
                    c = slice(u * P, (u + 1) * P)
                    if u:
                        nc.vector.tensor_scalar(b[:, u, 0:u * P], m.masks[:, 0:u * P], 0.0,
                                                lf[:, u, h:h + 1], ALU.mult, ALU.add)
                    step(nc.vector.tensor_scalar(b[:, u, c], m.after, lf[:, u, h:h + 1], None, ALU.mult))
                    ins = nc.vector.scalar_tensor_tensor(out=b[:, u, c], in0=m.ident, scalar=ig[:, u, h:h + 1],
                                                         in1=b[:, u, c], op0=ALU.mult, op1=ALU.add)
                ins.then_inc(b_ready, 1)

            def head(u):
                h, t = units[u]
                w = (t + 1) * P
                x = ps[:, u % 2, 0:w]
                dve.wait_ge(decayed, u + 1)
                step(nc.vector.tensor_tensor(x[:, t * P:w], x[:, t * P:w], m.causal, ALU.add))
                step(nc.vector.tensor_reduce(st[:, u % 6, 0:1], x, AX.X, ALU.max, negate=True))
                nc.vector.tensor_tensor(st[:, u % 6, 1:2], st[:, u % 6, 0:1], nb[:, t, h:h + 1],
                                        ALU.min).then_inc(maxed, 1)

            def weigh(u):
                h, t = units[u]
                w = (t + 1) * P
                s = st[:, u % 6, :]
                dve.wait_ge(exped, u + 1)
                dve.wait_ge(scored, u + 1)
                if u >= 3:
                    dve.wait_ge(turned, u - 2)
                nc.vector.scalar_tensor_tensor(out=p[:, u % 3, 0:w], in0=ps[:, 2 + u % 2, 0:w], scalar=QS,
                                               in1=e[:, u % 2, 0:w], op0=ALU.mult, op1=ALU.mult,
                                               accum_out=s[:, 3:4]).then_inc(p_ready, 1)
                dve.wait_ge(p_ready, u + 1)
                step(nc.vector.tensor_scalar(s[:, 4:5], s[:, 3:4], -1.0, None, ALU.mult))
                step(nc.vector.tensor_tensor(s[:, 4:5], s[:, 4:5], s[:, 3:4], ALU.max))
                step(nc.vector.tensor_tensor(s[:, 4:5], s[:, 4:5], s[:, 2:3], ALU.max))
                nc.vector.reciprocal(s[:, 5:6], s[:, 4:5]).then_inc(den_ready, 1)

            def squares(u):
                h, t = units[u]
                dve.wait_ge(h_ready, u + 1)
                x = ht[:, t, h * MDH:(h + 1) * MDH]
                nc.vector.tensor_tensor_reduce(
                    out=junk[:], in0=x, in1=x, scale=1.0 / MDH, scalar=0.0, op0=ALU.mult, op1=ALU.add,
                    accum_out=ss[:, 0, t * MH + h:t * MH + h + 1]).then_inc(squared, 1)
                dve.wait_ge(squared, u + 1)

            build(0)
            for u in range(nu + 4):
                if u < nu:
                    head(u)
                if u % 4 == 3 and u + 1 < nu:
                    build((u + 1) // 4)
                if 1 <= u <= nu:
                    weigh(u - 1)
                if u >= 4:
                    squares(u - 4)
            dve.wait_ge(root, 1)
            step(nc.vector.reciprocal(ss[:, 2, :], ss[:, 1, :]))
            for t in range(4):
                x = ht[:, t, :].rearrange("p (h w) -> p h w", h=MH)
                nc.vector.tensor_tensor(x, x, spread(ss[:, 2, t * MH:(t + 1) * MH], MDH),
                                        ALU.mult).then_inc(scaled, 1)
            for f in range(MW // P):
                dve.wait_ge(h_turned, f + 1)
                nc.vector.scalar_tensor_tensor(out=y[:, f, :], in0=ps[:, f % 4, :], scalar=m.col("a_h_norm", f),
                                               in1=y[:, f, :], op0=ALU.mult, op1=ALU.mult).then_inc(y_taken, 1)

        @block.scalar
        def _(act):
            act.wait_ge(abs_ready, 1)
            nc.scalar.activation(tmp[:, 1, :], tmp[:, 0, :], ACT.Exp, scale=-1.0).then_inc(exp_ready, 1)
            act.wait_ge(one_ready, 1)
            nc.scalar.activation(tmp[:, 0, :], tmp[:, 1, :], ACT.Ln).then_inc(ln_ready, 1)

            def exps(u):
                h, t = units[u]
                w = (t + 1) * P
                act.wait_ge(maxed, u + 1)
                if u >= 2:
                    act.wait_ge(p_ready, u - 1)
                nc.scalar.activation(st[:, u % 6, 2:3], st[:, u % 6, 1:2], ACT.Exp)
                nc.scalar.activation(e[:, u % 2, 0:w], ps[:, u % 2, 0:w], ACT.Exp,
                                     bias=st[:, u % 6, 1:2]).then_inc(exped, 1)

            def take_turned(u):
                w = (units[u][1] + 1) * P
                act.wait_ge(turned, u + 1)
                if u >= 2:
                    act.wait_ge(summed, u - 1)
                nc.scalar.activation(pt[:, u % 2, 0:w], ps[:, 4 + u % 2, 0:w], ACT.Copy).then_inc(pt_ready, 1)

            def take_values(u):
                h, t = units[u]
                act.wait_ge(summed, u + 1)
                act.wait_ge(den_ready, u + 1)
                nc.scalar.activation(ht[:, t, h * MDH:(h + 1) * MDH], ps[:, 6 + u % 2, 0:MDH], ACT.Copy,
                                     scale=st[:, u % 6, 5:6]).then_inc(h_ready, 1)

            for u in range(nu + 3):
                if u < nu:
                    exps(u)
                if 2 <= u < nu + 2:
                    take_turned(u - 2)
                if u >= 3:
                    take_values(u - 3)
            act.wait_ge(squared, nu)
            nc.scalar.activation(ss[:, 1, :], ss[:, 0, :], ACT.Sqrt, bias=m.eps[:, 0:1]).then_inc(root, 1)


def copy_stage(m, name, jobs):
    g = Gemm(m, name, jobs)
    with m.nc.Block() as block:
        @block.sync
        def _(sp):
            g.send(sp)

        @block.tensor
        def _(pe):
            g.products(pe)

        @block.scalar
        def _(act):
            g.take("act", act, None)


def rotary_stage(m, turn, at):
    nc = m.nc
    pos = m.area("ro_pos", [P, 4], at, mybir.dt.int32)
    posf = m.area("ro_posf", [P, 4], at + 32)
    ang = m.area("ro_ang", [P, 4, 32], at + 64)
    k = m.area("ro_k", [P, 4, 32], at + 64 + 512)
    loaded = m.sem("ro_loaded")
    reduced = m.sem("ro_reduced")
    sines = m.sem("ro_sines")
    with nc.Block() as block:
        @block.sync
        def _(sp):
            for t in range(4):
                sp.dma_start(pos[:, t:t + 1], m.dram["positions_2"][0, t * P:(t + 1) * P].unsqueeze(1)).then_inc(
                    loaded, 16)

        @block.vector
        def _(dve):
            step = m.dve_steps.on(dve)
            dve.wait_ge(loaded, 64)
            step(nc.vector.tensor_copy(posf[:], pos[:]))
            step(nc.vector.tensor_tensor(ang[:], spread(posf[:], 32),
                                         m.freqs.unsqueeze(1).to_broadcast([P, 4, 32]), ALU.mult))
            step(nc.vector.tensor_scalar(k[:], ang[:], 1.0 / TWO_PI, None, ALU.mult))
            step(nc.vector.tensor_scalar(k[:], k[:], ROUND, None, ALU.add))
            step(nc.vector.tensor_scalar(k[:], k[:], -ROUND, None, ALU.add))
            for part in (PI_A, PI_B, PI_C):
                step(nc.vector.scalar_tensor_tensor(out=ang[:], in0=k[:], scalar=-part, in1=ang[:],
                                                    op0=ALU.mult, op1=ALU.add))
            nc.vector.tensor_scalar(ang[:], ang[:], 3.1415925, -3.1415925, ALU.min, ALU.max).then_inc(reduced, 1)
            dve.wait_ge(sines, 1)
            step(nc.vector.tensor_tensor(turn[:, 0], turn[:, 0], turn[:, 0], ALU.mult))
            step(nc.vector.tensor_scalar(turn[:, 0], turn[:, 0], -2.0, 1.0, ALU.mult, ALU.add))

        @block.scalar
        def _(act):
            act.wait_ge(reduced, 1)
            nc.scalar.activation(turn[:, 0], ang[:], ACT.Sin, scale=0.5)
            nc.scalar.activation(turn[:, 1], ang[:], ACT.Sin).then_inc(sines, 1)


def finish_stage(m, name, nope, pe_part, gpe, gain, factor, turn, nope_t, pe_t, at, x_at, padded=False):
    nc, ps = m.nc, m.ps
    junk = m.area(f"{name}_junk", [P, BH, NOPE], at)
    x = m.at(f"{name}_pe", [P, 2, BH, ROPE], x_at)
    w = m.area(f"{name}_work", [P, BH, ROPE], at + 4096)
    ss = m.area(f"{name}_ss", [P, 4, 4, BH], at + 6144)
    cleared = m.sem(f"{name}_cleared")
    squared = m.sem(f"{name}_squared")
    root = m.sem(f"{name}_root")
    ready = m.sem(f"{name}_ready")
    turned = m.sem(f"{name}_turned")
    taken = m.sem(f"{name}_taken")

    with nc.Block() as block:
        @block.vector
        def _(dve):
            step = m.dve_steps.on(dve)
            tt, ts = nc.vector.tensor_tensor, nc.vector.tensor_scalar
            if padded:
                nc.vector.memset(pe_t[:], 0.0).then_inc(cleared, 1)
            for t in range(4):
                step(tt(junk[:], nope(t), nope(t), ALU.mult))
                step(nc.vector.tensor_reduce(ss[:, 0, t, :], junk[:], AX.X, ALU.add))
                step(tt(w[:], pe_part(t), pe_part(t), ALU.mult))
                step(nc.vector.tensor_reduce(ss[:, 3, t, :], w[:], AX.X, ALU.add))
            step(tt(ss[:, 0], ss[:, 0], ss[:, 3], ALU.add))
            ts(ss[:, 0], ss[:, 0], 1.0 / QKH, None, ALU.mult).then_inc(squared, 1)
            dve.wait_ge(root, 1)
            step(nc.vector.reciprocal(ss[:, 2], ss[:, 1]))
            step(ts(ss[:, 2], ss[:, 2], factor, None, ALU.mult))
            for t in range(4):
                r = ss[:, 2, t, :]
                if t >= 2:
                    dve.wait_ge(turned, t - 1)
                step(tt(nope(t), nope(t), spread(r, NOPE), ALU.mult))
                g = gpe.unsqueeze(1).to_broadcast([P, BH, ROPE])
                c = turn[:, 0, t, :].unsqueeze(1).to_broadcast([P, BH, 32])
                s = turn[:, 1, t, :].unsqueeze(1).to_broadcast([P, BH, 32])
                o = x[:, t % 2]
                step(tt(w[:], pe_part(t), g, ALU.mult))
                step(tt(w[:], w[:], spread(r, ROPE), ALU.mult))
                j = junk[:, :, 0:32]
                step(tt(j, w[:, :, 32:64], s, ALU.mult))
                step(tt(o[:, :, 0:32], w[:, :, 0:32], c, ALU.mult))
                step(tt(o[:, :, 0:32], o[:, :, 0:32], j, ALU.subtract))
                step(tt(j, w[:, :, 0:32], s, ALU.mult))
                step(tt(o[:, :, 32:64], w[:, :, 32:64], c, ALU.mult))
                tt(o[:, :, 32:64], o[:, :, 32:64], j, ALU.add).then_inc(ready, 1)
                dve.wait_ge(ready, t + 1)

        @block.scalar
        def _(act):
            act.wait_ge(squared, 1)
            nc.scalar.activation(ss[:, 1], ss[:, 0], ACT.Sqrt, bias=m.eps[:, 0:1]).then_inc(root, 1)
            for t in range(4):
                c = slice(t * P, (t + 1) * P)
                b = 4 * (t % 2)
                act.wait_ge(turned, t + 1)
                for half in range(2):
                    nc.scalar.activation(nope_t[:, 4 * half:4 * half + 4, c],
                                         ps[:, b + half, :].rearrange("p (k c) -> p k c", k=4), ACT.Copy,
                                         scale=m.col(gain))
                stacked = ps[:, b + 2, :].rearrange("p (k c) -> p k c", k=4)
                if padded:
                    if t == 0:
                        act.wait_ge(cleared, 1)
                    for i in range(2):
                        r = slice(64 * i, 64 * i + 64)
                        ins = nc.scalar.activation(pe_t[r, i:BH:2, c], stacked[r], ACT.Copy)
                else:
                    ins = nc.scalar.activation(pe_t[:, :, c], stacked, ACT.Copy)
                ins.then_inc(taken, 1)

        @block.tensor
        def _(pe):
            for t in range(4):
                b = 4 * (t % 2)
                pe.wait_ge(ready, t + 1)
                if t >= 2:
                    pe.wait_ge(taken, t - 1)
                for h in range(BH):
                    pe.transpose(ps[:, b + h // 4, (h % 4) * P:(h % 4 + 1) * P], nope(t)[:, h, :], m.ident)
                for h in range(BH // 2):
                    ins = pe.transpose(ps[:, b + 2, h * P:(h + 1) * P],
                                       x[:, t % 2, 2 * h:2 * h + 2, :].rearrange("p a b -> p (a b)"), m.ident)
                ins.then_inc(turned, 1)


def two_blocks(nc, dram):
    with ExitStack() as ctx:
        ctx.enter_context(nc.allow_non_contiguous_dma("short rows of gains and gate weights"))
        m = Machine(nc, ctx, dram)
        m.gates = m.keep("gates", [CAP, NE])
        m.rows = m.keep("rows", [CAP, NE], U32)
        m.arena = m.keep_end
        m.xhat = nc.dram_tensor("xhat_scratch", [L1, D], F32, kind="Internal").ap()
        m.resid = nc.dram_tensor("resid_scratch", [L1, D], F32, kind="Internal").ap()

        def columns(w, widths, start=0):
            k = w.shape[0] // P
            for c in widths:
                m.blocks.append((w[:, start:start + c], k, c))
                start += c

        columns(dram["w_in"][0], [512] * 6)
        columns(dram["w_out"][0], [512] * 2)
        for l in range(2):
            columns(dram["mem_w_kv_2"][l], [512] * 2)
        for _, _, start, width in MLSTM_IN:
            columns(dram["a_w_in_2"][0], [width], start)
        columns(dram["a_w_out_2"][0], [512] * 2)
        columns(dram["w_kv_a_2"], [KVL + ROPE])
        columns(dram["w_kv_b_2"], [512] * 4)
        columns(dram["b_w_in_2"][0], [QL] + [512] * 4)
        columns(dram["b_w_q_up_2"][0], [512] * 3)
        columns(dram["b_w_out_2"][0], [512] * 2)

        def rows(name, n, flat=None):
            a = dram[name] if flat is None else flat
            return a.rearrange("(k p) -> k p", p=P)

        names = [
            ("mix_g", rows(None, 8, dram["mix_norm_g"][0])),
            ("conv_w", dram["conv_w"][0].rearrange("j (k p) -> (j k) p", p=P)),
            ("subln", rows(None, 1, dram["attn_subln_g"][0])),
            ("ffn_g", rows(None, 8, dram["ffn_norm_g"][0])),
            ("a_norm", rows(None, 8, dram["a_norm_2"][0])),
            ("a_conv_b", rows(None, 16, dram["a_conv_b_2"][0])),
            ("a_h_norm", rows(None, 8, dram["a_h_norm_2"][0])),
            ("b_norm", rows(None, 8, dram["b_norm_2"][0])),
            ("q_lat", rows(None, 3, dram["b_q_lat_norm_2"][0])),
            ("kv_norm", rows(None, 8, dram["kv_norm_2"])),
            ("kv_lat", rows(None, 2, dram["kv_lat_norm_2"])),
            ("q_nope", rows(None, 1, dram["b_q_gain_2"][0, 0:NOPE])),
            ("k_nope", rows(None, 1, dram["k_gain_2"][0:NOPE])),
            ("mem_norm", rows(None, 8, dram["mem_norm_2"])),
            ("mem_q", dram["mem_q_gain_2"]),
            ("mem_k", dram["mem_k_gain_2"]),
            ("a_conv_w", dram["a_conv_w_2"][0].rearrange("j (k p) -> (j k) p", p=P)),
        ]

        feat = 4 * KD * L1
        h = m.area("h", [P, len(TILES1), D], 0)
        hn = m.area("hn1", [P, KD, L1], 20480)
        qk = m.area("qk1", [P, KD, L1], 20480 + feat)
        v = m.area("v1", [P, len(TILES1), AH * AV], 20480 + 2 * feat)
        at = 20480 + 2 * feat + 10240
        raw = m.area("raw1", [P, 12, L1], at)
        turns = m.area("turns1", [P, 2, L1], at + 48 * L1)
        work = at + 56 * L1
        setup_stage(m, h, turns, work, names)
        m.close()
        norm_stage(m, "n1", h, TILES1, [(hn, "mix_g")], m.arena + work)
        m.close()
        rot_work = m.area("rot_work", [P, 2, L1], work)
        projection_stage(m, hn, qk, v, raw, turns, rot_work)
        m.close()
        diff_attention_stage(m, qk, v, raw, hn, at + 48 * L1)
        m.close()
        spare = [m.arena + 20480 + feat + 8320 * i for i in range(3)]
        out_stage(m, "out1", hn, h, TILES1, spare, ahead=0)
        m.close()

        def store_tokens(sp, normed, ready, stored):
            for t, (t0, n) in enumerate(TILES1):
                sp.dma_start(m.resid[t0:t0 + n, :], h[0:n, t, :]).then_inc(m.resid_stored, 16)
            for t, (t0, n) in enumerate(TILES1):
                sp.wait_ge(ready, t + 1)
                sp.dma_start(m.xhat[t0:t0 + n, :], normed[0:n, t % 2, :]).then_inc(stored[t % 2], 16)
            sp.wait_ge(m.resid_stored, 16 * len(TILES1))
            for i in range(2):
                sp.wait_ge(stored[i], 16 * len(range(i, len(TILES1), 2)))

        m.resid_stored = m.sem("resid_stored")
        norm_stage(m, "n2", h, TILES1, [(hn, "ffn_g")], m.arena + work, tail=store_tokens)
        m.close()
        router_stage(m, hn, work)
        m.close()
        experts_stage(m, 0)
        m.close()

        x = m.area("x", [P, 4, D], 0)
        mk = [m.area(f"mk{l}", [P, MEMH, MEM], 16384 + 8192 * l) for l in range(2)]
        mv = [m.area(f"mv{l}", [P, 2, 512], 16384 + 8192 * l + 4096) for l in range(2)]
        final_norm_stage(m, x, 32768)
        m.close()
        mem_x = m.area("mem_x", [P, 2, D], 32768)
        mem_t = m.area("mem_t", [P, KD, MEM], 40960)
        mk_tok = [m.area(f"mk_tok{l}", [P, 2, 512], 49152 + 4096 * l) for l in range(2)]
        mem_load_stage(m, mem_x)
        m.close()
        norm_stage(m, "nm", mem_x, TILES2[:2], [(mem_t, "mem_norm")], m.arena + 57344)
        m.close()
        memory_stage(m, mem_t, mk_tok, mv, [m.arena + 57344 + 8192 * i for i in range(3)])
        m.close()

        hn = m.low("hn2", [P, KD, SEQ], 0)
        qk = m.low("qk2", [P, 16, SEQ], 16384)
        v = m.area("v2", [P, 4, MW], 32768)
        y = m.area("y2", [P, 12, SEQ], 49152)
        mq = m.area("mq2", [P, 4, MEMH * MEMD], 73728)
        work = 81920
        gates = m.area("ml_gates", [P, 4, 2 * MH], 106496)
        mqt = m.low("mqt2", [P, MEMH, SEQ], 16384)
        by_head = lambda t: t.rearrange("p t (g w) -> p t g w", g=MEMH)
        group_norm_stage(m, "gm", [dict(src=by_head(mk_tok[l][:]), dst=mk[l], gain=("mem_k", l), factor=1.0)
                                   for l in range(2)], work)
        m.close()
        norm_stage(m, "n3", x, TILES2, [(hn, "a_norm")], m.arena + work)
        m.close()
        mlstm_in_stage(m, hn, qk, v, y, mq, gates, work)
        m.close()
        ht = m.low("ht", [P, 4, MW], 0)
        mlstm_stage(m, qk, v, gates, ht, y, work)
        m.close()
        group_norm_stage(m, "gq1", [dict(src=by_head(mq[:]), dst=mqt, gain=("mem_q", 0),
                                         factor=MEMD ** -0.5)], work)
        m.close()
        attention_stage(m, "ma1", memory_units(mqt, mk[0], mv[0], y), work)
        m.close()
        work_slots = [m.arena + 81920 + 8192 * i for i in range(3)]
        out_stage(m, "out2", y, x, TILES2, work_slots)
        m.close()

        hb = m.low("hb", [P, KD, SEQ], 0)
        hkv = m.low("hkv", [P, KD, SEQ], 16384)
        qt = m.low("qt3", [P, BH, SEQ], 16384)
        kt = m.low("kt3", [P, BH, SEQ], 32768)
        v = m.area("v3", [P, 4, BH, NOPE], 32768)
        y = m.area("y3", [P, 12, SEQ], 49152)
        kn = m.area("kn", [P, 4, BH, NOPE], 49152)
        lat = m.area("lat", [P, 4, KVL + ROPE], 65536)
        kpt = m.area("kpt", [P, BH // 2, SEQ], 73728)
        qpt = m.area("qpt", [P, BH, SEQ], 81920)
        mq = m.area("mq3", [P, 4, MEMH * MEMD], 90112)
        latt = m.area("latt", [P, KVL // P, SEQ], 81920)
        turn = m.area("turn3", [P, 2, 4, 32], 106496)
        norm_stage(m, "n4", x, TILES2, [(hb, "b_norm"), (hkv, "kv_norm")], m.arena + 49152)
        m.close()

        def copies(*dsts):
            act = m.nc.scalar
            return [lambda step, u, psum, f=f: f(act, u, psum) for f in dsts]

        def job(kind, src, take):
            return dict(kind=kind, act=src, tiles=TILES2, engine="act", take=take)

        take_lat, = copies(lambda act, u, ps: act.activation(lat[:, u, :], ps, ACT.Copy))
        copy_stage(m, "kva", [job("tokens", hkv, take_lat)])
        m.close()
        one_group = lambda t: t.unsqueeze(2)
        group_norm_stage(m, "gkv", [dict(src=one_group(lat[:, :, 0:KVL]), dst=latt, gain=("kv_lat", 0),
                                         factor=1.0)], 90112)
        m.close()
        rotary_stage(m, turn, 90112)
        m.close()

        def take_kv(c):
            def f(step, u, psum):
                act = m.nc.scalar
                pair = psum.rearrange("p (h w) -> p h w", h=2)
                act.activation(kn[:, u, 2 * c:2 * c + 2, :], pair[:, :, 0:NOPE], ACT.Copy)
                return act.activation(v[:, u, 2 * c:2 * c + 2, :], pair[:, :, NOPE:], ACT.Copy)
            return f

        SplitGemm(m, "kvb", [job("tokens", latt, take_kv(c)) for c in range(4)],
                  [m.arena + at for at in (73728, 90112, 98304)]).stage()
        m.close()
        finish_stage(m, "fk", lambda t: kn[:, t],
                     lambda t: lat[:, t, KVL:].unsqueeze(1).to_broadcast([P, BH, ROPE]), m.gpe[:, 1, :],
                     "k_nope", 1.0, turn, kt, kpt, 90112, m.arena + 98304)
        m.close()

        qlat = m.area("qlat", [P, 4, QL], 81920)
        take_ql, take_mq = copies(lambda act, u, ps: act.activation(qlat[:, u, :], ps, ACT.Copy),
                                  lambda act, u, ps: act.activation(mq[:, u, :], ps, ACT.Copy))
        take_z = copies(*[lambda act, u, ps, c=c: act.activation(y[:, c + u, :], ps, ACT.Silu)
                          for c in (0, 4, 8)])
        SplitGemm(m, "in3", [job("tokens", hb, take_ql), job("features", hb, take_z[0]),
                             job("features", hb, take_z[1]), job("tokens", hb, take_mq),
                             job("features", hb, take_z[2])], m.gaps + [m.arena + 98304]).stage()
        m.close()
        qlt = m.low("qlt", [P, QL // P, SEQ], 16384)
        mqt = m.low("mqt3", [P, MEMH, SEQ], 16384 + 6144)
        group_norm_stage(m, "gq2", [dict(src=one_group(qlat[:]), dst=qlt, gain=("q_lat", 0), factor=1.0),
                                    dict(src=by_head(mq[:]), dst=mqt, gain=("mem_q", 1),
                                         factor=MEMD ** -0.5)], 98304)
        m.close()
        attention_stage(m, "ma2", memory_units(mqt, mk[1], mv[1], y), 90112)
        m.close()
        q_low = m.area("q_low", [P, 2, BH, QKH], 16384)
        q_high = m.low("q_high", [P, 2, BH, QKH], 0)
        q_of = lambda t: (q_low if t < 2 else q_high)[:, t % 2]

        def take_q(c):
            def f(step, u, psum):
                flat = q_of(u).rearrange("p h w -> p (h w)")
                return m.nc.scalar.activation(flat[:, 512 * c:512 * (c + 1)], psum, ACT.Copy)
            return f

        SplitGemm(m, "qup", [job("tokens", qlt, take_q(c)) for c in range(3)], work_slots).stage()
        m.close()
        finish_stage(m, "fq", lambda t: q_of(t)[:, :, 0:NOPE], lambda t: q_of(t)[:, :, NOPE:], m.gpe[:, 0, :],
                     "q_nope", QKH ** -0.5, turn, qt, qpt, 98304, m.low_ring + 12288, padded=True)
        m.close()
        units = []
        for hd in range(BH):
            for t in range(4):
                c, w = slice(t * P, (t + 1) * P), (t + 1) * P
                units.append(dict(scores=[(qt[:, hd, c], kt[:, hd, 0:w]), (qpt[:, hd, c], kpt[:, hd // 2, 0:w])],
                                  width=w, mask=m.chunk, values=[v[:, s, hd, :] for s in range(t + 1)],
                                  y=y[:, hd, c]))
        attention_stage(m, "ba", units, 16384)
        m.close()
        out_stage(m, "out3", y, x, TILES2, work_slots, ahead=0)
        m.close()
        result_stage(m, x)
        m.close()


def mem_load_stage(m, mem_x):
    loaded = m.sem("mem_loaded")
    with m.nc.Block() as block:
        @block.sync
        def _(sp):
            sp.dma_start(mem_x[:], m.dram["mem_2"][0].rearrange("(t p) d -> p t d", p=P)).then_inc(loaded, 16)
            sp.wait_ge(loaded, 16)


def result_stage(m, x):
    stored = m.sem("result_stored")
    with m.nc.Block() as block:
        @block.sync
        def _(sp):
            sp.dma_start(m.dram["out"][0].rearrange("(t p) d -> p t d", p=P), x[:]).then_inc(stored, 16)
            sp.wait_ge(stored, 16)


INPUTS = ["x", "meta_tokens", "mix_norm_g", "w_in", "conv_w", "lambda_q1", "lambda_k1", "lambda_q2", "lambda_k2",
          "attn_subln_g", "w_out", "ffn_norm_g", "w_router", "w_gate", "w_up", "w_down", "final_norm_g", "mem_2",
          "positions_2", "a_norm_2", "a_w_in_2", "a_conv_w_2", "a_conv_b_2", "a_ig_bias_2", "a_fg_bias_2",
          "a_h_norm_2", "a_w_out_2", "b_norm_2", "b_w_in_2", "b_q_lat_norm_2", "b_w_q_up_2", "b_q_gain_2",
          "b_w_out_2", "kv_norm_2", "w_kv_a_2", "kv_lat_norm_2", "w_kv_b_2", "k_gain_2", "mem_norm_2",
          "mem_w_kv_2", "mem_q_gain_2", "mem_k_gain_2"]


def kernel(**inputs):
    import numpy as _np
    import concourse.bacc as _bacc
    from concourse import mybir as _mybir
    from concourse.bass_utils import run_bass_kernel_spmd as _run

    nc = _bacc.Bacc("TRN2", target_bir_lowering=False, num_devices=1)
    arrays, dram = {}, {}
    masks, turns = fixed_tables()
    given = {name: _np.ascontiguousarray(inputs[name]) for name in INPUTS}
    given["masks"], given["turns"] = masks, turns
    for name, a in given.items():
        arrays[f"in_{name}"] = a
        dram[name] = nc.dram_tensor(f"in_{name}", a.shape, _mybir.dt.from_np(a.dtype), kind="ExternalInput").ap()
    dram["out"] = nc.dram_tensor("out_0", (1, SEQ, D), _mybir.dt.float32, kind="ExternalOutput").ap()
    two_blocks(nc, dram)
    r = _run(nc, [arrays], core_ids=[0])
    return r.results[0]["out_0"]
```

```python
from contextlib import ExitStack

import numpy as np
import concourse.bass as bass
from concourse import mybir

F32 = mybir.dt.float32
F32R = mybir.dt.float32r
U32 = mybir.dt.uint32
ALU = mybir.AluOpType
ACT = mybir.ActivationFunctionType
AX = mybir.AxisListType

P = 128
D = 1024
KD = D // P
META = 16
SEQ = 512
L1 = META + SEQ
TILES1 = [(i * P, min(P, L1 - i * P)) for i in range(-(-L1 // P))]
TILES2 = [(i * P, P) for i in range(SEQ // P)]
HALF1 = L1 // 2
EPS = 1e-6
LAM_INIT = 0.2
AH, AV = 4, 128
NE = 16
CAP = 2 * L1 // NE
FF = 2 * D
FH = FF // 2
ROUNDS = -(-CAP // 8)
MEM = 256
MH, MDH = 4, 256
MW = MH * MDH
MEMH, MEMD = 4, 128
BH = 8
NOPE, ROPE = 128, 64
QKH = NOPE + ROPE
QL, KVL = 384, 256
NEG = -1.0e30
SLOT = 2048
NSLOT = 12
NPIECE, NSPLIT = 6, 3
MLSTM_IN = [("gates", 0, 5120, 8), ("qk", 0, 0, 512), ("v", 0, 2048, 512), ("qk", 1, 512, 512), ("v", 1, 2560, 512),
            ("qk", 2, 1024, 512), ("o", 0, 3072, 512), ("qk", 3, 1536, 512), ("o", 1, 3584, 512),
            ("z", 0, 4096, 512), ("z", 1, 4608, 512), ("mq", 0, 5128, 512),
            ("mz", 0, 5640, 512)]
TWO_PI = 2.0 * np.pi
PI_A = 6.28125
PI_B = float(np.float32(np.round((TWO_PI - PI_A) * 2 ** 19) / 2 ** 19))
PI_C = float(np.float32(TWO_PI - PI_A - PI_B))
ROUND = 12582912.0


def fixed_tables():
    i = np.arange(P)
    ident = np.eye(P)
    rot = np.zeros((P, P))
    for m in range(P):
        if m % 64 < 32:
            rot[m + 32, m] = -1.0
        else:
            rot[m - 32, m] = 1.0
    upto = (i[:, None] <= i[None, :])
    ones = np.ones((P, P))
    after = (i[:, None] > i[None, :])
    causal = np.where(i[None, :] > i[:, None], NEG, 0.0)
    chunk = np.where(i[None, :] // 64 > i[:, None] // 64, NEG, 0.0)
    freq = (np.float32(10000.0) ** (-np.arange(0, 64, 2, dtype=np.float32) / np.float32(64))).astype(np.float32)
    freqs = np.broadcast_to(freq[None, :], (P, 32))
    masks = np.concatenate([ident, rot, upto, after, causal, chunk, ones, freqs], axis=1).astype(np.float32)
    ang = (np.arange(L1, dtype=np.float32)[:, None] * freq[None, :]).astype(np.float32)
    ang = np.concatenate([ang] * 4, axis=1).T
    turns = np.stack([np.cos(ang), np.sin(ang)], axis=1).astype(np.float32)
    return np.ascontiguousarray(masks), np.ascontiguousarray(turns)


class Steps:

    def __init__(self, sem):
        self.sem, self.count = sem, 0

    def on(self, engine):
        def step(ins):
            self.count += 1
            ins.then_inc(self.sem, 1)
            engine.wait_ge(self.sem, self.count)
        return step


class Machine:

    def __init__(self, nc, ctx, dram):
        self.nc, self.ctx, self.dram = nc, ctx, dram
        self.stage, self.stage_sems, self.cooling = 0, [], []
        self.ps = ctx.enter_context(nc.psum_tensor("ps", [P, 8, 512], F32))
        self.ring_at = 16640
        self.keep_at = self.ring_at + NSLOT * SLOT * 4
        self.keep_end = self.keep_at
        self.ring = self.at("ring", [P, NSLOT, SLOT], self.ring_at)
        self.low_ring = self.ring_at + 6 * SLOT * 4
        self.pieces = self.at("pieces", [P, NPIECE, SLOT], self.low_ring)
        self.high = self.at("pieces_high", [P, NSPLIT, SLOT], self.ring_at, F32R)
        self.low_part = self.at("pieces_low", [P, NSPLIT, SLOT], self.ring_at + NSPLIT * SLOT * 4, F32R)
        self.gaps = [self.ring_at + 3 * SLOT * 4 * i + 2 * SLOT * 4 for i in range(2)]
        self.masks = self.keep("masks", [P, 7 * P + 32])
        self.ident = self.masks[:, 0:P]
        self.rot = self.masks[:, P:2 * P]
        self.upto = self.masks[:, 2 * P:3 * P]
        self.after = self.masks[:, 3 * P:4 * P]
        self.causal = self.masks[:, 4 * P:5 * P]
        self.chunk = self.masks[:, 5 * P:6 * P]
        self.ones = self.masks[:, 6 * P:7 * P]
        self.freqs = self.masks[:, 7 * P:7 * P + 32]
        self.cols = self.keep("cols", [P, 2, P])
        self.eps = self.keep("eps", [P, 1])
        self.lam = self.keep("lam", [P, 1])
        self.gpe = self.keep("gpe", [P, 2, ROPE])
        self.gate_bias = self.keep("gate_bias", [P, 2 * MH])
        self.arena = self.keep_end
        self.dve_steps = Steps(self.lasting("dve_step"))
        self.act_steps = Steps(self.lasting("act_step"))
        self.pool_steps = Steps(self.lasting("pool_step"))
        self.block_loaded = [self.lasting("block_loaded0"), self.lasting("block_loaded1")]
        self.block_free = {}
        self.sent = 0
        self.taken = 0
        self.blocks = []
        self.experts_sent = 0
        self.expert_loaded = [self.lasting(f"expert_loaded{i}") for i in range(NPIECE)]

    def lasting(self, name):
        return self.ctx.enter_context(self.nc.semaphore(name))

    def sem(self, name):
        s = self.nc.alloc_semaphore(name)
        self.stage_sems.append(s)
        return s

    def close(self):
        for s in self.cooling:
            self.nc.release_semaphore(s)
        for s in self.stage_sems:
            self.nc.gpsimd.sem_clear(s)
        self.cooling, self.stage_sems = self.stage_sems, []
        self.stage += 1

    def at(self, name, shape, offset, dt=F32):
        return self.nc.alloc_sbuf_tensor_at(name, shape, dt, offset=offset)

    def keep(self, name, shape, dt=F32):
        t = self.at(name, shape, self.keep_end, dt)
        size = 4 * int(np.prod(shape[1:]))
        self.keep_end += -(-size // 32) * 32
        return t

    def area(self, name, shape, offset, dt=F32):
        assert self.arena + offset + 4 * int(np.prod(shape[1:])) <= 229344, name
        return self.at(name, shape, self.arena + offset, dt)

    def low(self, name, shape, offset):
        assert offset + 4 * int(np.prod(shape[1:])) <= 6 * SLOT * 4
        return self.at(name, shape, self.low_ring + offset)

    def col(self, name, k=0):
        n = self.col_of[name] + k
        return self.cols[:, n // P, n % P:n % P + 1]

    def colrange(self, name, k):
        n = self.col_of[name]
        assert n // P == (n + k - 1) // P, name
        return self.cols[:, n // P, n % P:n % P + k]

    def block_view(self, n):
        _, k, cols = self.blocks[n]
        flat = self.ring[:, 3 * (n % 2):3 * (n % 2) + 3, :].rearrange("p a b -> p (a b)")
        return flat[:, 0:k * cols].rearrange("p (k c) -> p k c", k=k)

    def send_blocks(self, sp, upto):
        while self.sent < min(upto, len(self.blocks)):
            n = self.sent
            src, k, cols = self.blocks[n]
            if n >= 2 and self.block_free[n - 2][0] == self.stage:
                sp.wait_ge(*self.block_free[n - 2][1:])
            sp.dma_start(self.block_view(n), src.rearrange("(k p) c -> p k c", p=P)).then_inc(
                self.block_loaded[n % 2], 16)
            self.sent += 1

    def expert_load(self, sp, j, e, slot):
        w_gate, w_up, w_down = self.dram["w_gate"], self.dram["w_up"], self.dram["w_down"]
        if j < 8 or 12 <= j < 20:
            half = 1 if j < 8 else 0
            i = j if j < 8 else j - 12
            w = w_up if i % 2 else w_gate
            src = w[0, e, 2 * P * (i // 2):2 * P * (i // 2 + 1), half * FH:(half + 1) * FH]
        else:
            half = 0 if j < 12 else 1
            i = j - 8 if j < 12 else j - 20
            src = w_down[0, e, half * FH + 2 * P * i:half * FH + 2 * P * (i + 1), :]
        if len(src.shape) == 3:
            src = src.rearrange("o (k p) c -> p (o k) c", p=P)
        else:
            src = src.rearrange("(k p) c -> p k c", p=P)
        sp.dma_start(self.pieces[:, slot, :].rearrange("p (k c) -> p k c", k=2), src).then_inc(
            self.expert_loaded[slot], 16)

    def send_experts(self, sp, upto):
        while self.experts_sent < upto:
            n = self.experts_sent
            self.expert_load(sp, 12 + n if n < 8 else n - 8, 0, n % NPIECE)
            self.experts_sent += 1

    def wait_block(self, pe, n):
        pe.wait_ge(self.block_loaded[n % 2], 16 * (n // 2 + 1))


def wait_counted(engine, sem, value, passed):
    engine.wait_ge(sem, value)
    engine.sem_inc(passed, 1)


def spread(ap, n):
    p, k = ap.shape
    return ap.unsqueeze(2).to_broadcast([p, k, n])


def rows_of(x, tiles, outs):
    return [(x[0:n, t, :], n, [(out[:, :, t0:t0 + n], gain) for out, gain in outs])
            for t, (t0, n) in enumerate(tiles)]


def norm_stage(m, name, items, temp, tail=None, buffers=2):
    nc, ps = m.nc, m.ps
    nt = len(items)
    normed = m.at(f"{name}_normed", [P, buffers, D], temp)
    junk = m.at(f"{name}_junk", [P, D], temp + 4 * buffers * D)
    act_junk = m.at(f"{name}_act_junk", [P, D], temp + 4 * D)
    ss = m.at(f"{name}_ss", [P, 3, nt], temp + 4 * (buffers + 1) * D)
    cleared = m.sem(f"{name}_cleared")
    squared = m.sem(f"{name}_squared")
    act_squared = m.sem(f"{name}_act_squared")
    root_ready = m.sem(f"{name}_root")
    inverse_ready = m.sem(f"{name}_inverse")
    normed_ready = m.sem(f"{name}_normed")
    turned = m.sem(f"{name}_turned")
    evicted = m.sem(f"{name}_evicted")
    stored = [m.sem(f"{name}_stored{i}") for i in range(buffers)] if tail else None

    with nc.Block() as block:
        if tail:
            @block.sync
            def _(sp):
                tail(sp, normed, normed_ready, stored)

        @block.vector
        def _(dve):
            nc.vector.memset(ss[:], 1.0).then_inc(cleared, 1)
            dve.wait_ge(cleared, 1)
            for i, t in enumerate(range(0, nt, 2)):
                rows, n, _ = items[t]
                nc.vector.tensor_tensor_reduce(
                    out=junk[0:n, :], in0=rows, in1=rows, scale=1.0 / D, scalar=0.0,
                    op0=ALU.mult, op1=ALU.add, accum_out=ss[0:n, 0, t:t + 1]).then_inc(squared, 1)
                dve.wait_ge(squared, i + 1)
            dve.wait_ge(root_ready, 1)
            nc.vector.reciprocal(ss[:, 2, :], ss[:, 1, :]).then_inc(inverse_ready, 1)
            u = 0
            for rows, n, outs in items:
                for half in range(2):
                    dve.wait_ge(turned, u + 1)
                    bank = ps[:, u % 8, :].rearrange("p (k c) -> p k c", k=4)[:, :, 0:n]
                    for out, gain in outs:
                        g = spread(m.colrange(gain, KD)[:, 4 * half:4 * half + 4], n)
                        ins = nc.vector.tensor_tensor(out[:, 4 * half:4 * half + 4, :], bank, g, ALU.mult)
                    ins.then_inc(evicted, 1)
                    u += 1

        @block.scalar
        def _(act):
            act.wait_ge(cleared, 1)
            for i, t in enumerate(range(1, nt, 2)):
                rows, n, _ = items[t]
                nc.scalar.activation(act_junk[0:n, :], rows, ACT.Square, scale=D ** -0.5,
                                     accum_out=ss[0:n, 0, t:t + 1]).then_inc(act_squared, 1)
                act.wait_ge(act_squared, i + 1)
            act.wait_ge(squared, -(-nt // 2))
            nc.scalar.activation(ss[:, 1, :], ss[:, 0, :], ACT.Sqrt, bias=m.eps[:, 0:1]).then_inc(root_ready, 1)
            act.wait_ge(inverse_ready, 1)
            for t, (rows, n, _) in enumerate(items):
                if t >= buffers:
                    act.wait_ge(turned, 2 * (t - buffers + 1))
                    if stored is not None:
                        act.wait_ge(stored[t % buffers], 16 * (t // buffers))
                nc.scalar.activation(normed[0:n, t % buffers, :], rows, ACT.Copy,
                                     scale=ss[0:n, 2, t:t + 1]).then_inc(normed_ready, 1)

        @block.tensor
        def _(pe):
            u = 0
            for t, (_, n, _) in enumerate(items):
                pe.wait_ge(normed_ready, t + 1)
                for half in range(2):
                    if u >= 8:
                        pe.wait_ge(evicted, u - 7)
                    for k in range(4):
                        f = 4 * half + k
                        ins = pe.transpose(ps[:, u % 8, k * P:k * P + n],
                                           normed[0:n, t % buffers, f * P:(f + 1) * P], m.ident[0:n, 0:n])
                    ins.then_inc(turned, 1)
                    u += 1


class Gemm:

    def __init__(self, m, name, jobs, pairs=4):
        self.m, self.name, self.jobs, self.pairs = m, name, jobs, pairs
        self.first = m.taken
        self.ready = m.sem(f"{name}_ready")
        self.out = {"act": m.sem(f"{name}_act_took"), "dve": m.sem(f"{name}_dve_took")}
        self.units = []
        count = {"act": 0, "dve": 0}
        for j, job in enumerate(jobs):
            _, k, cols = m.blocks[self.first + j]
            tiles = job["tiles"]
            n_units = cols // P if job["kind"] == "features" else len(tiles)
            for u in range(n_units):
                count[job["engine"]] += 1
                self.units.append((j, u, job["engine"], count[job["engine"]]))
            m.block_free[self.first + j] = (m.stage, self.ready, len(self.units))
        m.taken += len(jobs)

    def psum(self, n):
        j, u, _, _ = self.units[n]
        job = self.jobs[j]
        pair = 2 * (n % self.pairs)
        ps = self.m.ps
        if job["kind"] == "features":
            tokens = job["act"].shape[2]
            if tokens > 512:
                return ps[:, pair:pair + 2, 0:tokens // 2]
            return ps[:, pair, 0:tokens]
        cols = self.m.blocks[self.first + j][2]
        rows = job["tiles"][u][1]
        return ps[0:rows, pair, 0:cols]

    def products(self, pe, after=None):
        m = self.m
        for n, (j, u, _, _) in enumerate(self.units):
            job = self.jobs[j]
            w = m.block_view(self.first + j)
            k_tiles, cols = m.blocks[self.first + j][1:]
            if u == 0:
                m.wait_block(pe, self.first + j)
                if "needs" in job:
                    pe.wait_ge(*job["needs"])
            if n >= self.pairs:
                _, _, engine, count = self.units[n - self.pairs]
                pe.wait_ge(self.out[engine], count)
            act = job["act"]
            out = self.psum(n)
            if job["kind"] == "features":
                tokens = act.shape[2]
                halves = [(0, tokens)] if tokens <= 512 else [(0, tokens // 2), (tokens // 2, tokens)]
                for h, (a, b) in enumerate(halves):
                    to = out if len(halves) == 1 else out[:, h, :]
                    for k in range(k_tiles):
                        ins = pe.matmul(to, w[:, k, u * P:(u + 1) * P], act[:, k, a:b],
                                        start=(k == 0), stop=(k == k_tiles - 1))
            else:
                t0, rows = job["tiles"][u]
                for k in range(k_tiles):
                    ins = pe.matmul(out, act[:, k, t0:t0 + rows], w[:, k, :],
                                    start=(k == 0), stop=(k == k_tiles - 1))
            ins.then_inc(self.ready, 1)
            if after:
                after(pe, n)

    def take(self, which, engine, step):
        for n, (j, u, name, count) in enumerate(self.units):
            if name != which:
                continue
            engine.wait_ge(self.ready, n + 1)
            ins = self.jobs[j]["take"](step, u, self.psum(n))
            if ins is None:
                engine.sem_inc(self.out[which], 1)
            else:
                ins.then_inc(self.out[which], 1)

    def send(self, sp, ahead=2):
        self.m.send_blocks(sp, self.first + len(self.jobs) + ahead)


class Unit:

    def __init__(self, job, u, engine, bank):
        self.job, self.u, self.engine, self.bank = job, u, engine, bank
        self.count = self.done = self.place = self.before = None


class SplitGemm:

    def __init__(self, m, name, jobs, slots, banks=8, rest_tokens=None, pool_lows=False):
        self.m, self.name, self.jobs, self.banks = m, name, jobs, banks
        self.n_lows = 1 if pool_lows else 2
        if pool_lows:
            self.pool_low = m.sem(f"{name}_pool_low")
        self.first, self.ns = m.taken, len(slots)
        tokens = max(self.tokens(job) for job in jobs)
        self.w_split = [m.at(f"{name}_w{i}", [P, 2, 512], at, F32R) for i, at in enumerate(slots)]
        self.a_split = [m.at(f"{name}_a{i}", [P, 2, tokens], at + 4096, F32R) for i, at in enumerate(slots)]
        self.high = m.sem(f"{name}_high")
        self.low = m.sem(f"{name}_low")
        self.used = m.sem(f"{name}_used")
        self.ready = m.sem(f"{name}_ready")
        self.out = {"act": m.sem(f"{name}_act_took"), "dve": m.sem(f"{name}_dve_took")}
        self.rest_tokens = rest_tokens
        if rest_tokens is not None:
            self.rest_ready, self.rest_copied = m.sem(f"{name}_rest_ready"), m.sem(f"{name}_rest_copied")
        self.rests = []
        self.steps, self.units, self.first_unit = [], [], []
        count, n_ready, ring, last_in = {"act": 0, "dve": 0}, 0, 0, {}
        for j, job in enumerate(jobs):
            _, k, cols = m.blocks[self.first + j]
            n_units = self.main_units(j)
            self.first_unit.append(len(self.units))
            s0 = len(self.steps)
            self.steps += [(j, i) for i in range(k)]
            early = 2 if job.get("early") else 1
            new = [Unit(j, u, job["engine"], (ring + u) % banks) for u in range(n_units)]
            ring += n_units
            if job.get("rest") and job["kind"] == "tokens":
                new.append(Unit(j, n_units, job["engine"], banks))
                n_ready += 1
                new[-1].done = (self.ready, n_ready)
            for unit in new:
                count[unit.engine] += 1
                unit.count = count[unit.engine]
                unit.before = last_in.get(unit.bank)
                last_in[unit.bank] = unit
                assert unit.before is None or unit.before.place <= s0 + self.ns - 1, name
                if unit.done is None and unit is new[n_units - 1]:
                    unit.done = (self.used, len(self.steps))
                elif unit.done is None:
                    n_ready += 1
                    unit.done = (self.ready, n_ready)
                unit.place = len(self.steps) + self.ns - early + job.get("spread", 0) * unit.u
                if self.units:
                    unit.place = max(unit.place, self.units[-1].place)
                self.units.append(unit)
            if job.get("rest") and job["kind"] == "features":
                last_in[banks] = new[-1]
                self.rests.append(s0)
            m.block_free[self.first + j] = (m.stage, self.low,
                                               self.n_lows * (len(self.steps) - 1) + 1)
        m.taken += len(jobs)

    @staticmethod
    def tokens(job):
        return 512 if job.get("rest") else job["act"].shape[2]

    def main_units(self, j):
        job = self.jobs[j]
        if job["kind"] == "features":
            return -(-self.m.blocks[self.first + j][2] // P)
        return len(job["tiles"]) - (1 if job.get("rest") else 0)

    def psum(self, unit):
        bank = self.m.ps[:, unit.bank, :]
        job = self.jobs[unit.job]
        if job["kind"] == "features":
            return bank[0:min(P, self.m.blocks[self.first + unit.job][2]), 0:self.tokens(job)]
        return bank[0:job["tiles"][unit.u][1], 0:self.m.blocks[self.first + unit.job][2]]

    def rest_psum(self, u):
        return self.m.ps[:, self.banks, META * u:META * (u + 1)]

    def wait_bank(self, pe, unit):
        if unit.before is not None:
            pe.wait_ge(self.out[unit.before.engine], unit.before.count)

    def float_products(self, pe, to, lhs, rhs, k_tiles):
        for k in range(k_tiles):
            ins = pe.matmul(to, lhs(k), rhs(k), start=(k == 0), stop=(k == k_tiles - 1))
        return ins

    def rest(self, pe, j):
        job, w = self.jobs[j], self.m.block_view(self.first + j)
        act, k_tiles = job["act"], self.m.blocks[self.first + j][1]
        n_units = self.main_units(j)
        if job["kind"] == "tokens":
            unit = self.units[self.first_unit[j] + n_units]
            self.wait_bank(pe, unit)
            self.float_products(pe, self.psum(unit), lambda k: act[:, k, 512:], lambda k: w[:, k, :],
                                k_tiles).then_inc(self.ready, 1)
            return
        if j:
            before = self.units[self.first_unit[j] - 1]
            pe.wait_ge(self.out[before.engine], before.count)
        self.float_products(pe, self.m.ps[0:META, self.banks, :], lambda k: act[:, k, 512:],
                            lambda k: w[:, k, :], k_tiles).then_inc(self.rest_ready, 1)

    def turn_rest(self, pe, n):
        pe.wait_ge(self.rest_copied, n + 1)
        for u in range(4):
            pe.transpose(self.rest_psum(u), self.rest_tokens[:, u * P:(u + 1) * P],
                         self.m.ident[0:META, 0:META])

    def products(self, pe, after=None):
        m, s = self.m, 0
        for j, job in enumerate(self.jobs):
            k_tiles, cols = m.blocks[self.first + j][1:]
            n_units = self.main_units(j)
            for k in range(k_tiles):
                w, a = self.w_split[s % self.ns], self.a_split[s % self.ns]
                pe.wait_ge(self.low, self.n_lows * (s + 1))
                if self.n_lows == 1:
                    pe.wait_ge(self.pool_low, s + 1)
                for u in range(n_units):
                    unit = self.units[self.first_unit[j] + u]
                    if k == 0:
                        self.wait_bank(pe, unit)
                    for i, (x, y) in enumerate(((0, 0), (0, 1), (1, 0))):
                        if job["kind"] == "features":
                            lhs, rhs = w[:, x, u * P:min((u + 1) * P, cols)], a[:, y, 0:self.tokens(job)]
                        else:
                            t0, rows = job["tiles"][u]
                            lhs, rhs = a[:, x, t0:t0 + rows], w[:, y, 0:cols]
                        ins = pe.matmul(self.psum(unit), lhs, rhs, start=(k == 0 and i == 0),
                                        stop=(k == k_tiles - 1 and i == 2))
                    if k == k_tiles - 1 and u < n_units - 1:
                        ins.then_inc(self.ready, 1)
                ins.then_inc(self.used, 1)
                if k == 1 and job.get("rest"):
                    self.rest(pe, j)
                if s - self.ns - 2 in self.rests:
                    self.turn_rest(pe, self.rests.index(s - self.ns - 2))
                for work in (after or {}).get(s, []):
                    work()
                s += 1

    def operands(self, s):
        j, k = self.steps[s]
        cols = self.m.blocks[self.first + j][2]
        act = self.jobs[j]["act"]
        tokens = self.tokens(self.jobs[j])
        return ((self.m.block_view(self.first + j)[:, k, :], self.w_split[s % self.ns][:, :, 0:cols]),
                (act[:, k, 0:tokens], self.a_split[s % self.ns][:, :, 0:tokens]))

    def highs(self, act, s):
        j, k = self.steps[s]
        if k == 0:
            self.m.wait_block(act, self.first + j)
        if s >= self.ns:
            act.wait_ge(self.used, s - self.ns + 1)
        for x, parts in self.operands(s):
            self.m.nc.scalar.activation(parts[:, 0, :], x, ACT.Copy).then_inc(self.high, 1)

    def lows(self, dve, s):
        for i, (x, parts) in enumerate(self.operands(s)[0:self.n_lows]):
            dve.wait_ge(self.high, 2 * s + i + 1)
            self.m.nc.vector.tensor_tensor(parts[:, 1, :], x, parts[:, 0, :].bitcast(F32),
                                           ALU.subtract).then_inc(self.low, 1)

    def pool_split(self, pool):
        for s in range(len(self.steps)):
            x, parts = self.operands(s)[1]
            pool.wait_ge(self.high, 2 * s + 2)
            self.m.nc.gpsimd.tensor_tensor(parts[:, 1, :], x, parts[:, 0, :].bitcast(F32),
                                           ALU.subtract).then_inc(self.pool_low, 1)
            pool.wait_ge(self.pool_low, s + 1)

    def take(self, engine, unit):
        engine.wait_ge(*unit.done)
        ins = self.jobs[unit.job]["take"](None, unit.u, self.psum(unit))
        if ins is None:
            engine.sem_inc(self.out[unit.engine], 1)
        else:
            ins.then_inc(self.out[unit.engine], 1)

    def split(self, which, engine, after=None):
        last = max(len(self.steps) - 1, self.units[-1].place, max(after) if after else 0)
        for s in range(last + 1):
            if s < len(self.steps):
                if which == "act":
                    self.highs(engine, s)
                    if s - self.ns - 1 in self.rests:
                        n = self.rests.index(s - self.ns - 1)
                        engine.wait_ge(self.rest_ready, n + 1)
                        self.m.nc.scalar.activation(self.rest_tokens[:], self.m.ps[0:META, self.banks, :],
                                                    ACT.Copy).then_inc(self.rest_copied, 1)
                else:
                    self.lows(engine, s)
            for unit in self.units:
                if unit.place == s and unit.engine == which:
                    self.take(engine, unit)
            for work in (after or {}).get(s, []):
                work()

    def send(self, sp, ahead=2):
        self.m.send_blocks(sp, self.first + len(self.jobs) + ahead)

    def stage(self, ahead=2, tail=None, pe_work=None, act_work=None, dve_work=None):
        with self.m.nc.Block() as block:
            @block.sync
            def _(sp):
                self.send(sp, ahead)
                if tail:
                    tail(sp, self)

            @block.tensor
            def _(pe):
                self.products(pe, pe_work(pe) if pe_work else None)

            @block.scalar
            def _(act):
                self.split("act", act, act_work(act) if act_work else None)

            @block.vector
            def _(dve):
                self.split("dve", dve, dve_work(dve) if dve_work else None)


def setup_stage(m, h, turns, rows, names):
    nc, ps, dram = m.nc, m.ps, m.dram
    stage = m.area("gain_rows", [P, 2, P], rows)
    lq = m.area("lambda_rows", [P, 4, 64], rows + 1024)
    lw = m.area("lambda_work", [P, 2, 64], rows + 2048)
    ls = m.area("lambda_sums", [P, 4], rows + 2560)
    small = m.sem("small_loaded")
    cleared = m.sem("rows_cleared")
    turned = m.sem("gains_turned")
    sums = m.sem("lambda_sums_ready")
    exps = m.sem("lambda_exps_ready")
    m.tokens_loaded = m.sem("tokens_loaded")
    m.turns_loaded = m.sem("turns_loaded")
    at, m.col_of, loads = 0, {}, []
    for name, src in names:
        k = src.shape[0]
        if at < P and at + k > P:
            at = P
        m.col_of[name] = at
        loads.append((src, at // P, at % P, k))
        at += k
    assert at <= 2 * P
    n_small = 1 + len(loads) + 4 + 2 + 2

    with nc.Block() as block:
        @block.sync
        def _(sp):
            x = dram["x"][0]
            sp.dma_start(h[0:META, 0, :], dram["meta_tokens"]).then_inc(m.tokens_loaded, 16)
            sp.dma_start(h[META:P, 0, :], x[0:P - META, :]).then_inc(m.tokens_loaded, 16)
            for t, (t0, n) in enumerate(TILES1[1:], 1):
                sp.dma_start(h[0:n, t, :], x[t0 - META:t0 - META + n, :]).then_inc(m.tokens_loaded, 16)
            sp.dma_start(m.masks[:], dram["masks"]).then_inc(small, 16)
            sp.wait_ge(cleared, 1)
            for src, g, at, k in loads:
                sp.dma_start(stage[at:at + k, g, :], src).then_inc(small, 16)
            for i, name in enumerate(("lambda_q1", "lambda_k1", "lambda_q2", "lambda_k2")):
                sp.dma_start(lq[:, i, :], dram[name].to_broadcast([P, 64])).then_inc(small, 16)
            for i, src in enumerate((dram["b_q_gain_2"], dram["k_gain_2"].unsqueeze(0))):
                sp.dma_start(m.gpe[:, i, :], src[:, NOPE:].to_broadcast([P, ROPE])).then_inc(small, 16)
            for i, name in enumerate(("a_ig_bias_2", "a_fg_bias_2")):
                sp.dma_start(m.gate_bias[:, MH * i:MH * (i + 1)],
                             dram[name].to_broadcast([P, MH])).then_inc(small, 16)
            sp.dma_start(turns[:], dram["turns"]).then_inc(m.turns_loaded, 16)
            m.send_blocks(sp, 2)
            sp.wait_ge(m.tokens_loaded, 16 * (1 + len(TILES1)))
            sp.wait_ge(m.turns_loaded, 16)

        @block.tensor
        def _(pe):
            pe.wait_ge(small, 16 * n_small)
            for g in range(2):
                ins = pe.transpose(ps[:, g, 0:P], stage[:, g, :], m.ident)
            ins.then_inc(turned, 1)

        @block.vector
        def _(dve):
            step = m.dve_steps.on(dve)
            nc.vector.memset(stage[:], 0.0).then_inc(cleared, 1)
            nc.vector.memset(m.eps[:], EPS)
            dve.wait_ge(small, 16 * n_small)
            for i in range(2):
                ins = nc.vector.tensor_tensor_reduce(
                    out=lw[:, i, :], in0=lq[:, 2 * i, :], in1=lq[:, 2 * i + 1, :], scale=1.0, scalar=0.0,
                    op0=ALU.mult, op1=ALU.add, accum_out=ls[:, i:i + 1])
                ins.then_inc(sums, 1)
            dve.wait_ge(turned, 1)
            step(nc.vector.tensor_copy(m.cols[:], ps[:, 0:2, 0:P]))
            dve.wait_ge(exps, 1)
            step(nc.vector.tensor_tensor(m.lam[:], ls[:, 3:4], ls[:, 2:3], ALU.subtract))
            step(nc.vector.tensor_scalar(m.lam[:], m.lam[:], -LAM_INIT, None, ALU.add))

        @block.scalar
        def _(act):
            act.wait_ge(sums, 2)
            nc.scalar.activation(ls[:, 2:4], ls[:, 0:2], ACT.Exp).then_inc(exps, 1)


def projection_stage(m, hn, qk, v, raw, turns, rot_work, slot):
    nc, ps = m.nc, m.ps
    halved = lambda t: t.rearrange("p (a b) -> p a b", a=2)
    scale = 64.0 ** -0.5

    def take_features(to, scale=1.0):
        def take(step, u, psum):
            nc.scalar.activation(to(u)[:, 512:], g.rest_psum(u), ACT.Copy, scale=scale)
            return nc.scalar.activation(to(u)[:, 0:512], psum, ACT.Copy, scale=scale)
        return take

    def take_v(step, u, psum):
        return nc.scalar.activation(v[0:TILES1[u][1], u, :], psum, ACT.Copy)

    takes = [("features", take_features(lambda u: qk[:, u, :], scale)),
             ("features", take_features(lambda u: qk[:, 4 + u, :])), ("tokens", take_v)] + [
        ("features", take_features(lambda u, i=i: raw[:, 4 * i + u, :])) for i in range(3)]
    jobs = [dict(kind=kind, act=hn, tiles=TILES1, engine="act", take=take, rest=True, early=True)
            for kind, take in takes]
    g = SplitGemm(m, "in1", jobs, m.gaps + [slot], banks=5,
                  rest_tokens=m.at("in1_rest", [META, 512], slot + 8192))
    rotated = m.sem("in1_rotated")
    rot_taken = m.sem("in1_rot_taken")

    with nc.Block() as block:
        @block.sync
        def _(sp):
            g.send(sp)
            m.send_experts(sp, 3)

        @block.tensor
        def _(pe):
            def rotate(n):
                pe.wait_ge(g.out["act"], n + 1)
                if n >= 1:
                    pe.wait_ge(rot_taken, n)
                for a in range(2):
                    ins = pe.matmul(ps[:, 6 + a, 0:HALF1], m.rot, qk[:, n, a * HALF1:(a + 1) * HALF1],
                                    start=True, stop=True)
                ins.then_inc(rotated, 1)

            g.products(pe, {KD + 1 + 2 * n: [lambda n=n: rotate(n)] for n in range(8)})

        @block.scalar
        def _(act):
            g.split("act", act)

        @block.vector
        def _(dve):
            step = m.dve_steps.on(dve)

            def turn(n):
                dve.wait_ge(rotated, n + 1)
                nc.vector.tensor_tensor(halved(rot_work[:, n % 2, :]), ps[:, 6:8, 0:HALF1],
                                        halved(turns[:, 1, :]), ALU.mult).then_inc(rot_taken, 1)
                step(nc.vector.tensor_tensor(qk[:, n, :], qk[:, n, :], turns[:, 0, :], ALU.mult))
                dve.wait_ge(rot_taken, n + 1)
                step(nc.vector.tensor_tensor(qk[:, n, :], qk[:, n, :], rot_work[:, n % 2, :], ALU.add))

            g.split("dve", dve, {KD + 4 + 2 * n: [lambda n=n: turn(n)] for n in range(8)})


def diff_attention_stage(m, qk, v, raw, mixed, at):
    nc, ps = m.nc, m.ps
    units = [(h, t) for h in range(AH) for t in range(len(TILES1))]
    e = m.area("da_e", [P, 3, 2, L1], at)
    at += 24 * L1
    st = m.area("da_st", [P, 3, 8], at)
    ss = m.area("da_ss", [P, 3, len(TILES1) * AH], at + 96)
    qz = m.area("da_qz", [P, 3, 2, P], at + 96 + 256)
    spare = m.ring_at + 9 * SLOT * 4
    pt = m.at("da_pt", [P, 2, len(TILES1), P], spare)
    spare += 8 * len(TILES1) * P
    o = m.at("da_o", [P, len(TILES1), AH, AV], spare)
    cw = m.at("da_conv", [P, 2, L1], spare + 4 * len(TILES1) * AH * AV)
    junk = m.at("da_junk", [P, AV], spare + 4 * len(TILES1) * AH * AV + 8 * L1)
    scored = m.sem("da_scored")
    maxed = m.sem("da_maxed")
    q_ready = m.sem("da_q_ready")
    exped = m.sem("da_exped")
    mixed_ready = m.sem("da_weights")
    turned = m.sem("da_turned")
    pt_ready = m.sem("da_pt_ready")
    summed = m.sem("da_summed")
    o_ready = m.sem("da_o_ready")
    squared = m.sem("da_squared")
    root = m.sem("da_root")
    scaled = m.sem("da_scaled")
    o_turned = m.sem("da_o_turned")
    cleared = m.sem("da_cleared")
    mixed_taken = m.sem("da_mixed_taken")
    nt, nu = len(TILES1), len(units)

    def pair(u, i):
        return (0, 2, 6)[(2 * u + i) % 3]

    with nc.Block() as block:
        @block.tensor
        def _(pe):
            def scores(u):
                h, t = units[u]
                t0, n = TILES1[t]
                pe.wait_ge(q_ready, 2 * u + 3)
                for i in range(2):
                    if 2 * u + i >= 3:
                        pe.wait_ge(exped, 2 * u + i - 2)
                    for a in range(2):
                        ins = pe.matmul(ps[0:n, pair(u, i) + a, 0:HALF1], qz[:, u % 3, i, 0:n],
                                        qk[:, 4 + h, a * HALF1:(a + 1) * HALF1], start=True, stop=True)
                    ins.then_inc(scored, 1)

            def turn(u):
                n = TILES1[units[u][1]][1]
                pe.wait_ge(mixed_ready, u + 1)
                for s, (s0, w) in enumerate(TILES1):
                    if s == 4 and u >= 1:
                        pe.wait_ge(o_ready, u)
                    ins = pe.transpose(ps[0:w, 4 + s // 4, (s % 4) * P:(s % 4) * P + n],
                                       e[0:n, u % 3, 0, s0:s0 + w], m.ident[0:n, 0:n])
                ins.then_inc(turned, 1)

            def values(u):
                h, t = units[u]
                n = TILES1[t][1]
                pe.wait_ge(pt_ready, u + 1)
                for s, (s0, w) in enumerate(TILES1):
                    ins = pe.matmul(ps[0:n, 5, 0:AV], pt[0:w, u % 2, s, 0:n],
                                    v[0:w, s, h * AV:(h + 1) * AV], start=(s == 0), stop=(s == nt - 1))
                ins.then_inc(summed, 1)

            for u in range(nu + 2):
                if u >= 2:
                    turn(u - 2)
                if u < nu:
                    scores(u)
                if u >= 2:
                    values(u - 2)
            for t, (_, n) in enumerate(TILES1):
                pe.wait_ge(scaled, t + 1)
                for h in range(AH):
                    ins = pe.transpose(ps[:, t % 4, h * P:h * P + n], o[0:n, t, h, :], m.ident[0:n, 0:n])
                ins.then_inc(o_turned, 1)
                if t == 3:
                    pe.wait_ge(mixed_taken, 1)

        @block.vector
        def _(dve):
            step = m.dve_steps.on(dve)
            nc.vector.memset(ss[:], 1.0).then_inc(cleared, 1)
            dve.wait_ge(cleared, 1)
            step(nc.vector.tensor_scalar(m.col("subln"), m.col("subln"), 1.0 - LAM_INIT, None, ALU.mult))

            def combine(u):
                n = TILES1[units[u][1]][1]
                b = u % 3
                dve.wait_ge(exped, 2 * u + 2)
                step(nc.vector.reciprocal(st[0:n, b, 4:6], st[0:n, b, 2:4]))
                step(nc.vector.tensor_tensor(st[0:n, b, 6:7], st[0:n, b, 5:6], m.lam[0:n, :], ALU.mult))
                step(nc.vector.tensor_scalar(e[0:n, b, 1, :], e[0:n, b, 1, :], st[0:n, b, 6:7], None, ALU.mult))
                nc.vector.scalar_tensor_tensor(out=e[0:n, b, 0, :], in0=e[0:n, b, 0, :], scalar=st[0:n, b, 4:5],
                                               in1=e[0:n, b, 1, :], op0=ALU.mult,
                                               op1=ALU.add).then_inc(mixed_ready, 1)

            def squares(u):
                h, t = units[u]
                n = TILES1[t][1]
                dve.wait_ge(o_ready, u + 1)
                nc.vector.tensor_tensor_reduce(
                    out=junk[0:n, :], in0=o[0:n, t, h, :], in1=o[0:n, t, h, :], scale=1.0 / AV, scalar=0.0,
                    op0=ALU.mult, op1=ALU.add,
                    accum_out=ss[0:n, 0, t * AH + h:t * AH + h + 1]).then_inc(squared, 1)
                dve.wait_ge(squared, u + 1)

            def maxima(u):
                n = TILES1[units[u][1]][1]
                for i in range(2):
                    dve.wait_ge(scored, 2 * u + i + 1)
                    nc.vector.tensor_reduce(st[0:n, u % 3, i:i + 1], ps[0:n, pair(u, i):pair(u, i) + 2, 0:HALF1],
                                            AX.XY, ALU.max, negate=True).then_inc(maxed, 1)

            for u in range(nu + 4):
                if 1 <= u <= nu:
                    combine(u - 1)
                if u < nu:
                    maxima(u)
                if u >= 4:
                    squares(u - 4)
            dve.wait_ge(root, 1)
            step(nc.vector.reciprocal(ss[:, 2, :], ss[:, 1, :]))
            for t, (_, n) in enumerate(TILES1):
                nc.vector.tensor_tensor(o[0:n, t], o[0:n, t], spread(ss[0:n, 2, t * AH:(t + 1) * AH], AV),
                                        ALU.mult).then_inc(scaled, 1)
            for t, (t0, n) in enumerate(TILES1):
                dve.wait_ge(o_turned, t + 1)
                bank = ps[:, t % 4, :].rearrange("p (k c) -> p k c", k=4)[:, :, 0:n]
                nc.vector.tensor_scalar(mixed[:, 0:AH, t0:t0 + n], bank, m.col("subln"), None,
                                        ALU.mult).then_inc(mixed_taken, 1)

        def take_turned(act, u):
            n = TILES1[units[u][1]][1]
            w = TILES1[-1][1]
            act.wait_ge(turned, u + 1)
            nc.scalar.activation(pt[:, u % 2, 0:4, 0:n], ps[:, 4, :].rearrange("p (k c) -> p k c", k=4)[:, :, 0:n],
                                 ACT.Copy)
            nc.scalar.activation(pt[0:w, u % 2, 4, 0:n], ps[0:w, 5, 0:n], ACT.Copy).then_inc(pt_ready, 1)

        def take_values(act, u):
            h, t = units[u]
            n = TILES1[t][1]
            act.wait_ge(summed, u + 1)
            nc.scalar.activation(o[0:n, t, h, :], ps[0:n, 5, 0:AV], ACT.Copy).then_inc(o_ready, 1)

        @block.scalar
        def _(act):
            def exps(u, i):
                n = TILES1[units[u][1]][1]
                b = u % 3
                act.wait_ge(maxed, 2 * u + i + 1)
                if u >= 3:
                    act.wait_ge(turned, u - 2)
                nc.scalar.activation(e[0:n, b, i, :].rearrange("p (a c) -> p a c", a=2),
                                     ps[0:n, pair(u, i):pair(u, i) + 2, 0:HALF1], ACT.Exp, bias=st[0:n, b, i:i + 1],
                                     accum_out=st[0:n, b, 2 + i:3 + i]).then_inc(exped, 1)

            for u in range(nu + 2):
                if u >= 2:
                    take_turned(act, u - 2)
                if u < nu:
                    exps(u, 0)
                if u >= 2:
                    take_values(act, u - 2)
                if u < nu:
                    exps(u, 1)
            act.wait_ge(squared, len(units))
            nc.scalar.activation(ss[:, 1, :], ss[:, 0, :], ACT.Sqrt, bias=m.eps[:, 0:1]).then_inc(root, 1)

        @block.gpsimd
        def _(pool):
            step = m.pool_steps.on(pool)
            g = nc.gpsimd
            g.memset(qz[:], 0.0).then_inc(q_ready, 1)
            pool.wait_ge(q_ready, 1)

            def queries(u):
                h, t = units[u]
                t0, n = TILES1[t]
                if u >= 3:
                    pool.wait_ge(scored, 2 * (u - 2))
                for i in range(2):
                    d = slice(64 * i, 64 * i + 64)
                    g.tensor_copy(qz[d, u % 3, i, 0:n], qk[d, h, t0:t0 + n]).then_inc(q_ready, 1)
                    pool.wait_ge(q_ready, 2 * u + i + 2)

            def convolution(c):
                cx, cb, cc = raw[:, c, :], raw[:, 4 + c, :], raw[:, 8 + c, :]
                yield g.tensor_tensor(cc, cc, cx, ALU.mult)
                yield g.tensor_scalar(cw[:, 0, :], cc, m.col("conv_w", 4 + c), None, ALU.mult)
                yield g.tensor_scalar(cw[:, 1, :], cc, m.col("conv_w", c), None, ALU.mult)
                yield g.tensor_tensor(cw[:, 0, 1:], cw[:, 0, 1:], cw[:, 1, 0:L1 - 1], ALU.add)
                yield g.tensor_scalar(cw[:, 1, :], cc, m.col("conv_w", 8 + c), None, ALU.mult)
                yield g.tensor_tensor(cw[:, 0, 0:L1 - 1], cw[:, 0, 0:L1 - 1], cw[:, 1, 1:], ALU.add)
                yield g.tensor_tensor(mixed[:, AH + c, :], cw[:, 0, :], cb, ALU.mult)

            conv = (ins for c in range(4) for ins in convolution(c))
            for u in range(len(units)):
                queries(u)
                if u >= 2:
                    for _ in range(2):
                        ins = next(conv, None)
                        if ins is not None:
                            step(ins)


def out_stage(m, name, mixed, x, tiles, slots, ahead=2, tail=None):
    def take(c):
        def f(step, u, psum):
            to = x[0:tiles[u][1], u, c * 512:(c + 1) * 512]
            return m.nc.vector.tensor_tensor(to, psum, to, ALU.add)
        return f

    SplitGemm(m, name, [dict(kind="tokens", act=mixed, tiles=tiles, engine="dve", take=take(c))
                        for c in range(2)], slots).stage(ahead, tail=tail)


def router_stage(m, hn, mem_t, mk_tok, mv, at, slots):
    nc, ps = m.nc, m.ps
    nt = len(TILES1)
    w = m.area("router_w", [P, KD, NE], at)
    aff = m.area("router_aff", [P, nt, NE], at + 512)
    st = m.area("router_st", [P, 3, 8], at + 832)
    afft = m.area("router_afft", [NE, 2, L1], at + 960)
    vals = m.area("router_vals", [NE, 8 * ROUNDS], at + 960 + 8 * L1)
    idx = m.area("router_idx", [NE, 8 * ROUNDS], at + 1280 + 8 * L1, U32)
    idxf = m.area("router_idxf", [NE, 8 * ROUNDS], at + 1600 + 8 * L1)
    loaded = m.sem("router_loaded")
    logits_done = m.sem("router_logits_done")
    logits_copied = m.sem("router_logits_copied")
    scored = m.sem("router_scored")
    shifted = m.sem("router_shifted")
    exped = m.sem("router_exped")
    normed = m.sem("router_normed")
    turned = m.sem("router_turned")
    picked = m.sem("router_picked")
    picks_turned = m.sem("router_picks_turned")

    def take(dst):
        return lambda step, u, psum: nc.scalar.activation(dst[:, u, :], psum, ACT.Copy)

    g = SplitGemm(m, "mem", [dict(kind="tokens", act=mem_t, tiles=TILES2[:2], engine="act", take=take(dst))
                             for dst in (mk_tok[0], mv[0], mk_tok[1], mv[1])], slots, banks=5,
                  pool_lows=True)
    SCORED, SHIFTED, NORMED, TAKEN = 1, 5, 7, 11

    with nc.Block() as block:
        @block.sync
        def _(sp):
            sp.dma_start(w[:], m.dram["w_router"][0].rearrange("(k p) e -> p k e", p=P)).then_inc(loaded, 16)
            g.send(sp, 0)
            m.send_experts(sp, NPIECE)

        @block.gpsimd
        def _(pool):
            g.pool_split(pool)

        @block.tensor
        def _(pe):
            def scores():
                pe.wait_ge(loaded, 16)
                for half in range(2):
                    for k in range(KD):
                        ins = pe.matmul(ps[0:NE, 6 + half, 0:HALF1], w[:, k, :],
                                        hn[:, k, half * HALF1:(half + 1) * HALF1],
                                        start=(k == 0), stop=(k == KD - 1))
                ins.then_inc(logits_done, 1)

            def turn_scores():
                pe.wait_ge(logits_copied, 1)
                for t, (t0, n) in enumerate(TILES1):
                    ins = pe.transpose(ps[0:n, 5, t * NE:(t + 1) * NE], afft[:, 1, t0:t0 + n],
                                       m.ident[0:NE, 0:NE])
                ins.then_inc(scored, 1)

            def turn():
                pe.wait_ge(normed, 1)
                for t, (_, n) in enumerate(TILES1):
                    ins = pe.transpose(ps[0:NE, 6 + t // 4, (t % 4) * P:(t % 4) * P + n], aff[0:n, t, :],
                                       m.ident[0:n, 0:n])
                ins.then_inc(turned, 1)

            g.products(pe, {SCORED: [scores], SCORED + 1: [turn_scores], NORMED: [turn]})
            pe.wait_ge(picked, 1)
            pe.transpose(ps[0:CAP, 5, 0:NE], vals[:, 0:CAP], m.ident[0:NE, 0:NE])
            pe.transpose(ps[0:CAP, 5, NE:2 * NE], idxf[:, 0:CAP], m.ident[0:NE, 0:NE]).then_inc(picks_turned, 1)

        @block.vector
        def _(dve):
            step = m.dve_steps.on(dve)

            def copy_logits():
                dve.wait_ge(logits_done, 1)
                nc.vector.tensor_copy(afft[:, 1, :].rearrange("p (a b) -> p a b", a=2),
                                      ps[0:NE, 6:8, 0:HALF1]).then_inc(logits_copied, 1)

            def shift():
                dve.wait_ge(scored, 1)
                last = TILES1[-1][1]
                nc.vector.tensor_copy(aff[:, 0:nt - 1, :],
                                      ps[:, 5, 0:(nt - 1) * NE].rearrange("p (t e) -> p t e", e=NE))
                step(nc.vector.tensor_copy(aff[0:last, nt - 1, :], ps[0:last, 5, (nt - 1) * NE:nt * NE]))
                step(nc.vector.tensor_reduce(st[:, 0, 0:nt], aff[:], AX.X, ALU.max))
                nc.vector.tensor_tensor(aff[:], aff[:], spread(st[:, 0, 0:nt], NE), ALU.subtract).then_inc(shifted, 1)

            def normalise():
                dve.wait_ge(exped, 1)
                step(nc.vector.tensor_reduce(st[:, 1, 0:nt], aff[:], AX.X, ALU.add))
                step(nc.vector.reciprocal(st[:, 2, 0:nt], st[:, 1, 0:nt]))
                nc.vector.tensor_tensor(aff[:], aff[:], spread(st[:, 2, 0:nt], NE), ALU.mult).then_inc(normed, 1)

            def take_turned():
                dve.wait_ge(turned, 1)
                nc.vector.tensor_copy(afft[:, 0, 0:512], ps[0:NE, 6, :])
                step(nc.vector.tensor_copy(afft[:, 0, 512:L1], ps[0:NE, 7, 0:L1 - 512]))

            def pick(r):
                a = afft[:, r % 2, :]
                best = vals[:, 8 * r:8 * r + 8]
                step(nc.vector.max(best, a))
                step(nc.vector.max_index(idx[:, 8 * r:8 * r + 8], best, a))
                if r + 1 < ROUNDS:
                    step(nc.vector.match_replace(afft[:, (r + 1) % 2, :], best, a, -1.0))
                else:
                    nc.vector.tensor_copy(idxf[:], idx[:]).then_inc(picked, 1)

            step(nc.vector.memset(aff[:], 0.0))
            work = {TAKEN + 1 + 2 * r: [lambda r=r: pick(r)] for r in range(ROUNDS)}
            work.update({SCORED + 2: [copy_logits], SHIFTED: [shift], NORMED: [normalise], TAKEN: [take_turned]})
            g.split("dve", dve, work)
            dve.wait_ge(picks_turned, 1)
            nc.vector.tensor_copy(m.gates[:], ps[0:CAP, 5, 0:NE])
            step(nc.vector.tensor_copy(m.rows[:], ps[0:CAP, 5, NE:2 * NE]))

        @block.scalar
        def _(act):
            def exponential():
                act.wait_ge(shifted, 1)
                nc.scalar.activation(aff[:], aff[:], ACT.Exp).then_inc(exped, 1)

            g.split("act", act, {SHIFTED + 1: [exponential]})


def experts_stage(m, at):
    nc, ps = m.nc, m.ps
    PIECES = 24
    FIRST = 8
    AHEAD = 2
    size = 4 * KD * CAP
    xg = m.area("ex_rows", [CAP, D], at)
    hid = m.area("ex_hidden", [CAP, FH], at + 4096)
    y = m.area("ex_y", [CAP, D], at + 8192)
    at += 12288
    x_part = [m.area(f"ex_x{i}", [P, KD, CAP], at + size * i, F32R) for i in range(2)]
    h_part = [m.area(f"ex_h{i}", [P, KD, CAP], at + size * (2 + i), F32R) for i in range(2)]
    xs = m.area("ex_x_scaled", [P, KD, CAP], at + size * 4)
    at += 5 * size
    rows_in = m.area("ex_rows_in", [CAP, 1], at, U32)
    rows_out = m.area("ex_rows_out", [CAP, 1], at + 32, U32)
    gate = m.area("ex_gate", [CAP, 1], at + 64)
    high_done = m.sem("ex_high_done")
    low_done = m.sem("ex_low_done")
    used = m.sem("ex_pieces_used")
    silu_done = m.sem("ex_silu_done")
    hid_done = m.sem("ex_hidden_done")
    turned = m.sem("ex_hidden_turned")
    h_high = m.sem("ex_h_high")
    h_done = m.sem("ex_h_split")
    rows_ready = m.sem("ex_rows_ready")
    gathered = m.lasting("ex_gathered")
    x_turned = m.sem("ex_x_turned")
    x_scaled = m.sem("ex_x_scaled")
    x_high = m.sem("ex_x_high")
    x_done = m.sem("ex_x_split")
    gate_ready = m.sem("ex_gate_ready")
    y_done = m.sem("ex_y_done")
    y_free = m.sem("ex_y_free")
    scattered = m.lasting("ex_scattered")
    sp_passed = m.sem("ex_sp_waits_passed")
    pool_passed = m.sem("ex_pool_waits_passed")
    quarter = lambda bank: bank[:, 0:4 * CAP].rearrange("p (k c) -> p k c", k=4)

    with nc.Block() as block:
        @block.sync
        def _(sp):
            for n in range(NPIECE, 12):
                sp.wait_ge(low_done, n - NPIECE + 1)
                m.expert_load(sp, 12 + n if n < FIRST else n - FIRST, 0, n % NPIECE)
            with sp.Fori(0, NE - 1) as e:
                for i in range(PIECES):
                    wait_counted(sp, low_done, e * PIECES + (12 - NPIECE + 1 + i), sp_passed)
                    j = (4 + i) % PIECES
                    ahead = (4 + i) // PIECES + (1 if 12 <= j < 20 else 0)
                    m.expert_load(sp, j, bass.ds(e + ahead, 1), i % NPIECE)
            n = 12 + PIECES * (NE - 1)
            for j in list(range(4, 12)) + list(range(20, 24)):
                sp.wait_ge(low_done, n - NPIECE + 1)
                m.expert_load(sp, j, NE - 1, n % NPIECE)
                n += 1

        @block.tensor
        def _(pe):
            first_unit = 0

            def products(n, e, banks, parts, k0, start, stop):
                pe.wait_ge(low_done, e * PIECES + (n + 1))
                w = [x[:, n % NSPLIT, :].rearrange("p (k c) -> p k c", k=2) for x in (m.high, m.low_part)]
                for k in range(2):
                    for a, b in ((0, 0), (0, 1), (1, 0)):
                        for c in range(2):
                            ins = pe.matmul(ps[0:CAP, banks + c, :], parts[a][:, k0 + k, :],
                                            w[b][:, k, c * 512:(c + 1) * 512],
                                            start=start and k == 0 and a == b == 0,
                                            stop=stop and k == 1 and a == 1)
                ins.then_inc(used, 1)

            def gate_up(n, e, unit, turn_unit=None):
                for i in range(8):
                    if i == 0 and unit is not first_unit:
                        pe.wait_ge(hid_done, unit)
                    products(n + i, e, 2 * (i % 2), x_part, 2 * (i // 2), i < 2, i >= 6)
                    if i == 3 and turn_unit is not None:
                        turn(turn_unit)

            def turn(unit):
                for k in range(KD):
                    ins = pe.transpose(ps[:, 6 + k // 4, (k % 4) * CAP:(k % 4 + 1) * CAP],
                                       hid[:, k * P:(k + 1) * P], m.ident[0:CAP, 0:CAP])
                ins.then_inc(turned, 1)

            def turn_x(count):
                pe.wait_ge(gathered, count * 16)
                for k in range(KD):
                    ins = pe.transpose(ps[:, 6 + k // 4, (k % 4) * CAP:(k % 4 + 1) * CAP],
                                       xg[:, k * P:(k + 1) * P], m.ident[0:CAP, 0:CAP])
                ins.then_inc(x_turned, 1)

            def down(n, e, unit, half, next_x=None):
                for i in range(4):
                    if i == 0:
                        pe.wait_ge(h_done, unit + 1)
                        if half == 0:
                            pe.wait_ge(y_free, e + 1)
                    products(n + i, e, 4, h_part, 2 * i, half == 0 and i == 0, half == 1 and i == 3)
                    if i == 0 and next_x is not None:
                        turn_x(next_x)

            turn_x(1)
            pe.wait_ge(x_done, 1)
            gate_up(0, 0, first_unit)
            with pe.Fori(0, NE - 1) as e:
                gate_up(FIRST, e, e * 2 + 1, turn_unit=e * 2)
                down(FIRST + 8, e, e * 2, 0, next_x=e + 2)
                pe.wait_ge(x_done, e + 2)
                gate_up(FIRST + 12, e, e * 2 + 2, turn_unit=e * 2 + 1)
                down(FIRST + 20, e, e * 2 + 1, 1)
            e = NE - 1
            gate_up(FIRST, e, e * 2 + 1, turn_unit=e * 2)
            down(FIRST + 8, e, e * 2, 0)
            pe.wait_ge(hid_done, e * 2 + 2)
            turn(e * 2 + 1)
            down(FIRST + 12, e, e * 2 + 1, 1)

        @block.scalar
        def _(act):
            def high(n, e=None):
                rounds = 16 * (n // NPIECE + 1)
                act.wait_ge(m.expert_loaded[n % NPIECE],
                            rounds if e is None else e * (16 * PIECES // NPIECE) + rounds)
                if e is not None:
                    act.wait_ge(used, e * PIECES + (n - NSPLIT + 1))
                elif n >= NSPLIT:
                    act.wait_ge(used, n - NSPLIT + 1)
                nc.scalar.activation(m.high[:, n % NSPLIT, :], m.pieces[:, n % NPIECE, :],
                                     ACT.Copy).then_inc(high_done, 1)

            def silu(pieces):
                act.wait_ge(used, pieces)
                nc.scalar.activation(hid[:].rearrange("p (a c) -> p a c", a=2), ps[0:CAP, 0:2, :],
                                     ACT.Silu).then_inc(silu_done, 1)

            def take_turned(unit):
                act.wait_ge(turned, unit + 1)
                nc.scalar.activation(h_part[0][:].rearrange("p (a k) c -> p a (k c)", a=2),
                                     ps[:, 6:8, 0:4 * CAP], ACT.Copy).then_inc(h_high, 1)

            for n in range(FIRST + AHEAD):
                high(n)
            silu(FIRST)
            with act.Fori(0, NE - 1) as e:
                for i in range(PIECES):
                    high(FIRST + AHEAD + i, e)
                    if i == 3:
                        take_turned(e * 2)
                    if i == 7:
                        silu(e * PIECES + (FIRST + 8))
                    if i == 15:
                        take_turned(e * 2 + 1)
                    if i == 19:
                        silu(e * PIECES + (FIRST + 20))
            base = PIECES * (NE - 1) + FIRST
            for i in range(16):
                if i + AHEAD < 16:
                    high(base + AHEAD + i)
                if i == 3:
                    take_turned(2 * NE - 2)
                if i == 7:
                    silu(base + 8)
                if i == 11:
                    take_turned(2 * NE - 1)

        @block.vector
        def _(dve):
            def low(n, e=None):
                dve.wait_ge(high_done, n + 1 if e is None else e * PIECES + (n + 1))
                nc.vector.tensor_tensor(m.low_part[:, n % NSPLIT, :], m.pieces[:, n % NPIECE, :],
                                        m.high[:, n % NSPLIT, :].bitcast(F32), ALU.subtract).then_inc(low_done, 1)

            def next_rows(e):
                nc.vector.tensor_copy(rows_in[:], m.rows[:, bass.ds(e, 1)]).then_inc(rows_ready, 1)

            def hidden(unit):
                dve.wait_ge(silu_done, unit + 1)
                h = hid[:].rearrange("p (a c) -> p a c", a=2)
                nc.vector.tensor_tensor(h, ps[0:CAP, 2:4, :], h, ALU.mult).then_inc(hid_done, 1)

            def split_hidden(unit):
                dve.wait_ge(h_high, unit + 1)
                for a in range(2):
                    ins = nc.vector.tensor_tensor(h_part[1][:, 4 * a:4 * a + 4, :], quarter(ps[:, 6 + a, :]),
                                                  h_part[0][:, 4 * a:4 * a + 4, :].bitcast(F32), ALU.subtract)
                ins.then_inc(h_done, 1)

            def take_x(count):
                dve.wait_ge(x_turned, count)
                for a in range(2):
                    ins = nc.vector.tensor_tensor(xs[:, 4 * a:4 * a + 4, :], quarter(ps[:, 6 + a, :]),
                                                  spread(m.colrange("ffn_g", KD)[:, 4 * a:4 * a + 4], CAP),
                                                  ALU.mult)
                ins.then_inc(x_scaled, 1)
                dve.wait_ge(x_scaled, count)
                nc.vector.tensor_copy(x_part[0][:], xs[:]).then_inc(x_high, 1)
                dve.wait_ge(x_high, count)
                nc.vector.tensor_tensor(x_part[1][:], xs[:], x_part[0][:].bitcast(F32),
                                        ALU.subtract).then_inc(x_done, 1)

            def take_y(e, pieces):
                dve.wait_ge(y_free, e + 1)
                nc.vector.tensor_copy(rows_out[:], m.rows[:, bass.ds(e, 1)])
                nc.vector.tensor_copy(gate[:], m.gates[:, bass.ds(e, 1)]).then_inc(gate_ready, 1)
                dve.wait_ge(gate_ready, e + 1)
                dve.wait_ge(used, pieces)
                nc.vector.tensor_scalar(y[:].rearrange("p (a c) -> p a c", a=2), ps[0:CAP, 4:6, :],
                                        gate[:, 0:1], None, ALU.mult).then_inc(y_done, 1)

            next_rows(0)
            for n in range(FIRST + AHEAD):
                low(n)
                if n == 0:
                    take_x(1)
            hidden(0)
            with dve.Fori(0, NE - 1) as e:
                for i in range(PIECES):
                    if i == 0:
                        dve.wait_ge(gathered, e * 16 + 16)
                        next_rows(e + 1)
                    low(FIRST + AHEAD + i, e)
                    if i == 3:
                        split_hidden(e * 2)
                    if i == 7:
                        hidden(e * 2 + 1)
                    if i == 8:
                        take_x(e + 2)
                    if i == 15:
                        split_hidden(e * 2 + 1)
                    if i == 19:
                        hidden(e * 2 + 2)
                    if i == 23:
                        take_y(e, e * PIECES + (FIRST + 24))
            base = PIECES * (NE - 1) + FIRST
            for i in range(16):
                if i + AHEAD < 16:
                    low(base + AHEAD + i)
                if i == 3:
                    split_hidden(2 * NE - 2)
                if i == 7:
                    hidden(2 * NE - 1)
                if i == 11:
                    split_hidden(2 * NE - 1)
            take_y(NE - 1, NE * PIECES)

        @block.gpsimd
        def _(pool):
            def gather(count):
                wait_counted(pool, rows_ready, count, pool_passed)
                nc.gpsimd.indirect_dma_start(
                    out=xg[:], out_offset=None, in_=m.xhat[:],
                    in_offset=bass.IndirectOffsetOnAxis(ap=rows_in[:, 0:1], axis=0)).then_inc(gathered, 16)

            def scatter(e):
                wait_counted(pool, y_done, e + 1, pool_passed)
                nc.gpsimd.indirect_dma_start(
                    out=m.resid[:], out_offset=bass.IndirectOffsetOnAxis(ap=rows_out[:, 0:1], axis=0),
                    in_=y[:], in_offset=None, compute_op=ALU.add).then_inc(scattered, 16)
                pool.wait_ge(scattered, e * 16 + 16)
                pool.sem_inc(y_free, 1)

            pool.sem_inc(y_free, 1)
            gather(1)
            with pool.Fori(0, NE - 1) as e:
                wait_counted(pool, x_turned, e + 1, pool_passed)
                gather(e + 2)
                scatter(e)
            scatter(NE - 1)


def final_norm_stage(m, x, at):
    nc = m.nc
    grow = m.area("fin_gain", [P, D], at)
    junk = m.area("fin_junk", [P, D], at + 4096)
    ss = m.area("fin_ss", [P, 3, 4], at + 8192)
    gain_loaded = m.sem("fin_gain_loaded")
    loaded = [m.sem(f"fin_loaded{t}") for t in range(4)]
    squared = m.sem("fin_squared")
    root = m.sem("fin_root")
    with nc.Block() as block:
        @block.sync
        def _(sp):
            for t in range(4):
                sp.dma_start(x[:, t, :], m.resid[META + t * P:META + (t + 1) * P, :]).then_inc(loaded[t], 16)
            sp.dma_start(grow[:], m.dram["final_norm_g"].unsqueeze(0).to_broadcast([P, D])).then_inc(gain_loaded, 16)
            m.send_blocks(sp, m.taken + 2)

        @block.vector
        def _(dve):
            step = m.dve_steps.on(dve)
            for t in range(4):
                dve.wait_ge(loaded[t], 16)
                nc.vector.tensor_tensor_reduce(
                    out=junk[:], in0=x[:, t, :], in1=x[:, t, :], scale=1.0 / D, scalar=0.0,
                    op0=ALU.mult, op1=ALU.add, accum_out=ss[:, 0, t:t + 1]).then_inc(squared, 1)
                dve.wait_ge(squared, t + 1)
            dve.wait_ge(root, 1)
            step(nc.vector.reciprocal(ss[:, 2, :], ss[:, 1, :]))
            dve.wait_ge(gain_loaded, 16)
            for t in range(4):
                step(nc.vector.scalar_tensor_tensor(out=x[:, t, :], in0=x[:, t, :], scalar=ss[:, 2, t:t + 1],
                                                    in1=grow[:], op0=ALU.mult, op1=ALU.mult))

        @block.scalar
        def _(act):
            act.wait_ge(squared, 4)
            nc.scalar.activation(ss[:, 1, :], ss[:, 0, :], ACT.Sqrt, bias=m.eps[:, 0:1]).then_inc(root, 1)


def group_norm_stage(m, name, jobs, at):
    nc, ps = m.nc, m.ps
    n_ss = sum(j["src"].shape[1] * j["src"].shape[2] for j in jobs)
    ss = m.area(f"{name}_ss", [P, 3, n_ss], at)
    junk = m.area(f"{name}_junk", [P, 2, 512], at + -(-12 * n_ss // 32) * 32)
    squares_ready = m.sem(f"{name}_squares")
    summed = m.sem(f"{name}_summed")
    squared = m.sem(f"{name}_squared")
    root = m.sem(f"{name}_root")
    scaled = m.sem(f"{name}_scaled")
    turned = m.sem(f"{name}_turned")
    taken = m.sem(f"{name}_taken")
    work, c = [], 0
    for j in jobs:
        _, nt, g, width = j["src"].shape
        for t in range(nt):
            work.append((j, t, g, width, c))
            c += g

    def squares_of(n):
        _, _, g, width, _ = work[n]
        return junk[:, n % 2, 0:g * width].rearrange("p (g w) -> p g w", g=g)

    with nc.Block() as block:
        @block.vector
        def _(dve):
            step = m.dve_steps.on(dve)
            for n, (j, t, g, width, c) in enumerate(work):
                dve.wait_ge(squares_ready, n + 1)
                nc.vector.tensor_reduce(ss[:, 0, c:c + g], squares_of(n), AX.X, ALU.add).then_inc(summed, 1)
            dve.wait_ge(summed, len(work))
            c = 0
            for n, j in enumerate(jobs):
                _, nt, g, width = j["src"].shape
                ins = nc.vector.tensor_scalar(ss[:, 0, c:c + nt * g], ss[:, 0, c:c + nt * g], 1.0 / width, None,
                                              ALU.mult)
                c += nt * g
                ins.then_inc(squared, 1)
            dve.wait_ge(root, 1)
            step(nc.vector.reciprocal(ss[:, 2, :], ss[:, 1, :]))
            c = 0
            for j in jobs:
                n = j["src"].shape[1] * j["src"].shape[2]
                step(nc.vector.tensor_scalar(ss[:, 2, c:c + n], ss[:, 2, c:c + n], j["factor"], None, ALU.mult))
                c += n
            for j, t, g, width, c in work:
                x = j["src"][:, t]
                nc.vector.tensor_tensor(x, x, spread(ss[:, 2, c:c + g], width), ALU.mult).then_inc(scaled, 1)

        @block.scalar
        def _(act):
            for n, (j, t, g, width, c) in enumerate(work):
                if n >= 2:
                    act.wait_ge(summed, n - 1)
                nc.scalar.activation(squares_of(n), j["src"][:, t], ACT.Square).then_inc(squares_ready, 1)
            act.wait_ge(squared, len(jobs))
            nc.scalar.activation(ss[:, 1, :], ss[:, 0, :], ACT.Sqrt, bias=m.eps[:, 0:1]).then_inc(root, 1)
            for n, (j, t, g, width, c) in enumerate(work):
                act.wait_ge(turned, n + 1)
                per = width // P
                bank = ps[:, n % 8, :].rearrange("p (k c) -> p k c", k=4)
                for i in range(per):
                    ins = nc.scalar.activation(j["dst"][:, i:g * per:per, t * P:(t + 1) * P],
                                               bank[:, i:g * per:per, :], ACT.Copy,
                                               scale=m.col(j["gain"][0], j["gain"][1] + i))
                ins.then_inc(taken, 1)

        @block.tensor
        def _(pe):
            for n, (j, t, g, width, c) in enumerate(work):
                pe.wait_ge(scaled, n + 1)
                if n >= 8:
                    pe.wait_ge(taken, n - 7)
                x = j["src"][:, t].rearrange("p g w -> p (g w)")
                for i in range(g * width // P):
                    ins = pe.transpose(ps[:, n % 8, i * P:(i + 1) * P], x[:, i * P:(i + 1) * P], m.ident)
                ins.then_inc(turned, 1)


def attention_stage(m, name, units, at):
    nc, ps = m.nc, m.ps
    probs = m.area(f"{name}_probs", [P, 4, 512], at)
    pt = m.area(f"{name}_pt", [P, 2, 512], at + 8192)
    st = m.area(f"{name}_st", [P, 4, 4], at + 12288)
    scored = m.sem(f"{name}_scored")
    maxed = m.sem(f"{name}_maxed")
    exped = m.sem(f"{name}_exped")
    ready = m.sem(f"{name}_ready")
    turned = m.sem(f"{name}_turned")
    pt_ready = m.sem(f"{name}_pt_ready")
    summed = m.sem(f"{name}_summed")
    taken = m.sem(f"{name}_taken")
    nu = len(units)

    with nc.Block() as block:
        @block.tensor
        def _(pe):
            def scores(u):
                if u >= 3:
                    pe.wait_ge(exped, u - 2)
                for i, (lhs, rhs) in enumerate(units[u]["scores"]):
                    ins = pe.matmul(ps[:, u % 3, 0:units[u]["width"]], lhs, rhs,
                                    start=(i == 0), stop=(i == len(units[u]["scores"]) - 1))
                ins.then_inc(scored, 1)

            def turn(u):
                pe.wait_ge(ready, u + 1)
                if u >= 2:
                    pe.wait_ge(pt_ready, u - 1)
                for s in range(units[u]["width"] // P):
                    ins = pe.transpose(ps[:, 3 + u % 2, s * P:(s + 1) * P], probs[:, u % 4, s * P:(s + 1) * P],
                                       m.ident)
                ins.then_inc(turned, 1)

            def values(u):
                pe.wait_ge(pt_ready, u + 1)
                if u >= 2:
                    pe.wait_ge(taken, u - 1)
                vs = units[u]["values"]
                for s, v in enumerate(vs):
                    ins = pe.matmul(ps[:, 5 + u % 2, 0:P], v, pt[:, u % 2, s * P:(s + 1) * P],
                                    start=(s == 0), stop=(s == len(vs) - 1))
                ins.then_inc(summed, 1)

            for u in range(nu + 3):
                if u < nu:
                    scores(u)
                if 2 <= u < nu + 2:
                    turn(u - 2)
                if u >= 3:
                    values(u - 3)

        @block.vector
        def _(dve):
            step = m.dve_steps.on(dve)

            def head(u):
                w = units[u]["width"]
                dve.wait_ge(scored, u + 1)
                s = ps[:, u % 3, 0:w]
                if units[u]["mask"] is not None:
                    step(nc.vector.tensor_tensor(s[:, w - P:w], s[:, w - P:w], units[u]["mask"], ALU.add))
                nc.vector.tensor_reduce(st[:, u % 4, 0:1], s, AX.X, ALU.max, negate=True).then_inc(maxed, 1)

            def norm(u):
                w = units[u]["width"]
                dve.wait_ge(exped, u + 1)
                step(nc.vector.reciprocal(st[:, u % 4, 2:3], st[:, u % 4, 1:2]))
                p = probs[:, u % 4, 0:w]
                nc.vector.tensor_scalar(p, p, st[:, u % 4, 2:3], None, ALU.mult).then_inc(ready, 1)

            def take(u):
                dve.wait_ge(summed, u + 1)
                y = units[u]["y"]
                nc.vector.tensor_tensor(y, ps[:, 5 + u % 2, 0:P], y, ALU.mult).then_inc(taken, 1)

            for u in range(nu + 4):
                if u < nu:
                    head(u)
                if 1 <= u <= nu:
                    norm(u - 1)
                if u >= 4:
                    take(u - 4)

        @block.scalar
        def _(act):
            for u in range(nu + 2):
                if u < nu:
                    w = units[u]["width"]
                    act.wait_ge(maxed, u + 1)
                    if u >= 4:
                        act.wait_ge(turned, u - 3)
                    nc.scalar.activation(probs[:, u % 4, 0:w], ps[:, u % 3, 0:w], ACT.Exp,
                                         bias=st[:, u % 4, 0:1], accum_out=st[:, u % 4, 1:2]).then_inc(exped, 1)
                if u >= 2:
                    w = units[u - 2]["width"]
                    act.wait_ge(turned, u - 1)
                    if u >= 4:
                        act.wait_ge(summed, u - 3)
                    nc.scalar.activation(pt[:, u % 2, 0:w], ps[:, 3 + u % 2, 0:w],
                                         ACT.Copy).then_inc(pt_ready, 1)


def memory_units(mq, mk, mv, y):
    return [dict(scores=[(mq[:, h, t * P:(t + 1) * P], mk[:, h, :])], width=MEM, mask=None,
                 values=[mv[:, s, h * P:(h + 1) * P] for s in range(MEM // P)],
                 y=y[:, 8 + h, t * P:(t + 1) * P])
            for h in range(MEMH) for t in range(4)]


def mlstm_in_stage(m, hn, qk, v, y, mq, gates, at):
    nc = m.nc
    raw = m.area("ml_raw", [P, 3, SEQ + 3], at)
    acc = m.area("ml_acc", [P, 2, SEQ], at + 6208)
    zs = m.area("ml_zs", [P, 2, SEQ], at + 6208 + 8 * SEQ)
    slots = m.gaps + [m.arena + at + 6208 + 16 * SEQ]
    padded = m.sem("ml_padded")
    raw_ready = m.sem("ml_raw_ready")
    conv_done = m.sem("ml_conv_done")
    silu_done = m.sem("ml_silu_done")
    z_ready = m.sem("ml_z_ready")
    z_used = m.sem("ml_z_used")
    act = nc.scalar
    NQK = 2 * MW // P

    def finish(n):
        act.wait_ge(conv_done, n + 1)
        act.activation(qk[:, n, :], acc[:, n % 2, :], ACT.Silu,
                       bias=m.col("a_conv_b", n)).then_inc(silu_done, 1)

    def take_qk(block):
        def f(step, u, psum):
            n = 4 * block + u
            if n == 0:
                act.wait_ge(padded, 1)
            if n >= 2:
                finish(n - 2)
            act.activation(raw[:, n % 3, 3:], psum, ACT.Copy).then_inc(raw_ready, 1)
            act.wait_ge(raw_ready, n + 1)
            return None
        return f

    def take_v(block):
        def f(step, u, psum):
            return act.activation(v[:, u, 512 * block:512 * (block + 1)], psum, ACT.Copy)
        return f

    def take_o(block):
        def f(step, u, psum):
            if block == 1 and u < 2:
                finish(NQK - 2 + u)
            return act.activation(y[:, 4 * block + u, :], psum, ACT.Tanh, scale=0.5)
        return f

    def take_z(block):
        def f(step, u, psum):
            n = 4 * block + u
            if n >= 2:
                act.wait_ge(z_used, n - 1)
            act.activation(zs[:, n % 2, :], psum, ACT.Silu).then_inc(z_ready, 1)
            act.wait_ge(z_ready, n + 1)
            return None
        return f

    def take_gates(step, u, psum):
        return act.activation(gates[:], psum, ACT.Copy)

    def take_mq(step, u, psum):
        return act.activation(mq[:, u, :], psum, ACT.Copy)

    def take_mz(step, u, psum):
        return act.activation(y[:, 8 + u, :], psum, ACT.Silu)

    takes = {"qk": ("features", take_qk), "v": ("tokens", take_v), "o": ("features", take_o),
             "z": ("features", take_z), "gates": ("features", lambda _: take_gates),
             "mq": ("tokens", lambda _: take_mq), "mz": ("features", lambda _: take_mz)}
    jobs = [dict(kind=takes[part][0], act=hn, tiles=TILES2, engine="act", take=takes[part][1](block),
                 spread=1)
            for part, block, _, _ in MLSTM_IN]
    g = SplitGemm(m, "in2", jobs, slots)

    def convolve(step, n):
        nc.vector.wait_ge(raw_ready, n + 1)
        if n >= 2:
            nc.vector.wait_ge(silu_done, n - 1)
        r, a = raw[:, n % 3, :], acc[:, n % 2, :]
        step(nc.vector.tensor_scalar(a, r[:, 3:], m.col("a_conv_w", 3 * NQK + n), None, ALU.mult))
        for j in (2, 1, 0):
            ins = nc.vector.scalar_tensor_tensor(out=a, in0=r[:, j:j + SEQ],
                                                 scalar=m.col("a_conv_w", j * NQK + n), in1=a,
                                                 op0=ALU.mult, op1=ALU.add)
            if j:
                step(ins)
        ins.then_inc(conv_done, 1)

    def open_gate(n):
        nc.vector.wait_ge(z_ready, n + 1)
        nc.vector.scalar_tensor_tensor(out=y[:, n, :], in0=y[:, n, :], scalar=1.0, in1=zs[:, n % 2, :],
                                       op0=ALU.add, op1=ALU.mult).then_inc(z_used, 1)

    with nc.Block() as block:
        @block.sync
        def _(sp):
            g.send(sp, ahead=0)

        @block.tensor
        def _(pe):
            g.products(pe)

        @block.scalar
        def _(act):
            g.split("act", act)

        @block.vector
        def _(dve):
            step = m.dve_steps.on(dve)
            nc.vector.memset(raw[:, :, 0:3], 0.0).then_inc(padded, 1)
            after = {}
            for unit in g.units:
                part, b = MLSTM_IN[unit.job][0:2]
                work = {"qk": lambda n: convolve(step, n), "z": open_gate}.get(part)
                if work:
                    after.setdefault(unit.place + 1, []).append(lambda n=4 * b + unit.u, f=work: f(n))
            g.split("dve", dve, after)


def mlstm_stage(m, qk, v, gates, ht, y, at):
    nc, ps = m.nc, m.ps
    units = [(h, t) for h in range(MH) for t in range(4)]
    b = m.area("xl_b", [P, 4, SEQ], at)
    e = m.area("xl_e", [P, 2, SEQ], at + 8192)
    p = m.area("xl_p", [P, 3, SEQ], at + 12288)
    pt = m.area("xl_pt", [P, 2, SEQ], at + 18432)
    at += 22528
    lf = m.area("xl_lf", [P, 4, MH], at)
    ig = m.area("xl_ig", [P, 4, MH], at + 64)
    tmp = m.area("xl_tmp", [P, 2, 4 * MH], at + 128)
    nb = m.area("xl_nb", [P, 4, MH], at + 256)
    st = m.area("xl_st", [P, 6, 8], at + 320)
    ss = m.area("xl_ss", [P, 3, 4 * MH], at + 512)
    junk = m.area("xl_junk", [P, MDH], at + 704)
    gates_turned = m.sem("xl_gates_turned")
    abs_ready = m.sem("xl_abs")
    exp_ready = m.sem("xl_exp")
    one_ready = m.sem("xl_one")
    ln_ready = m.sem("xl_ln")
    lf_ready = m.sem("xl_lf")
    total_ready = m.sem("xl_totals")
    b_ready = m.sem("xl_b_ready")
    decayed = m.sem("xl_decays")
    scored = m.sem("xl_scored")
    maxed = m.sem("xl_maxed")
    exped = m.sem("xl_exped")
    p_ready = m.sem("xl_p_ready")
    den_ready = m.sem("xl_den_ready")
    turned = m.sem("xl_turned")
    pt_ready = m.sem("xl_pt_ready")
    summed = m.sem("xl_summed")
    h_ready = m.sem("xl_h_ready")
    squared = m.sem("xl_squared")
    root = m.sem("xl_root")
    scaled = m.sem("xl_scaled")
    h_turned = m.sem("xl_h_turned")
    y_taken = m.sem("xl_y_taken")
    nu = len(units)
    QS = MDH ** -0.5

    with nc.Block() as block:
        @block.sync
        def _(sp):
            m.send_blocks(sp, m.taken + 2)

        @block.tensor
        def _(pe):
            for t in range(4):
                ins = pe.transpose(ps[:, 7, t * 2 * MH:(t + 1) * 2 * MH], gates[:, t * P:(t + 1) * P],
                                   m.ident[0:2 * MH, 0:2 * MH])
            ins.then_inc(gates_turned, 1)
            pe.wait_ge(lf_ready, 1)
            for t in range(4):
                for u in range(t + 1):
                    ins = pe.matmul(ps[:, 6, t * MH:(t + 1) * MH], m.upto if u == t else m.ones, lf[:, u, :],
                                    start=(u == 0), stop=(u == t))
            ins.then_inc(total_ready, 1)

            def scores(u):
                h, t = units[u]
                w = (t + 1) * P
                if u >= 2:
                    pe.wait_ge(p_ready, u - 1)
                pe.wait_ge(b_ready, h + 1)
                for i in range(t, -1, -1):
                    ins = pe.matmul(ps[:, u % 2, 0:(i + 1) * P], m.upto if i == t else m.ones,
                                    b[:, i, 0:(i + 1) * P], start=(i == t), stop=(i == 0))
                ins.then_inc(decayed, 1)
                for k in range(2):
                    ins = pe.matmul(ps[:, 2 + u % 2, 0:w], qk[:, 2 * h + k, t * P:(t + 1) * P],
                                    qk[:, 8 + 2 * h + k, 0:w], start=(k == 0), stop=(k == 1))
                ins.then_inc(scored, 1)

            def turn(u):
                t = units[u][1]
                pe.wait_ge(p_ready, u + 1)
                if u >= 2:
                    pe.wait_ge(pt_ready, u - 1)
                for s in range(t + 1):
                    ins = pe.transpose(ps[:, 4 + u % 2, s * P:(s + 1) * P], p[:, u % 3, s * P:(s + 1) * P], m.ident)
                ins.then_inc(turned, 1)

            def values(u):
                h, t = units[u]
                pe.wait_ge(pt_ready, u + 1)
                if u == 0:
                    pe.wait_ge(b_ready, 1)
                if u >= 2:
                    pe.wait_ge(h_ready, u - 1)
                for s in range(t + 1):
                    ins = pe.matmul(ps[:, 6 + u % 2, 0:MDH], pt[:, u % 2, s * P:(s + 1) * P],
                                    v[:, s, h * MDH:(h + 1) * MDH], start=(s == 0), stop=(s == t))
                ins.then_inc(summed, 1)

            for u in range(nu + 3):
                if u < nu:
                    scores(u)
                if 2 <= u < nu + 2:
                    turn(u - 2)
                if u >= 3:
                    values(u - 3)
            pe.wait_ge(scaled, 4)
            for f in range(MW // P):
                if f >= 4:
                    pe.wait_ge(y_taken, f - 3)
                for t in range(4):
                    ins = pe.transpose(ps[:, f % 4, t * P:(t + 1) * P], ht[:, t, f * P:(f + 1) * P], m.ident)
                ins.then_inc(h_turned, 1)

        @block.vector
        def _(dve):
            step = m.dve_steps.on(dve)
            gb = lambda k: m.gate_bias[:, MH * k:MH * (k + 1)].unsqueeze(1).to_broadcast([P, 4, MH])
            flat = lambda x: x.rearrange("p a b -> p (a b)")
            g = ps[:, 7, 0:8 * MH].rearrange("p (t g) -> p t g", t=4)
            dve.wait_ge(gates_turned, 1)
            nc.vector.tensor_tensor(ig[:], g[:, :, 0:MH], gb(0), ALU.add)
            step(nc.vector.tensor_tensor(lf[:], g[:, :, MH:2 * MH], gb(1), ALU.add))
            step(nc.vector.tensor_scalar(tmp[:, 0, :], flat(lf[:]), -1.0, None, ALU.mult))
            nc.vector.tensor_tensor(tmp[:, 0, :], tmp[:, 0, :], flat(lf[:]), ALU.max).then_inc(abs_ready, 1)
            dve.wait_ge(exp_ready, 1)
            nc.vector.tensor_scalar(tmp[:, 1, :], tmp[:, 1, :], 1.0, None, ALU.add).then_inc(one_ready, 1)
            dve.wait_ge(ln_ready, 1)
            nc.vector.scalar_tensor_tensor(out=flat(lf[:]), in0=flat(lf[:]), scalar=0.0, in1=tmp[:, 0, :],
                                           op0=ALU.min, op1=ALU.subtract).then_inc(lf_ready, 1)
            dve.wait_ge(lf_ready, 1)
            dve.wait_ge(total_ready, 1)
            step(nc.vector.tensor_scalar(flat(nb[:]), ps[:, 6, 0:4 * MH], -1.0, None, ALU.mult))
            step(nc.vector.tensor_scalar(m.colrange("a_h_norm", 8), m.colrange("a_h_norm", 8), 0.5, None,
                                         ALU.mult))

            def build(h):
                if h:
                    dve.wait_ge(decayed, 4 * h)
                for u in range(4):
                    c = slice(u * P, (u + 1) * P)
                    if u:
                        nc.vector.tensor_scalar(b[:, u, 0:u * P], m.masks[:, 0:u * P], 0.0,
                                                lf[:, u, h:h + 1], ALU.mult, ALU.add)
                    step(nc.vector.tensor_scalar(b[:, u, c], m.after, lf[:, u, h:h + 1], None, ALU.mult))
                    ins = nc.vector.scalar_tensor_tensor(out=b[:, u, c], in0=m.ident, scalar=ig[:, u, h:h + 1],
                                                         in1=b[:, u, c], op0=ALU.mult, op1=ALU.add)
                ins.then_inc(b_ready, 1)

            def head(u):
                h, t = units[u]
                w = (t + 1) * P
                x = ps[:, u % 2, 0:w]
                dve.wait_ge(decayed, u + 1)
                step(nc.vector.tensor_tensor(x[:, t * P:w], x[:, t * P:w], m.causal, ALU.add))
                step(nc.vector.tensor_reduce(st[:, u % 6, 0:1], x, AX.X, ALU.max, negate=True))
                nc.vector.tensor_tensor(st[:, u % 6, 1:2], st[:, u % 6, 0:1], nb[:, t, h:h + 1],
                                        ALU.min).then_inc(maxed, 1)

            def weigh(u):
                h, t = units[u]
                w = (t + 1) * P
                s = st[:, u % 6, :]
                dve.wait_ge(exped, u + 1)
                dve.wait_ge(scored, u + 1)
                if u >= 3:
                    dve.wait_ge(turned, u - 2)
                nc.vector.scalar_tensor_tensor(out=p[:, u % 3, 0:w], in0=ps[:, 2 + u % 2, 0:w], scalar=QS,
                                               in1=e[:, u % 2, 0:w], op0=ALU.mult, op1=ALU.mult,
                                               accum_out=s[:, 3:4]).then_inc(p_ready, 1)
                dve.wait_ge(p_ready, u + 1)
                step(nc.vector.tensor_scalar(s[:, 4:5], s[:, 3:4], -1.0, None, ALU.mult))
                step(nc.vector.tensor_tensor(s[:, 4:5], s[:, 4:5], s[:, 3:4], ALU.max))
                step(nc.vector.tensor_tensor(s[:, 4:5], s[:, 4:5], s[:, 2:3], ALU.max))
                nc.vector.reciprocal(s[:, 5:6], s[:, 4:5]).then_inc(den_ready, 1)

            def squares(u):
                h, t = units[u]
                dve.wait_ge(h_ready, u + 1)
                x = ht[:, t, h * MDH:(h + 1) * MDH]
                nc.vector.tensor_tensor_reduce(
                    out=junk[:], in0=x, in1=x, scale=1.0 / MDH, scalar=0.0, op0=ALU.mult, op1=ALU.add,
                    accum_out=ss[:, 0, t * MH + h:t * MH + h + 1]).then_inc(squared, 1)
                dve.wait_ge(squared, u + 1)

            build(0)
            for u in range(nu + 4):
                if 1 <= u <= nu:
                    weigh(u - 1)
                if u < nu:
                    head(u)
                if u % 4 == 3 and u + 1 < nu:
                    build((u + 1) // 4)
                if u >= 4:
                    squares(u - 4)
            dve.wait_ge(root, 1)
            step(nc.vector.reciprocal(ss[:, 2, :], ss[:, 1, :]))
            for t in range(4):
                x = ht[:, t, :].rearrange("p (h w) -> p h w", h=MH)
                nc.vector.tensor_tensor(x, x, spread(ss[:, 2, t * MH:(t + 1) * MH], MDH),
                                        ALU.mult).then_inc(scaled, 1)
            for f in range(MW // P):
                dve.wait_ge(h_turned, f + 1)
                nc.vector.scalar_tensor_tensor(out=y[:, f, :], in0=ps[:, f % 4, :], scalar=m.col("a_h_norm", f),
                                               in1=y[:, f, :], op0=ALU.mult, op1=ALU.mult).then_inc(y_taken, 1)

        @block.scalar
        def _(act):
            act.wait_ge(abs_ready, 1)
            nc.scalar.activation(tmp[:, 1, :], tmp[:, 0, :], ACT.Exp, scale=-1.0).then_inc(exp_ready, 1)
            act.wait_ge(one_ready, 1)
            nc.scalar.activation(tmp[:, 0, :], tmp[:, 1, :], ACT.Ln).then_inc(ln_ready, 1)

            def exps(u):
                h, t = units[u]
                w = (t + 1) * P
                act.wait_ge(maxed, u + 1)
                if u >= 2:
                    act.wait_ge(p_ready, u - 1)
                nc.scalar.activation(st[:, u % 6, 2:3], st[:, u % 6, 1:2], ACT.Exp)
                nc.scalar.activation(e[:, u % 2, 0:w], ps[:, u % 2, 0:w], ACT.Exp,
                                     bias=st[:, u % 6, 1:2]).then_inc(exped, 1)

            def take_turned(u):
                w = (units[u][1] + 1) * P
                act.wait_ge(turned, u + 1)
                if u >= 2:
                    act.wait_ge(summed, u - 1)
                nc.scalar.activation(pt[:, u % 2, 0:w], ps[:, 4 + u % 2, 0:w], ACT.Copy).then_inc(pt_ready, 1)

            def take_values(u):
                h, t = units[u]
                act.wait_ge(summed, u + 1)
                act.wait_ge(den_ready, u + 1)
                nc.scalar.activation(ht[:, t, h * MDH:(h + 1) * MDH], ps[:, 6 + u % 2, 0:MDH], ACT.Copy,
                                     scale=st[:, u % 6, 5:6]).then_inc(h_ready, 1)

            for u in range(nu + 3):
                if u < nu:
                    exps(u)
                if 2 <= u < nu + 2:
                    take_turned(u - 2)
                if u >= 3:
                    take_values(u - 3)
            act.wait_ge(squared, nu)
            nc.scalar.activation(ss[:, 1, :], ss[:, 0, :], ACT.Sqrt, bias=m.eps[:, 0:1]).then_inc(root, 1)


def copy_stage(m, name, jobs):
    g = Gemm(m, name, jobs)
    with m.nc.Block() as block:
        @block.sync
        def _(sp):
            g.send(sp)

        @block.tensor
        def _(pe):
            g.products(pe)

        @block.scalar
        def _(act):
            g.take("act", act, None)


def rotary_stage(m, turn, at):
    nc = m.nc
    pos = m.area("ro_pos", [P, 4], at, mybir.dt.int32)
    posf = m.area("ro_posf", [P, 4], at + 32)
    ang = m.area("ro_ang", [P, 4, 32], at + 64)
    k = m.area("ro_k", [P, 4, 32], at + 64 + 512)
    loaded = m.sem("ro_loaded")
    reduced = m.sem("ro_reduced")
    sines = m.sem("ro_sines")
    with nc.Block() as block:
        @block.sync
        def _(sp):
            for t in range(4):
                sp.dma_start(pos[:, t:t + 1], m.dram["positions_2"][0, t * P:(t + 1) * P].unsqueeze(1)).then_inc(
                    loaded, 16)

        @block.vector
        def _(dve):
            step = m.dve_steps.on(dve)
            dve.wait_ge(loaded, 64)
            step(nc.vector.tensor_copy(posf[:], pos[:]))
            step(nc.vector.tensor_tensor(ang[:], spread(posf[:], 32),
                                         m.freqs.unsqueeze(1).to_broadcast([P, 4, 32]), ALU.mult))
            step(nc.vector.tensor_scalar(k[:], ang[:], 1.0 / TWO_PI, None, ALU.mult))
            step(nc.vector.tensor_scalar(k[:], k[:], ROUND, None, ALU.add))
            step(nc.vector.tensor_scalar(k[:], k[:], -ROUND, None, ALU.add))
            for part in (PI_A, PI_B, PI_C):
                step(nc.vector.scalar_tensor_tensor(out=ang[:], in0=k[:], scalar=-part, in1=ang[:],
                                                    op0=ALU.mult, op1=ALU.add))
            nc.vector.tensor_scalar(ang[:], ang[:], 3.1415925, -3.1415925, ALU.min, ALU.max).then_inc(reduced, 1)
            dve.wait_ge(sines, 1)
            step(nc.vector.tensor_tensor(turn[:, 0], turn[:, 0], turn[:, 0], ALU.mult))
            step(nc.vector.tensor_scalar(turn[:, 0], turn[:, 0], -2.0, 1.0, ALU.mult, ALU.add))

        @block.scalar
        def _(act):
            act.wait_ge(reduced, 1)
            nc.scalar.activation(turn[:, 0], ang[:], ACT.Sin, scale=0.5)
            nc.scalar.activation(turn[:, 1], ang[:], ACT.Sin).then_inc(sines, 1)


class Finish:

    def __init__(self, m, name, nope, pe_part, gpe, gain, factor, turn, nope_t, pe_t, junk, x, w, ss,
                 bank, n_banks, padded=False):
        self.m, self.nope, self.pe_part, self.gpe, self.gain, self.factor = m, nope, pe_part, gpe, gain, factor
        self.turn, self.nope_t, self.pe_t, self.bank, self.n_banks, self.padded = \
            turn, nope_t, pe_t, bank, n_banks, padded
        self.junk = m.at(f"{name}_junk", [P, BH, NOPE], junk)
        self.x = m.at(f"{name}_pe", [P, 2, BH, ROPE], x)
        self.w = m.at(f"{name}_work", [P, BH, ROPE], w)
        self.ss = m.at(f"{name}_ss", [P, 4, 4, BH], ss)
        self.pool_scales = False
        self.inverse_ready = m.sem(f"{name}_inverse")
        self.nope_scaled = m.sem(f"{name}_nope_scaled")
        self.cleared = m.sem(f"{name}_cleared")
        self.nope_squared = m.sem(f"{name}_nope_squared")
        self.nope_summed = m.sem(f"{name}_nope_summed")
        self.squared = m.sem(f"{name}_squared")
        self.root_ready = m.sem(f"{name}_root")
        self.ready = m.sem(f"{name}_ready")
        self.turned = m.sem(f"{name}_turned")
        self.taken = m.sem(f"{name}_taken")

    def act_squares(self, act, t):
        if t:
            act.wait_ge(self.nope_summed, t)
        self.m.nc.scalar.activation(self.junk[:], self.nope(t), ACT.Square).then_inc(self.nope_squared, 1)

    def squares(self, dve, t):
        nc, ss, w, step = self.m.nc, self.ss, self.w, self.m.dve_steps.on(dve)
        tt = nc.vector.tensor_tensor
        step(tt(w[:], self.pe_part(t), self.pe_part(t), ALU.mult))
        step(nc.vector.tensor_reduce(ss[:, 3, t, :], w[:], AX.X, ALU.add))
        dve.wait_ge(self.nope_squared, t + 1)
        nc.vector.tensor_reduce(ss[:, 0, t, :], self.junk[:], AX.X, ALU.add).then_inc(self.nope_summed, 1)
        if t == 3:
            dve.wait_ge(self.nope_summed, 4)
            step(tt(ss[:, 0], ss[:, 0], ss[:, 3], ALU.add))
            nc.vector.tensor_scalar(ss[:, 0], ss[:, 0], 1.0 / QKH, None, ALU.mult).then_inc(self.squared, 1)

    def root(self, act):
        act.wait_ge(self.squared, 1)
        self.m.nc.scalar.activation(self.ss[:, 1], self.ss[:, 0], ACT.Sqrt,
                                    bias=self.m.eps[:, 0:1]).then_inc(self.root_ready, 1)

    def inverses(self, dve):
        step = self.m.dve_steps.on(dve)
        dve.wait_ge(self.root_ready, 1)
        step(self.m.nc.vector.reciprocal(self.ss[:, 2], self.ss[:, 1]))
        self.m.nc.vector.tensor_scalar(self.ss[:, 2], self.ss[:, 2], self.factor, None,
                                       ALU.mult).then_inc(self.inverse_ready, 1)
        dve.wait_ge(self.inverse_ready, 1)

    def tile(self, dve, t):
        step, w, turn = self.m.dve_steps.on(dve), self.w, self.turn
        tt = self.m.nc.vector.tensor_tensor
        r = self.ss[:, 2, t, :]
        if t >= 2:
            dve.wait_ge(self.turned, t - 1)
        g = self.gpe.unsqueeze(1).to_broadcast([P, BH, ROPE])
        c = turn[:, 0, t, :].unsqueeze(1).to_broadcast([P, BH, 32])
        s = turn[:, 1, t, :].unsqueeze(1).to_broadcast([P, BH, 32])
        o = self.x[:, t % 2]
        if not self.pool_scales:
            tt(self.nope(t), self.nope(t), spread(r, NOPE), ALU.mult)
        step(tt(w[:], self.pe_part(t), g, ALU.mult))
        step(tt(w[:], w[:], spread(r, ROPE), ALU.mult))
        j = self.junk[:, :, 0:ROPE]
        tt(j[:, :, 0:32], w[:, :, 32:64], s, ALU.mult)
        tt(j[:, :, 32:64], w[:, :, 0:32], s, ALU.mult)
        tt(o[:, :, 0:32], w[:, :, 0:32], c, ALU.mult)
        step(tt(o[:, :, 32:64], w[:, :, 32:64], c, ALU.mult))
        tt(o[:, :, 0:32], o[:, :, 0:32], j[:, :, 0:32], ALU.subtract)
        tt(o[:, :, 32:64], o[:, :, 32:64], j[:, :, 32:64], ALU.add).then_inc(self.ready, 1)
        dve.wait_ge(self.ready, t + 1)

    def takes(self, act, t):
        nc, ps = self.m.nc, self.m.ps
        c, b = slice(t * P, (t + 1) * P), self.bank(t)
        act.wait_ge(self.turned, t + 1)
        for half in range(2):
            nc.scalar.activation(self.nope_t[:, 4 * half:4 * half + 4, c],
                                 ps[:, b + half, :].rearrange("p (k c) -> p k c", k=4), ACT.Copy,
                                 scale=self.m.col(self.gain))
        stacked = ps[:, b + 2, :].rearrange("p (k c) -> p k c", k=4)
        if self.padded:
            if t == 0:
                act.wait_ge(self.cleared, 1)
            for i in range(2):
                r = slice(64 * i, 64 * i + 64)
                ins = nc.scalar.activation(self.pe_t[r, i:BH:2, c], stacked[r], ACT.Copy)
        else:
            ins = nc.scalar.activation(self.pe_t[:, :, c], stacked, ACT.Copy)
        ins.then_inc(self.taken, 1)

    def turns(self, pe, t):
        ps, b = self.m.ps, self.bank(t)
        pe.wait_ge(self.ready, t + 1)
        if self.pool_scales:
            pe.wait_ge(self.nope_scaled, t + 1)
        if t >= self.n_banks:
            pe.wait_ge(self.taken, t - self.n_banks + 1)
        for h in range(BH):
            pe.transpose(ps[:, b + h // 4, (h % 4) * P:(h % 4 + 1) * P], self.nope(t)[:, h, :], self.m.ident)
        for h in range(BH // 2):
            ins = pe.transpose(ps[:, b + 2, h * P:(h + 1) * P],
                               self.x[:, t % 2, 2 * h:2 * h + 2, :].rearrange("p a b -> p (a b)"), self.m.ident)
        ins.then_inc(self.turned, 1)

    def stage(self):
        self.pool_scales = True
        with self.m.nc.Block() as block:
            @block.gpsimd
            def _(pool):
                if self.padded:
                    self.m.nc.gpsimd.memset(self.pe_t[:], 0.0).then_inc(self.cleared, 1)
                    pool.wait_ge(self.cleared, 1)
                pool.wait_ge(self.inverse_ready, 1)
                for t in range(4):
                    self.m.nc.gpsimd.tensor_tensor(self.nope(t), self.nope(t), spread(self.ss[:, 2, t, :], NOPE),
                                                   ALU.mult).then_inc(self.nope_scaled, 1)
                    pool.wait_ge(self.nope_scaled, t + 1)

            @block.vector
            def _(dve):
                for t in range(4):
                    self.squares(dve, t)
                self.inverses(dve)
                for t in range(4):
                    self.tile(dve, t)

            @block.scalar
            def _(act):
                for t in range(4):
                    self.act_squares(act, t)
                self.root(act)
                for t in range(4):
                    self.takes(act, t)

            @block.tensor
            def _(pe):
                for t in range(4):
                    self.turns(pe, t)

    def between(self, start, gap, ahead):
        first_tile = start + 4 * gap + 1

        def vector(dve):
            work = {start + gap * t: [lambda t=t: self.squares(dve, t)] for t in range(4)}
            for t in range(4):
                work[first_tile + gap * t] = [lambda t=t: self.tile(dve, t)]
            work[first_tile].insert(0, lambda: self.inverses(dve))
            return work

        def scalar(act):
            work = {start - 1 + gap * t: [lambda t=t: self.act_squares(act, t)] for t in range(4)}
            work[start + 1 + 3 * gap] = [lambda: self.root(act)]
            for t in range(4):
                work[first_tile + ahead + 1 + gap * t] = [lambda t=t: self.takes(act, t)]
            return work

        def tensor(pe):
            return {first_tile + gap * t: [lambda t=t: self.turns(pe, t)] for t in range(4)}

        return dict(dve_work=vector, act_work=scalar, pe_work=tensor)


def two_blocks(nc, dram):
    with ExitStack() as ctx:
        ctx.enter_context(nc.allow_non_contiguous_dma("short rows of gains and gate weights"))
        m = Machine(nc, ctx, dram)
        m.gates = m.keep("gates", [CAP, NE])
        m.rows = m.keep("rows", [CAP, NE], U32)
        m.arena = m.keep_end
        m.xhat = nc.dram_tensor("xhat_scratch", [L1, D], F32, kind="Internal").ap()
        m.resid = nc.dram_tensor("resid_scratch", [L1, D], F32, kind="Internal").ap()

        def columns(w, widths, start=0):
            k = w.shape[0] // P
            for c in widths:
                m.blocks.append((w[:, start:start + c], k, c))
                start += c

        columns(dram["w_in"][0], [512] * 6)
        columns(dram["w_out"][0], [512] * 2)
        for l in range(2):
            columns(dram["mem_w_kv_2"][l], [512] * 2)
        for _, _, start, width in MLSTM_IN:
            columns(dram["a_w_in_2"][0], [width], start)
        columns(dram["a_w_out_2"][0], [512] * 2)
        columns(dram["w_kv_a_2"], [KVL + ROPE])
        columns(dram["w_kv_b_2"], [512] * 4)
        w = dram["b_w_in_2"][0]
        columns(w, [QL, 512, 512])
        columns(w, [512], QL + 3 * 512)
        columns(w, [512], QL + 2 * 512)
        columns(dram["b_w_q_up_2"][0], [512] * 3)
        columns(dram["b_w_out_2"][0], [512] * 2)

        def rows(name, n, flat=None):
            a = dram[name] if flat is None else flat
            return a.rearrange("(k p) -> k p", p=P)

        names = [
            ("mix_g", rows(None, 8, dram["mix_norm_g"][0])),
            ("conv_w", dram["conv_w"][0].rearrange("j (k p) -> (j k) p", p=P)),
            ("subln", rows(None, 1, dram["attn_subln_g"][0])),
            ("ffn_g", rows(None, 8, dram["ffn_norm_g"][0])),
            ("a_norm", rows(None, 8, dram["a_norm_2"][0])),
            ("a_conv_b", rows(None, 16, dram["a_conv_b_2"][0])),
            ("a_h_norm", rows(None, 8, dram["a_h_norm_2"][0])),
            ("b_norm", rows(None, 8, dram["b_norm_2"][0])),
            ("q_lat", rows(None, 3, dram["b_q_lat_norm_2"][0])),
            ("kv_norm", rows(None, 8, dram["kv_norm_2"])),
            ("kv_lat", rows(None, 2, dram["kv_lat_norm_2"])),
            ("q_nope", rows(None, 1, dram["b_q_gain_2"][0, 0:NOPE])),
            ("k_nope", rows(None, 1, dram["k_gain_2"][0:NOPE])),
            ("mem_norm", rows(None, 8, dram["mem_norm_2"])),
            ("mem_q", dram["mem_q_gain_2"]),
            ("mem_k", dram["mem_k_gain_2"]),
            ("a_conv_w", dram["a_conv_w_2"][0].rearrange("j (k p) -> (j k) p", p=P)),
        ]

        feat = 4 * KD * L1
        h = m.area("h", [P, len(TILES1), D], 0)
        hn = m.area("hn1", [P, KD, L1], 20480)
        qk = m.area("qk1", [P, KD, L1], 20480 + feat)
        v = m.area("v1", [P, len(TILES1), AH * AV], 20480 + 2 * feat)
        at = 20480 + 2 * feat + 10240
        raw = m.area("raw1", [P, 12, L1], at)
        turns = m.area("turns1", [P, 2, L1], at + 48 * L1)
        work = at + 56 * L1
        setup_stage(m, h, turns, work, names)
        m.close()
        norm_stage(m, "n1", rows_of(h, TILES1, [(hn, "mix_g")]), m.arena + work)
        m.close()
        rot_work = m.area("rot_work", [P, 2, L1], work)
        projection_stage(m, hn, qk, v, raw, turns, rot_work, m.arena + work + 8 * L1)
        m.close()
        diff_attention_stage(m, qk, v, raw, hn, at + 48 * L1)
        m.close()
        spare = [m.arena + 20480 + feat + 8320 * i for i in range(3)]
        mem_x = m.area("mem_x", [P, 2, D], 65536)
        mem_t = m.area("mem_t", [P, KD, MEM], 73728)
        mem_loaded = m.sem("mem_loaded")

        def load_memory(sp, g):
            sp.dma_start(mem_x[:], dram["mem_2"][0].rearrange("(t p) d -> p t d", p=P)).then_inc(mem_loaded, 16)
            sp.wait_ge(mem_loaded, 16)

        out_stage(m, "out1", hn, h, TILES1, spare, tail=load_memory)
        m.close()

        def store_tokens(sp, normed, ready, stored):
            for t, (t0, n) in enumerate(TILES1):
                sp.dma_start(m.resid[t0:t0 + n, :], h[0:n, t, :]).then_inc(m.resid_stored, 16)
            for t, (t0, n) in enumerate(TILES1):
                sp.wait_ge(ready, t + 1)
                sp.dma_start(m.xhat[t0:t0 + n, :], normed[0:n, t % 4, :]).then_inc(stored[t % 4], 16)
            sp.wait_ge(m.resid_stored, 16 * len(TILES1))
            for i in range(4):
                sp.wait_ge(stored[i], 16 * len(range(i, len(TILES1), 4)))

        m.resid_stored = m.sem("resid_stored")
        norm_stage(m, "n2", rows_of(h, TILES1, [(hn, "ffn_g")]) + rows_of(mem_x, TILES2[:2], [(mem_t, "mem_norm")]),
                   m.arena + 81920, tail=store_tokens, buffers=4)
        m.close()
        mk = [m.area(f"mk{l}", [P, MEMH, MEM], 16384 + 8192 * l) for l in range(2)]
        mv = [m.area(f"mv{l}", [P, 2, 512], 16384 + 8192 * l + 4096) for l in range(2)]
        mk_tok = [m.area(f"mk_tok{l}", [P, 2, 512], 40960 + 4096 * l) for l in range(2)]
        router_stage(m, hn, mem_t, mk_tok, mv, work, [m.arena + 49152 + 6144 * i for i in range(3)])
        m.close()
        by_head = lambda t: t.rearrange("p t (g w) -> p t g w", g=MEMH)
        group_norm_stage(m, "gm", [dict(src=by_head(mk_tok[l][:]), dst=mk[l], gain=("mem_k", l), factor=1.0)
                                   for l in range(2)], 81920)
        m.close()
        experts_stage(m, 32768)
        m.close()

        x = m.area("x", [P, 4, D], 0)
        final_norm_stage(m, x, 32768)
        m.close()
        hn = m.low("hn2", [P, KD, SEQ], 0)
        qk = m.low("qk2", [P, 16, SEQ], 16384)
        v = m.area("v2", [P, 4, MW], 32768)
        y = m.area("y2", [P, 12, SEQ], 49152)
        mq = m.area("mq2", [P, 4, MEMH * MEMD], 73728)
        work = 81920
        gates = m.area("ml_gates", [2 * MH, SEQ], 106496)
        mqt = m.low("mqt2", [P, MEMH, SEQ], 16384)
        norm_stage(m, "n3", rows_of(x, TILES2, [(hn, "a_norm")]), m.arena + work)
        m.close()
        mlstm_in_stage(m, hn, qk, v, y, mq, gates, work)
        m.close()
        ht = m.low("ht", [P, 4, MW], 0)
        mlstm_stage(m, qk, v, gates, ht, y, work)
        m.close()
        group_norm_stage(m, "gq1", [dict(src=by_head(mq[:]), dst=mqt, gain=("mem_q", 0),
                                         factor=MEMD ** -0.5)], work)
        m.close()
        attention_stage(m, "ma1", memory_units(mqt, mk[0], mv[0], y), work)
        m.close()
        work_slots = [m.arena + 81920 + 8192 * i for i in range(3)]
        out_stage(m, "out2", y, x, TILES2, work_slots)
        m.close()

        hb = m.low("hb", [P, KD, SEQ], 0)
        hkv = m.low("hkv", [P, KD, SEQ], 16384)
        qt = m.low("qt3", [P, BH, SEQ], 16384)
        kt = m.low("kt3", [P, BH, SEQ], 32768)
        v = m.area("v3", [P, 4, BH, NOPE], 32768)
        y = m.area("y3", [P, 12, SEQ], 49152)
        kn = m.low("kn", [P, 4, BH, NOPE], 16384)
        lat = m.area("lat", [P, 4, KVL + ROPE], 16384)
        kpt = m.area("kpt", [P, BH // 2, SEQ], 73728)
        qpt = m.area("qpt", [P, BH, SEQ], 81920)
        mq = m.area("mq3", [P, 4, MEMH * MEMD], 90112)
        latt = m.area("latt", [P, KVL // P, SEQ], 81920)
        turn = m.area("turn3", [P, 2, 4, 32], 106496)
        norm_stage(m, "n4", rows_of(x, TILES2, [(hb, "b_norm"), (hkv, "kv_norm")]), m.arena + 49152)
        m.close()

        def copies(*dsts):
            act = m.nc.scalar
            return [lambda step, u, psum, f=f: f(act, u, psum) for f in dsts]

        def job(kind, src, take):
            return dict(kind=kind, act=src, tiles=TILES2, engine="act", take=take)

        take_lat, = copies(lambda act, u, ps: act.activation(lat[:, u, :], ps, ACT.Copy))
        copy_stage(m, "kva", [job("tokens", hkv, take_lat)])
        m.close()
        one_group = lambda t: t.unsqueeze(2)
        group_norm_stage(m, "gkv", [dict(src=one_group(lat[:, :, 0:KVL]), dst=latt, gain=("kv_lat", 0),
                                         factor=1.0)], 90112)
        m.close()
        rotary_stage(m, turn, 90112)
        m.close()

        def take_kv(c):
            def f(step, u, psum):
                act = m.nc.scalar
                pair = psum.rearrange("p (h w) -> p h w", h=2)
                act.activation(kn[:, u, 2 * c:2 * c + 2, :], pair[:, :, 0:NOPE], ACT.Copy)
                return act.activation(v[:, u, 2 * c:2 * c + 2, :], pair[:, :, NOPE:], ACT.Copy)
            return f

        SplitGemm(m, "kvb", [job("tokens", latt, take_kv(c)) for c in range(4)],
                  [m.arena + at for at in (73728, 90112, 98304)]).stage()
        m.close()
        keys = Finish(m, "fk", lambda t: kn[:, t],
                      lambda t: lat[:, t, KVL:].unsqueeze(1).to_broadcast([P, BH, ROPE]), m.gpe[:, 1, :],
                      "k_nope", 1.0, turn, kt, kpt, m.arena + 90112, m.arena + 94208, m.arena + 88064,
                      m.arena + 107520, lambda t: 5, 1)
        qlat = m.area("qlat", [P, 4, QL], 81920)
        take_ql, take_mq = copies(lambda act, u, ps: act.activation(qlat[:, u, :], ps, ACT.Copy),
                                  lambda act, u, ps: act.activation(mq[:, u, :], ps, ACT.Copy))
        take_z = copies(*[lambda act, u, ps, c=c: act.activation(y[:, c + u, :], ps, ACT.Silu)
                          for c in (0, 4, 8)])
        SplitGemm(m, "in3", [dict(job("tokens", hb, take_ql), early=True)] +
                  [dict(job("features", hb, take), early=True) for take in take_z] +
                  [dict(job("tokens", hb, take_mq), early=True)],
                  m.gaps + [m.arena + 98304], banks=5).stage(**keys.between(2, 3, 3))
        m.close()
        qlt = m.low("qlt", [P, QL // P, SEQ], 16384)
        mqt = m.low("mqt3", [P, MEMH, SEQ], 16384 + 6144)
        group_norm_stage(m, "gq2", [dict(src=one_group(qlat[:]), dst=qlt, gain=("q_lat", 0), factor=1.0),
                                    dict(src=by_head(mq[:]), dst=mqt, gain=("mem_q", 1),
                                         factor=MEMD ** -0.5)], 98304)
        m.close()
        attention_stage(m, "ma2", memory_units(mqt, mk[1], mv[1], y), 90112)
        m.close()
        q_low = m.area("q_low", [P, 2, BH, QKH], 16384)
        q_high = m.low("q_high", [P, 2, BH, QKH], 0)
        q_of = lambda t: (q_low if t < 2 else q_high)[:, t % 2]

        def take_q(c):
            def f(step, u, psum):
                flat = q_of(u).rearrange("p h w -> p (h w)")
                return m.nc.scalar.activation(flat[:, 512 * c:512 * (c + 1)], psum, ACT.Copy)
            return f

        SplitGemm(m, "qup", [job("tokens", qlt, take_q(c)) for c in range(3)], work_slots).stage()
        m.close()
        Finish(m, "fq", lambda t: q_of(t)[:, :, 0:NOPE], lambda t: q_of(t)[:, :, NOPE:], m.gpe[:, 0, :],
               "q_nope", QKH ** -0.5, turn, qt, qpt, m.arena + 98304, m.low_ring + 12288,
               m.arena + 98304 + 4096, m.arena + 98304 + 6144, lambda t: 4 * (t % 2), 2, padded=True).stage()
        m.close()
        units = []
        for hd in range(BH):
            for t in range(4):
                c, w = slice(t * P, (t + 1) * P), (t + 1) * P
                units.append(dict(scores=[(qt[:, hd, c], kt[:, hd, 0:w]), (qpt[:, hd, c], kpt[:, hd // 2, 0:w])],
                                  width=w, mask=m.chunk, values=[v[:, s, hd, :] for s in range(t + 1)],
                                  y=y[:, hd, c]))
        attention_stage(m, "ba", units, 16384)
        m.close()
        result_stored = m.sem("result_stored")

        def store_result(sp, g):
            out = dram["out"][0].rearrange("(t p) d -> p t d", p=P)
            sp.wait_ge(g.out["dve"], 4)
            sp.dma_start(out[:, :, 0:512], x[:, :, 0:512]).then_inc(result_stored, 16)
            for t in range(4):
                sp.wait_ge(g.out["dve"], 5 + t)
                sp.dma_start(out[:, t, 512:], x[:, t, 512:]).then_inc(result_stored, 16)
            sp.wait_ge(result_stored, 16 * 5)

        out_stage(m, "out3", y, x, TILES2, work_slots, ahead=0, tail=store_result)
        m.close()


INPUTS = ["x", "meta_tokens", "mix_norm_g", "w_in", "conv_w", "lambda_q1", "lambda_k1", "lambda_q2", "lambda_k2",
          "attn_subln_g", "w_out", "ffn_norm_g", "w_router", "w_gate", "w_up", "w_down", "final_norm_g", "mem_2",
          "positions_2", "a_norm_2", "a_w_in_2", "a_conv_w_2", "a_conv_b_2", "a_ig_bias_2", "a_fg_bias_2",
          "a_h_norm_2", "a_w_out_2", "b_norm_2", "b_w_in_2", "b_q_lat_norm_2", "b_w_q_up_2", "b_q_gain_2",
          "b_w_out_2", "kv_norm_2", "w_kv_a_2", "kv_lat_norm_2", "w_kv_b_2", "k_gain_2", "mem_norm_2",
          "mem_w_kv_2", "mem_q_gain_2", "mem_k_gain_2"]


def kernel(**inputs):
    import numpy as _np
    import concourse.bacc as _bacc
    from concourse import mybir as _mybir
    from concourse.bass_utils import run_bass_kernel_spmd as _run

    nc = _bacc.Bacc("TRN2", target_bir_lowering=False, num_devices=1)
    arrays, dram = {}, {}
    masks, turns = fixed_tables()
    given = {name: _np.ascontiguousarray(inputs[name]) for name in INPUTS}
    given["masks"], given["turns"] = masks, turns
    for name, a in given.items():
        arrays[f"in_{name}"] = a
        dram[name] = nc.dram_tensor(f"in_{name}", a.shape, _mybir.dt.from_np(a.dtype), kind="ExternalInput").ap()
    dram["out"] = nc.dram_tensor("out_0", (1, SEQ, D), _mybir.dt.float32, kind="ExternalOutput").ap()
    two_blocks(nc, dram)
    r = _run(nc, [arrays], core_ids=[0])
    return r.results[0]["out_0"]
```
